# Optimizing a Trainium2 kernel written in Bass

```python
import math
import jax, jax.numpy as jnp
from jax import lax
import numpy as np

D_MODEL = 1024
BATCH = 1
SEQ = 512
DEPTH = 2

N_MIXERS = 2
N_NSA_LAYERS = (DEPTH + 1) // 2
N_DIFF_LAYERS = DEPTH // 2
EPS = 1e-6
ROPE_THETA = 500000.0
ROT_FRACTION_DIV = 4
D_FF = 4 * D_MODEL
NEG_INF = -1e30
BIG = 1e9

NSA_HEAD_DIM = 64
NSA_HEADS = D_MODEL // NSA_HEAD_DIM
NSA_KV_GROUPS = 4
NSA_HPG = NSA_HEADS // NSA_KV_GROUPS
CMP_BLOCK = 32
CMP_STRIDE = 16
CMP_HIDDEN = 4 * NSA_HEAD_DIM
SLC_BLOCK = 64
SLC_TOPK = 16
WINDOW = 512
NSA_Q_BLOCK = 32
NSA_KV_WIDTH = NSA_KV_GROUPS * NSA_HEAD_DIM
NSA_IN_SPLITS = [NSA_HEADS * NSA_HEAD_DIM] + [NSA_KV_WIDTH] * 6 + [NSA_HEADS * 3]
NSA_IN_WIDTH = sum(NSA_IN_SPLITS)

DIFF_HEAD_DIM = 64
DIFF_HEADS = D_MODEL // (2 * DIFF_HEAD_DIM)
DIFF_IN_WIDTH = 3 * D_MODEL
ATTN_Q_BLOCK = 128

kernel_name = "hybrid_nsa_diffattn_sqrelu"

def rms_norm(x, g):
    xf = x.astype(jnp.float32)
    y = xf * lax.rsqrt(jnp.mean(xf * xf, axis=-1, keepdims=True) + EPS)
    return (y * g.astype(jnp.float32)).astype(x.dtype)

def rope_tables(positions, head_dim):
    rot = head_dim // ROT_FRACTION_DIV
    inv = 1.0 / (ROPE_THETA ** (jnp.arange(0, rot, 2, dtype=jnp.float32) / rot))
    ang = positions.astype(jnp.float32)[:, None] * inv[None, :]
    return jnp.cos(ang), jnp.sin(ang)

def apply_partial_rope(x, cos, sin):
    half = cos.shape[-1]
    x1, x2, xp = x[..., :half], x[..., half:2 * half], x[..., 2 * half:]
    c = cos.astype(x.dtype)
    s = sin.astype(x.dtype)
    return jnp.concatenate([x1 * c - x2 * s, x2 * c + x1 * s, xp], axis=-1)

def masked_softmax(s, mask):
    s = jnp.where(mask, s.astype(jnp.float32), NEG_INF)
    p = jax.nn.softmax(s, axis=-1)
    return jnp.where(mask, p, 0.0)

def compress_blocks(kv, pos_emb, w1, w2):
    S = kv.shape[2]
    nc = (S - CMP_BLOCK) // CMP_STRIDE + 1
    idx = jnp.arange(nc)[:, None] * CMP_STRIDE + jnp.arange(CMP_BLOCK)[None, :]
    blocks = kv[:, :, idx, :] + pos_emb.astype(kv.dtype)
    flat = blocks.reshape(blocks.shape[:3] + (CMP_BLOCK * NSA_HEAD_DIM,))
    return jax.nn.gelu(flat @ w1) @ w2

def nsa_mixer(h, w_in, ck_pos, ck_w1, ck_w2, cv_pos, cv_w1, cv_w2, w_out):
    B, S, _ = h.shape
    G, P, hd = NSA_KV_GROUPS, NSA_HPG, NSA_HEAD_DIM
    proj = h @ w_in
    q, k_cmp, v_cmp, k_slc, v_slc, k_win, v_win, g_log = jnp.split(
        proj, list(np.cumsum(NSA_IN_SPLITS)[:-1]), axis=-1)
    q = q.reshape(B, S, G, P, hd).transpose(0, 2, 3, 1, 4)
    gates = jax.nn.sigmoid(g_log.reshape(B, S, G, P, 3).astype(jnp.float32))
    gates = gates.transpose(0, 2, 3, 1, 4).astype(h.dtype)
    kvg = lambda t: t.reshape(B, S, G, hd).transpose(0, 2, 1, 3)
    k_cmp, v_cmp, k_slc, v_slc, k_win, v_win = map(kvg, (k_cmp, v_cmp, k_slc, v_slc, k_win, v_win))

    pos = jnp.arange(S)
    cos, sin = rope_tables(pos, hd)
    q = apply_partial_rope(q, cos, sin)
    k_slc = apply_partial_rope(k_slc, cos, sin)
    k_win = apply_partial_rope(k_win, cos, sin)

    nc = (S - CMP_BLOCK) // CMP_STRIDE + 1
    cmp_start = jnp.arange(nc) * CMP_STRIDE
    cmp_end = cmp_start + CMP_BLOCK - 1
    kc = compress_blocks(k_cmp, ck_pos, ck_w1, ck_w2)
    vc = compress_blocks(v_cmp, cv_pos, cv_w1, cv_w2)
    ccos, csin = rope_tables(cmp_end, hd)
    kc = apply_partial_rope(kc, ccos, csin)

    n_slc = S // SLC_BLOCK
    topk = min(SLC_TOPK, n_slc)
    sj = jnp.arange(n_slc) * SLC_BLOCK
    sel_map = ((cmp_end[:, None] >= sj[None, :]) &
               (cmp_start[:, None] <= sj[None, :] + SLC_BLOCK - 1)).astype(jnp.float32)
    ks_blocks = k_slc.reshape(B, G, n_slc, SLC_BLOCK, hd)
    vs_blocks = v_slc.reshape(B, G, n_slc, SLC_BLOCK, hd)
    gather = jax.vmap(jax.vmap(lambda blk, ix: blk[ix]))

    k_win_pad = jnp.pad(k_win, ((0, 0), (0, 0), (WINDOW, 0), (0, 0)))
    v_win_pad = jnp.pad(v_win, ((0, 0), (0, 0), (WINDOW, 0), (0, 0)))

    scale = hd ** -0.5
    Cq = NSA_Q_BLOCK
    blk_ids = jnp.arange(n_slc)

    def chunk(c):
        t0 = c * Cq
        tq = t0 + jnp.arange(Cq)
        qc = lax.dynamic_slice_in_dim(q, t0, Cq, axis=3) * jnp.asarray(scale, q.dtype)
        gc = lax.dynamic_slice_in_dim(gates, t0, Cq, axis=3)

        s_c = jnp.einsum('bgpqd,bgnd->bgpqn', qc, kc)
        p_c = masked_softmax(s_c, cmp_end[None, :] <= tq[:, None])
        o_c = jnp.einsum('bgpqn,bgnd->bgpqd', p_c.astype(vc.dtype), vc)

        imp = jnp.einsum('bgpqn,nj->bgqj', p_c, sel_map)
        cur = (tq // SLC_BLOCK)[:, None]
        forced = (blk_ids[None, :] == 0) | (blk_ids[None, :] == cur) | (blk_ids[None, :] == cur - 1)
        future = blk_ids[None, :] * SLC_BLOCK > tq[:, None]
        imp = jnp.where(forced, BIG, jnp.where(future, -BIG, imp))
        _, sel = lax.top_k(imp, topk)
        ks = gather(ks_blocks, sel)
        vs = gather(vs_blocks, sel)
        tok = sel[..., None] * SLC_BLOCK + jnp.arange(SLC_BLOCK)
        m_s = (tok <= tq[None, None, :, None, None]).reshape(B, G, 1, Cq, topk * SLC_BLOCK)
        s_s = jnp.einsum('bgpqd,bgqkld->bgpqkl', qc, ks).reshape(B, G, P, Cq, topk * SLC_BLOCK)
        p_s = masked_softmax(s_s, m_s).reshape(B, G, P, Cq, topk, SLC_BLOCK)
        o_s = jnp.einsum('bgpqkl,bgqkld->bgpqd', p_s.astype(vs.dtype), vs)

        kw = lax.dynamic_slice_in_dim(k_win_pad, t0, WINDOW + Cq, axis=2)
        vw = lax.dynamic_slice_in_dim(v_win_pad, t0, WINDOW + Cq, axis=2)
        pw = t0 - WINDOW + jnp.arange(WINDOW + Cq)
        m_w = (pw[None, :] <= tq[:, None]) & (pw[None, :] > tq[:, None] - WINDOW) & (pw[None, :] >= 0)
        s_w = jnp.einsum('bgpqd,bgkd->bgpqk', qc, kw)
        p_w = masked_softmax(s_w, m_w)
        o_w = jnp.einsum('bgpqk,bgkd->bgpqd', p_w.astype(vw.dtype), vw)

        return gc[..., 0:1] * o_c + gc[..., 1:2] * o_s + gc[..., 2:3] * o_w

    out = lax.map(chunk, jnp.arange(S // Cq))
    out = out.transpose(1, 0, 4, 2, 3, 5).reshape(B, S, NSA_HEADS * hd)
    return out @ w_out

def diff_mixer(h, w_in, lq1, lk1, lq2, lk2, subln_g, w_out, lambda_init):
    B, S, _ = h.shape
    H, hd = DIFF_HEADS, DIFF_HEAD_DIM
    q, k, v = jnp.split(h @ w_in, 3, axis=-1)
    q = q.reshape(B, S, H, 2, hd).transpose(0, 2, 3, 1, 4)
    k = k.reshape(B, S, H, 2, hd).transpose(0, 2, 3, 1, 4)
    v = v.reshape(B, S, H, 2 * hd).transpose(0, 2, 1, 3)
    cos, sin = rope_tables(jnp.arange(S), hd)
    q = apply_partial_rope(q, cos, sin) * jnp.asarray(hd ** -0.5, q.dtype)
    k = apply_partial_rope(k, cos, sin)
    f32 = jnp.float32
    lam = (jnp.exp(jnp.sum(lq1.astype(f32) * lk1.astype(f32))) -
           jnp.exp(jnp.sum(lq2.astype(f32) * lk2.astype(f32))) + lambda_init)
    kpos = jnp.arange(S)
    Qb = ATTN_Q_BLOCK

    def block(c):
        t0 = c * Qb
        tq = t0 + jnp.arange(Qb)
        qc = lax.dynamic_slice_in_dim(q, t0, Qb, axis=3)
        s = jnp.einsum('bhiqd,bhikd->bhiqk', qc, k)
        p = masked_softmax(s, kpos[None, :] <= tq[:, None])
        a = p[:, :, 0] - lam * p[:, :, 1]
        o = jnp.einsum('bhqk,bhkd->bhqd', a.astype(v.dtype), v)
        return rms_norm(o, subln_g) * jnp.asarray(1.0 - lambda_init, o.dtype)

    out = lax.map(block, jnp.arange(S // Qb))
    out = out.transpose(1, 0, 3, 2, 4).reshape(B, S, H * 2 * hd)
    return out @ w_out

def sqrelu_mlp(h, w_up, w_down):
    u = jax.nn.relu(h @ w_up)
    return (u * u) @ w_down

def setup_inputs(seed: int = 0) -> dict:
    key = jax.random.key(seed)
    ks = list(jax.random.split(key, 24))
    nrm = lambda k, shape, s: jax.random.normal(k, shape, jnp.float32) * s
    LA, LB, hd = N_NSA_LAYERS, N_DIFF_LAYERS, NSA_HEAD_DIM
    return {
        "x": nrm(ks[0], (BATCH, SEQ, D_MODEL), 1.0),
        "attn_norm_g": 1.0 + nrm(ks[1], (DEPTH, D_MODEL), 0.02),
        "mlp_norm_g": 1.0 + nrm(ks[2], (DEPTH, D_MODEL), 0.02),
        "nsa_w_in": nrm(ks[3], (LA, D_MODEL, NSA_IN_WIDTH), D_MODEL ** -0.5),
        "nsa_ck_pos": nrm(ks[4], (LA, CMP_BLOCK, hd), 0.1),
        "nsa_ck_w1": nrm(ks[5], (LA, CMP_BLOCK * hd, CMP_HIDDEN), (CMP_BLOCK * hd) ** -0.5),
        "nsa_ck_w2": nrm(ks[6], (LA, CMP_HIDDEN, hd), CMP_HIDDEN ** -0.5),
        "nsa_cv_pos": nrm(ks[7], (LA, CMP_BLOCK, hd), 0.1),
        "nsa_cv_w1": nrm(ks[8], (LA, CMP_BLOCK * hd, CMP_HIDDEN), (CMP_BLOCK * hd) ** -0.5),
        "nsa_cv_w2": nrm(ks[9], (LA, CMP_HIDDEN, hd), CMP_HIDDEN ** -0.5),
        "nsa_w_out": nrm(ks[10], (LA, D_MODEL, D_MODEL), D_MODEL ** -0.5),
        "diff_w_in": nrm(ks[11], (LB, D_MODEL, DIFF_IN_WIDTH), D_MODEL ** -0.5),
        "diff_lq1": nrm(ks[12], (LB, DIFF_HEAD_DIM), 0.1),
        "diff_lk1": nrm(ks[13], (LB, DIFF_HEAD_DIM), 0.1),
        "diff_lq2": nrm(ks[14], (LB, DIFF_HEAD_DIM), 0.1),
        "diff_lk2": nrm(ks[15], (LB, DIFF_HEAD_DIM), 0.1),
        "diff_subln_g": 1.0 + nrm(ks[16], (LB, 2 * DIFF_HEAD_DIM), 0.02),
        "diff_w_out": nrm(ks[17], (LB, D_MODEL, D_MODEL), D_MODEL ** -0.5),
        "mlp_w_up": nrm(ks[18], (DEPTH, D_MODEL, D_FF), D_MODEL ** -0.5),
        "mlp_w_down": nrm(ks[19], (DEPTH, D_FF, D_MODEL), D_FF ** -0.5),
        "final_norm_g": 1.0 + nrm(ks[20], (D_MODEL,), 0.02),
    }

def reference(x, attn_norm_g, mlp_norm_g, nsa_w_in, nsa_ck_pos, nsa_ck_w1, nsa_ck_w2,
              nsa_cv_pos, nsa_cv_w1, nsa_cv_w2, nsa_w_out, diff_w_in, diff_lq1, diff_lk1,
              diff_lq2, diff_lk2, diff_subln_g, diff_w_out, mlp_w_up, mlp_w_down, final_norm_g):
    for i in range(DEPTH):
        h = rms_norm(x, attn_norm_g[i])
        j = i // N_MIXERS
        if i % N_MIXERS == 0:
            mix = nsa_mixer(h, nsa_w_in[j], nsa_ck_pos[j], nsa_ck_w1[j], nsa_ck_w2[j],
                            nsa_cv_pos[j], nsa_cv_w1[j], nsa_cv_w2[j], nsa_w_out[j])
        else:
            lambda_init = 0.8 - 0.6 * math.exp(-0.3 * i)
            mix = diff_mixer(h, diff_w_in[j], diff_lq1[j], diff_lk1[j], diff_lq2[j], diff_lk2[j],
                             diff_subln_g[j], diff_w_out[j], lambda_init)
        x = x + mix
        x = x + sqrelu_mlp(rms_norm(x, mlp_norm_g[i]), mlp_w_up[i], mlp_w_down[i])
    return rms_norm(x, final_norm_g)


_drawn_inputs = setup_inputs


def setup_inputs(seed=0):
    import zlib

    import numpy as np

    out = dict(_drawn_inputs(seed))
    spreads = {}
    factors = {'attn_norm_g': 4.751,
     'nsa_ck_pos': 8.0,
     'diff_lq1': 2.945,
     'diff_lq2': 200.0,
     'diff_lk2': 2.707,
     'diff_subln_g': 78.694,
     'final_norm_g': 25.757}
    for name, (base, spread) in spreads.items():
        noise = np.random.default_rng([zlib.crc32(name.encode()), seed]).standard_normal(out[name].shape)
        drawn = base * np.exp(spread * noise) if base else spread * noise
        out[name] = __import__('jax').numpy.asarray(drawn.astype(out[name].dtype))
    for name, factor in factors.items():
        out[name] = (out[name] * factor).astype(out[name].dtype)
    return out
```

```python
import math
from contextlib import ExitStack

import numpy as np
import concourse.bass as bass
from concourse import mybir

F32 = mybir.dt.float32
F32R = mybir.dt.float32r
BF16 = mybir.dt.bfloat16
ALU = mybir.AluOpType
ACT = mybir.ActivationFunctionType
X = mybir.AxisListType.X

P = 128
S = 512
D = 1024
T = S // P
KT = D // P
NB = 512
HD = 64
GROUPS = 4
HPG = 4
NC = 32
ROT = 16
FF = 4096
CHUNK = 1024
STEPS = FF // CHUNK
DH = 8
EPS = 1e-6
SCALE = HD ** -0.5
LAMBDA_INIT = 0.8 - 0.6 * math.exp(-0.3)
GELU_C = math.sqrt(2.0 / math.pi)
NEG = -1e30
PT_ROW = 384
PT_BR = 1664

C_ID, C_MASK, C_COS, C_SIN, C_CCOS, C_CSIN, C_CADD, C_CMUL, C_END = (
    0, 128, 256, 320, 384, 400, 416, 544, 672)
V_G, V_POS, V_SUB, V_END = 0, 32, 96, 97

B_CMP, B_W1K, B_W1V, B_SLC, B_WIN, B_Q0, B_Q1, B_OUT0 = 0, 1, 2, 3, 4, 5, 6, 7
B_MLP0, B_DIFF, B_OUT1, B_MLP1, B_ALL = 9, 25, 31, 33, 49
G_CMP, G_W1K, G_W1V, G_SLC, G_WIN, G_Q, G_GATE, G_OUT0 = 0, 4, 5, 6, 10, 14, 22, 26
G_MLP0, G_DIFF, G_OUT1, G_MLP1 = 34, 66, 90, 98


def build(nc, a, out):
    with ExitStack() as ctx:
        def sb(name, shape, dt=F32):
            return ctx.enter_context(nc.sbuf_tensor(name, shape, dt))

        def sem(name):
            return ctx.enter_context(nc.semaphore(name))

        x_res = sb("x_res", [P, T, D])
        act_hi = sb("act_hi", [P, KT, S], F32R)
        act_lo = sb("act_lo", [P, KT, S], F32R)
        w_raw = sb("w_raw", [P, 4, 1024])
        w_hi = sb("w_hi", [P, 2, 4096], F32R)
        w_lo = sb("w_lo", [P, 2, 4096], F32R)
        k_stack = sb("k_stack", [P, 2, 2, S], F32R)
        ar_r = sb("ar_r", [P, 8192], F32R)
        ar_f = sb("ar_f", [P, 10240])
        o_buf = sb("o_buf", [P, S])
        hid_t = sb("hid_t", [P, 2, 256], F32R)
        w2_r = sb("w2_r", [P, 2, 256], F32R)
        rtmp = sb("rtmp", [P, 512])
        cst = sb("cst", [P, C_END])
        vec = sb("vec", [P, V_END])
        ident_b = sb("ident_b", [P, P], BF16)
        mask_b = sb("mask_b", [P, P], BF16)
        lamv_in = sb("lamv_in", [P, 256])
        lam2 = sb("lam2", [P, 2])
        gate = sb("gate", [P, T, 48])
        st = sb("st", [P, 96])
        ps = ctx.enter_context(nc.psum_tensor("ps", [P, 8, NB], F32))

        ident = cst[:, C_ID:C_ID + P]

        def tab(c0, n, t=None):
            v = cst[:, c0:c0 + n]
            return v if t is None else v.rearrange("p (t r) -> p t r", t=t)

        def view(base, off, dims):
            return bass.AP(base.tensor, off, [list(base.ap[0])] + [list(d) for d in dims])

        y_buf = ar_f[:, 8192:9216]
        z_buf = ar_f[:, 9216:10240]
        x_cmp = ar_f[:, 8192:10240].rearrange("p (j c) -> p j c", j=16)
        q_raw = ar_f[:, 0:4096].rearrange("p (t c) -> p t c", t=T)
        k_raw = ar_f[:, 4096:6144].rearrange("p (b t c) -> p b t c", b=2, t=T)
        q_st = ar_f[:, 6144:7168].rearrange("p (t h d) -> p t h d", t=T, h=HPG)
        k_st = ar_f[:, 7168:7680].rearrange("p (t b d) -> p t b d", b=2, t=T)
        c_sc = ar_f[:, 7680:8192]
        prob = ar_f[:, 8192:10240].rearrange("p (u b k) -> p u b k", u=2, b=2)
        g_h, g_a, g_b = (ar_f[:, 6144 + 256 * i:6400 + 256 * i] for i in range(3))
        kc_f = ar_f[:, 6912:6976]
        kc_r = ar_f[:, 6976:7040]
        tail_raw = ar_f[:, 0:384]
        w2_raw = ar_f[:, 384:640]
        relu_b = ar_f[:, 0:1024].rearrange("p (u c) -> p u c", u=2)
        sq_b = ar_f[:, 1024:2048].rearrange("p (u c) -> p u c", u=2)
        gfin = ar_f[:, 2048:3072]
        fin = ar_f[:, 3072:5120].rearrange("p (u c) -> p u c", u=2)
        dk_raw = ar_f[:, 4096:8192].rearrange("p (t c) -> p t c", t=T)
        d_st = ar_f[:, 9216:10240].rearrange("p (t z c d) -> p t z c d", t=T, z=2, c=2)

        xc_hi = [ar_r[:, 4096 * v:4096 * v + 2048].rearrange("p (j c) -> p j c", j=16) for v in range(2)]
        xc_lo = [ar_r[:, 4096 * v + 2048:4096 * v + 4096].rearrange("p (j c) -> p j c", j=16) for v in range(2)]
        v_all = ar_r[:, 0:4096].rearrange("p (t b g c) -> p t b g c", t=T, b=2, g=GROUPS)
        v_st = ar_r[:, 4096:5120].rearrange("p (t b c) -> p t b c", t=T, b=2)
        kc = ar_r[:, 5120:5376].rearrange("p (z c) -> p z c", z=2)
        vc = ar_r[:, 5376:5504]
        vc_st = ar_r[:, 5504:5632]
        vc_rep = ar_r[:, 5632:6144].rearrange("p (g c) -> p g c", g=GROUPS)
        q_stack = ar_r[:, 6144:8192].rearrange("p (h q) -> p h q", h=HPG)
        tail_r = k_stack[:, :, :, :].rearrange("p z b q -> p (z b q)")[:, 0:768].rearrange("p (z c) -> p z c", z=2)
        a_hi = ar_r[:, 0:4096].rearrange("p (f c) -> p f c", f=8)
        a_lo = ar_r[:, 4096:8192].rearrange("p (f c) -> p f c", f=8)
        dv_all = ar_r[:, :].rearrange("p (t h c) -> p t h c", t=T, h=DH)
        slot0 = [w_hi[:, 0, :], w_lo[:, 0, :]]
        pct = [s[:, 3328:3840] for s in slot0]
        dq_stack = w_hi[:, 0, 1024:2048].rearrange("p (c q) -> p c q", c=2)
        dv_st = w_hi[:, 0, 2048:3072].rearrange("p (t c) -> p t c", t=T)
        dpt = [s[:, 0:1024].rearrange("p (u c) -> p u c", u=2) for s in slot0]

        ss, ms, rstd = st[:, 0:20], st[:, 20:40], st[:, 40:60]
        nmax = st[:, 60:64].rearrange("p (u b) -> p u b", u=2)
        rsum = st[:, 64:68].rearrange("p (u b) -> p u b", u=2)
        rinv = st[:, 68:72].rearrange("p (u b) -> p u b", u=2)
        coef = st[:, 72:76].rearrange("p (u b) -> p u b", u=2)
        d_ss, d_ms, d_rs = st[:, 76:80], st[:, 80:84], st[:, 84:88]
        half = st[:, 88:92]
        lam_s = st[:, 92:96]
        c_st = sb("c_st", [P, 4, 16])
        subg = sb("subg", [P, 1])

        x_landed = [sem(f"x_landed{t}") for t in range(T)]
        cst_landed, small_landed, gfin_landed = sem("cst_landed"), sem("small_landed"), sem("gfin_landed")
        part_landed = [sem(f"part_landed{j}") for j in range(4)]
        stored = [sem(f"stored{u}") for u in range(2)]
        hi_split, lo_split = sem("hi_split"), sem("lo_split")
        small_hi, small_lo = sem("small_hi"), sem("small_lo")
        tok_done, tok_free = sem("tok_done"), sem("tok_free")
        up_done, up_free, a_hi_done, a_ready = sem("up_done"), sem("up_free"), sem("a_hi_done"), sem("a_ready")
        sq_done = sem("sq_done")
        ss_done, rstd_done, y_done, turned, z_done, act_hi_done, act_ready = (
            sem(n) for n in ("ss_done", "rstd_done", "y_done", "turned", "z_done", "act_hi_done", "act_ready"))
        xc_hi_done, xc_ready = sem("xc_hi_done"), sem("xc_ready")
        gelu_arg, gelu_tanh, hid_done, hid_turned = sem("gelu_arg"), sem("gelu_tanh"), sem("hid_done"), sem("hid_turned")
        hid_hi, hid_lo, cmp_done, kc_roped, kc_turned, kc_hi = (
            sem(n) for n in ("hid_hi", "hid_lo", "cmp_done", "kc_roped", "kc_turned", "kc_hi"))
        cmp_ready = sem("cmp_ready")
        gate_tanh = sem("gate_tanh")
        lam_arg, lam_exp = sem("lam_arg"), sem("lam_exp")
        rest_copied, roped, st_turned, stack_hi, stack_lo = (
            sem(n) for n in ("rest_copied", "roped", "st_turned", "stack_hi", "stack_lo"))
        v_staged, cs_done, cs_sub, cs_exp, cs_coef, pc_ready, pc_turned, pc_hi, pc_lo = (
            sem(n) for n in ("v_staged", "cs_done", "cs_sub", "cs_exp", "cs_coef", "pc_ready", "pc_turned",
                             "pc_hi", "pc_lo"))
        s_done, max_done, exp_done, coef_done, normed, p_turned, pt_hi, pt_lo = (
            sem(n) for n in ("s_done", "max_done", "exp_done", "coef_done", "normed", "p_turned", "pt_hi", "pt_lo"))
        pv_done, o_half, o_sum, o_hi, o_lo = (sem(n) for n in ("pv_done", "o_half", "o_sum", "o_hi", "o_lo"))
        d_rest, d_roped, d_turned, d_hi, d_lo, dv_staged = (
            sem(n) for n in ("d_rest", "d_roped", "d_turned", "d_hi", "d_lo", "dv_staged"))
        ds_done, dmax_done, dexp_done, dcoef_done, dp1_done, da_done, dp_turned, dpt_hi, dpt_lo = (
            sem(n) for n in ("ds_done", "dmax_done", "dexp_done", "dcoef_done", "dp1_done", "da_done", "dp_turned",
                             "dpt_hi", "dpt_lo"))
        dpv_done, do_free, d_ss_done, d_ms_done, d_rs_done, dy_done, do_turned, dz_done, do_hi, do_lo = (
            sem(n) for n in ("dpv_done", "do_free", "d_ss_done", "d_ms_done", "d_rs_done", "dy_done", "do_turned",
                             "dz_done", "do_hi", "do_lo"))
        dve_order, act_order, pool_order = sem("dve_order"), sem("act_order"), sem("pool_order")
        pool_passed = sem("pool_passed")

        class Order:

            def __init__(self, eng, s):
                self.eng, self.s, self.base, self.loop = eng, s, 0, 0

            def after(self, ins):
                ins.then_inc(self.s, 1)
                self.base += 1
                self.eng.wait_ge(self.s, self.loop + self.base)

            def enter(self, i, per):
                self.loop, self.at, self.per = i * per, self.base, per

            def leave(self, count):
                assert self.base == self.at + self.per, (self.base - self.at, self.per)
                self.base, self.loop = self.at + self.per * count, 0

        def cols(w, c0, j):
            return w[256 * j:256 * (j + 1), c0:c0 + NB].rearrange("(k p) c -> p k c", p=P)

        CMP0, SLC0, WIN0, TAIL0 = D, D + 512, D + 1024, D + 1536

        def part_source(n, j):
            if n in (B_W1K, B_W1V):
                w = a["ck_w1"] if n == B_W1K else a["cv_w1"]
                return w[512 * j:512 * (j + 1), :].rearrange("(k p) c -> p k c", p=P)
            if n < B_OUT0:
                c0 = {B_CMP: CMP0, B_SLC: SLC0, B_WIN: WIN0, B_Q0: 0, B_Q1: NB}[n]
                return cols(a["w_in"], c0, j)
            if n < B_MLP0:
                return cols(a["w_out"], NB * (n - B_OUT0), j)
            if n < B_OUT1:
                return cols(a["diff_in"], NB * (n - B_DIFF), j)
            return cols(a["diff_out"], NB * (n - B_OUT1), j)

        def mlp_source(layer, it, c, j):
            if c < 2:
                w = a["w_up"][layer, 256 * j:256 * (j + 1), bass.ds(it * CHUNK + NB * c, NB)]
            else:
                w = a["w_down"][layer, bass.ds(it * CHUNK + 256 * j, 256), NB * (c - 2):NB * (c - 1)]
            return w.rearrange("(k p) c -> p k c", p=P)

        def slot_of(n):
            return n % 2

        block = ctx.enter_context(nc.Block())

        @block.sync
        def _(sp):
            for t in range(T):
                sp.dma_start(x_res[:, t, :], a["x"][P * t:P * (t + 1), :]).then_inc(x_landed[t], 16)

            def load(n, j, src):
                if not isinstance(n, int) or n > 0:
                    sp.wait_ge(lo_split, n * 4 + (j - 3))
                if len(src.shape) == 3 and src.shape[1] == 4:
                    dst = w_raw[:, j, :].rearrange("p (k c) -> p k c", k=4)
                else:
                    dst = w_raw[:, j, :].rearrange("p (k c) -> p k c", k=2)
                sp.dma_start(dst, src).then_inc(part_landed[j], 16)

            def straight(n0, n1):
                for n in range(n0, n1):
                    for j in range(4):
                        load(n, j, part_source(n, j))

            straight(0, B_MLP0)
            with sp.Fori(0, STEPS) as it:
                for c in range(4):
                    for j in range(4):
                        load(it * 4 + (B_MLP0 + c), j, mlp_source(0, it, c, j))
            straight(B_DIFF, B_MLP1)
            with sp.Fori(0, STEPS) as it:
                for c in range(4):
                    for j in range(4):
                        load(it * 4 + (B_MLP1 + c), j, mlp_source(1, it, c, j))
            for t in range(T):
                sp.wait_ge(z_done, 16 + t + 1)
                sp.dma_start(out[P * t:P * (t + 1), :], fin[:, t % 2, :]).then_inc(stored[t % 2], 16)
            for u in range(2):
                sp.wait_ge(stored[u], 16 * T // 2)

        @block.gpsimd
        def _(pool):
            order = Order(pool, pool_order)
            order.after(pool.memset(half, -0.5))

            def norm_stat(q):
                pool.wait_ge(ss_done, q + 1)
                order.after(pool.tensor_scalar(ms[:, q:q + 1], ss[:, q:q + 1], 1.0 / D, EPS, ALU.mult, ALU.add))
                pool.tensor_tensor(rstd[:, q:q + 1], ms[:, q:q + 1], half[:, 0:1], ALU.pow).then_inc(rstd_done, 1)

            for q in range(4):
                norm_stat(q)

            n0 = order.base
            with pool.Fori(0, GROUPS) as g:
                order.enter(g, 1)
                pool.wait_ge(st_turned, g * 3 + 1)
                pool.tensor_copy(v_st.rearrange("p t b c -> p (t b) c"),
                                 v_all[:, :, :, bass.ds(g, 1), :].bitcast(F32).rearrange("p t b o c -> p (t b) (o c)")
                                 ).then_inc(v_staged, 1)
                pool.tensor_copy(vc_st, vc_rep[:, bass.ds(g, 1), :].bitcast(F32).rearrange("p o c -> p (o c)")
                                 ).then_inc(v_staged, 1)
                e = c_sc.rearrange("p (i h n) -> p i h n", i=T, h=HPG)
                pool.wait_ge(cs_coef, g + 1)
                order.after(pool.tensor_tensor(e, e, tab(C_CMUL, 128, T).unsqueeze(2).broadcast_to([P, T, HPG, NC]),
                                               ALU.mult))
                ef = c_sc.rearrange("p (r n) -> p r n", n=NC)
                pool.tensor_tensor(ef, ef, c_st[:, 3, :].unsqueeze(2).broadcast_to([P, 16, NC]),
                                   ALU.mult).then_inc(pc_ready, 1)
                for s in range(16):
                    n = P * (s % 4 + 1)
                    pool.wait_ge(coef_done, g * 16 + (s + 1)).then_inc(pool_passed, 1)
                    for br in range(2):
                        p = prob[:, s % 2, br, 0:n]
                        pool.tensor_scalar(p, p, coef[:, s % 2, br:br + 1], 1.0, ALU.mult, ALU.mult).then_inc(normed, 1)
            order.leave(GROUPS)

            for q in range(4, 12):
                norm_stat(q)

            with pool.Fori(0, DH) as h:
                pool.wait_ge(d_turned, h * 2 + 1)
                pool.tensor_copy(dv_st, dv_all[:, :, bass.ds(h, 1), :].bitcast(F32).rearrange("p t o c -> p t (o c)")
                                 ).then_inc(dv_staged, 1)
                for i in range(T):
                    pool.wait_ge(dcoef_done, h * 4 + (i + 1)).then_inc(pool_passed, 1)
                    p = prob[:, i % 2, 1, 0:P * (i + 1)]
                    pool.tensor_scalar(p, p, coef[:, i % 2, 1:2], 1.0, ALU.mult, ALU.mult).then_inc(dp1_done, 1)
                pool.wait_ge(d_ms_done, h + 1)
                pool.tensor_tensor(d_rs, d_ms, half, ALU.pow).then_inc(d_rs_done, 1)
            for q in range(12, 20):
                norm_stat(q)

        @block.scalar
        def _(act):
            order = Order(act, act_order)
            act.dma_start(cst[:, :], a["consts"]).then_inc(cst_landed, 16)
            act.dma_start(vec[:, :], a["vectors"]).then_inc(cst_landed, 16)
            act.dma_start(tail_raw.rearrange("p (k c) -> p k c", k=KT),
                          a["w_in"][:, TAIL0:TAIL0 + 48].rearrange("(k p) c -> p k c", p=P)).then_inc(small_landed, 16)
            for v, w in enumerate((a["ck_w2"], a["cv_w2"])):
                act.dma_start(w2_raw[:, P * v:P * (v + 1)].rearrange("p (k c) -> p k c", k=2),
                              w.rearrange("(k p) c -> p k c", p=P)).then_inc(small_landed, 16)
            act.dma_start(lamv_in[:, :], a["lam_in"].partition_broadcast(P).rearrange("p o c -> p (o c)")
                          ).then_inc(small_landed, 16)

            def split_hi(n, j):
                act.wait_ge(part_landed[j], n * 16 + 16)
                act.copy(w_hi[:, slot_of(n), 1024 * j:1024 * (j + 1)], w_raw[:, j, :]).then_inc(hi_split, 1)

            def norm_sum(q, t):
                if q >= 1:
                    act.wait_ge(turned, q)
                act.activation(y_buf, x_res[:, t, :], ACT.Square, accum_out=ss[:, q:q + 1]).then_inc(ss_done, 1)

            def norm_scale(q, t):
                act.wait_ge(rstd_done, q + 1)
                act.activation(y_buf, x_res[:, t, :], ACT.Copy, scale=rstd[:, q:q + 1]).then_inc(y_done, 1)

            def norm_hi(q, t):
                act.wait_ge(z_done, q + 1)
                act.copy(act_hi[:, :, P * t:P * (t + 1)], z_buf.rearrange("p (k c) -> p k c", k=KT)
                         ).then_inc(act_hi_done, 1)

            def norm_tail(q0, g_last):
                for t in range(T):
                    act.wait_ge(tok_free, g_last + t + 1)
                    norm_sum(q0 + t, t)
                    norm_scale(q0 + t, t)
                    norm_hi(q0 + t, t)

            act.wait_ge(small_landed, 64)
            act.copy(tail_r[:, 0, :], tail_raw).then_inc(small_hi, 1)
            act.copy(w2_r[:, 0, :], w2_raw).then_inc(small_hi, 1)
            for t in range(T):
                act.wait_ge(x_landed[t], 16)
                norm_sum(t, t)
                norm_scale(t, t)
                split_hi(0, t)
                norm_hi(t, t)

            def split_next(n, j, wait):
                if j == 0:
                    act.wait_ge(*wait)
                split_hi(n, j)

            for j in range(2):
                split_hi(1, j)
            act.wait_ge(tok_free, G_CMP + 2)
            act.copy(xc_hi[0], x_cmp).then_inc(xc_hi_done, 1)
            for j in range(2, 4):
                split_hi(1, j)
            act.wait_ge(tok_free, G_CMP + 4)
            act.copy(xc_hi[1], x_cmp).then_inc(xc_hi_done, 1)
            for j in range(4):
                split_next(B_W1V, j, (tok_done, G_W1K))

            def gelu(v):
                act.wait_ge(gelu_arg, v + 1)
                act.activation(g_a, g_a, ACT.Tanh, scale=GELU_C).then_inc(gelu_tanh, 1)
                act.wait_ge(hid_turned, v + 1)
                act.copy(hid_t[:, 0, :], ps[:, 4, 0:256]).then_inc(hid_hi, 1)

            for j in range(4):
                split_next(B_SLC, j, (tok_done, G_W1V))
            gelu(0)
            act.wait_ge(kc_turned, 1)
            act.copy(kc[0:HD, 0, :], ps[0:HD, 6, 0:P]).then_inc(kc_hi, 1)
            act.copy(kc[HD:P, 0, :], ps[0:HD, 6, 0:P]).then_inc(kc_hi, 1)
            for j in range(4):
                split_next(B_WIN, j, (tok_done, G_SLC))
            gelu(1)
            for j in range(4):
                split_next(B_Q0, j, (tok_done, G_WIN))
            for j in range(4):
                split_next(B_Q1, j, (tok_done, G_Q))
            for j in range(4):
                split_next(B_OUT0, j, (tok_done, G_Q + 4))
            act.wait_ge(tok_free, G_GATE + T)
            act.activation(gate[:, :, :], gate[:, :, :], ACT.Tanh, scale=0.5).then_inc(gate_tanh, 1)
            act.wait_ge(lam_arg, 1)
            act.activation(lam_s[:, 2:4], lam_s[:, 0:2], ACT.Exp).then_inc(lam_exp, 1)

            with act.Fori(0, GROUPS) as g:
                act.wait_ge(roped, g + 1)
                act.copy(q_st[:, :, :, ROT:], q_raw[:, :, bass.ds(g * 256, 256)].rearrange(
                    "p t (h d) -> p t h d", h=HPG)[:, :, :, ROT:]).then_inc(rest_copied, 1)
                act.copy(k_st.rearrange("p t b d -> p b t d")[:, :, :, ROT:],
                         k_raw[:, :, :, bass.ds(g * HD, HD)][:, :, :, ROT:]).then_inc(rest_copied, 1)
                for e in range(3):
                    act.wait_ge(st_turned, g * 3 + (e + 1))
                    for c in range(2):
                        r = HD * c
                        if e == 0:
                            act.copy(k_stack[0:HD, 0, c, :], ps[r:r + HD, 0, :])
                            ins = act.copy(k_stack[HD:P, 0, c, :], ps[r:r + HD, 0, :])
                        else:
                            ins = act.mul(q_stack[r:r + HD, 2 * (e - 1) + c, :], ps[r:r + HD, e, :], SCALE)
                    ins.then_inc(stack_hi, 1)
                act.wait_ge(cs_sub, g + 1)
                act.activation(c_sc, c_sc, ACT.Exp).then_inc(cs_exp, 1)

                def exps(s):
                    n = P * (s % 4 + 1)
                    act.wait_ge(max_done, g * 16 + (s + 1))
                    if s >= 2:
                        act.wait_ge(p_turned, g * 16 + (s - 1))
                    for br in range(2):
                        act.activation(prob[:, s % 2, br, 0:n], ps[:, 2 * (s % 2) + br, 0:n], ACT.Exp,
                                       bias=nmax[:, s % 2, br:br + 1],
                                       accum_out=rsum[:, s % 2, br:br + 1]).then_inc(exp_done, 1)

                def turned_hi(s):
                    i = s % 4
                    act.wait_ge(p_turned, g * 16 + (s + 1))
                    if i == 0 and s:
                        act.wait_ge(pv_done, g * 4 + s // 4)
                    act.copy(view(slot0[0], P * i, [[PT_BR, 2], [PT_ROW, i + 1], [1, P]]),
                             view(ps[:, 4, :], 4 * NB, [[NB, 2], [P, i + 1], [1, P]])).then_inc(pt_hi, 1)

                def out_half(h):
                    r = HD * (h % 2)
                    act.wait_ge(pv_done, g * 4 + (h + 1))
                    act.copy(o_buf[r:r + HD, :], ps[HD:P, 6, :]).then_inc(o_half, 1)

                def out_hi(h):
                    r = HD * (h % 2)
                    act.wait_ge(o_sum, g * 4 + (h + 1))
                    act.copy(act_hi[r:r + HD, bass.ds(g * 2 + h // 2, 1), :].rearrange("p o c -> p (o c)"),
                             o_buf[r:r + HD, :]).then_inc(o_hi, 1)

                for s in range(16):
                    exps(s)
                    if s == 1:
                        act.wait_ge(pc_turned, g + 1)
                        act.copy(pct[0], ps[:, 7, :]).then_inc(pc_hi, 1)
                    if s >= 1:
                        turned_hi(s - 1)
                    if s >= 6 and s % 4 == 2:
                        out_half((s - 6) // 4)
                    if s >= 7 and s % 4 == 3:
                        out_hi((s - 7) // 4)
                turned_hi(15)
                out_half(3)
                out_hi(3)

            for j in range(4):
                split_next(B_OUT0 + 1, j, (o_lo, 4 * GROUPS))
            for j in range(4):
                split_next(B_MLP0, j, (tok_done, G_OUT0 + 4))
            norm_tail(4, G_OUT0 + 4)

            def relu(u, u_abs):
                act.wait_ge(up_done, u_abs + (u + 1))
                if u >= 2:
                    act.wait_ge(a_ready, u_abs + (u - 1))
                act.activation(relu_b[:, u % 2, :], ps[:, (u + 2) % 4, :], ACT.Relu).then_inc(up_free, 1)
                act.wait_ge(up_free, u_abs + (u + 1))
                act.activation(a_hi[:, u, :], relu_b[:, u % 2, :], ACT.Square).then_inc(a_hi_done, 1)

            def mlp_step(n, gr, up, last):
                for c in range(4):
                    for j in range(4):
                        if not (c == 3 and last == "end"):
                            w = [(tok_done, gr), (up_done, up + 4), (up_done, up + 8), (tok_done, gr + 4)][c]
                            if j == 0:
                                act.wait_ge(*w)
                            act.wait_ge(part_landed[j], (n + (c + 1)) * 16 + 16)
                            act.copy(w_hi[:, (c + B_MLP0 + 1) % 2, 1024 * j:1024 * (j + 1)],
                                     w_raw[:, j, :]).then_inc(hi_split, 1)
                        if c < 2:
                            relu(4 * c + j, up)

            def mlp_layer(n0, g0, u0, end):
                with act.Fori(0, STEPS - 1) as it:
                    mlp_step(it * 4 + n0, it * 8 + g0, it * 8 + u0, None)
                k = STEPS - 1
                mlp_step(n0 + 4 * k, g0 + 8 * k, u0 + 8 * k, end)

            mlp_layer(B_MLP0, G_MLP0, 0, None)
            norm_tail(8, G_DIFF - 4)

            for b in range(6):
                prev = (tok_done, G_DIFF + 4 * b)
                if b < 6:
                    for j in range(4):
                        split_next(B_DIFF + b + 1, j, prev)

            with act.Fori(0, DH) as h:
                act.wait_ge(d_roped, h + 1)
                for z, raw in enumerate((q_raw, dk_raw)):
                    act.copy(d_st[:, :, z, :, ROT:], raw[:, :, bass.ds(h * P, P)].rearrange(
                        "p t (c d) -> p t c d", c=2)[:, :, :, ROT:]).then_inc(d_rest, 1)
                act.wait_ge(d_turned, h * 2 + 1)
                act.mul(dq_stack[0:HD, 0, :], ps[0:HD, 0, :], SCALE)
                act.mul(dq_stack[HD:P, 1, :], ps[HD:P, 0, :], SCALE).then_inc(d_hi, 1)
                act.wait_ge(d_turned, h * 2 + 2)
                for c in range(2):
                    for r in (0, HD):
                        ins = act.copy(k_stack[r:r + HD, 0, c, :], ps[HD * c:HD * (c + 1), 1, :])
                ins.then_inc(d_hi, 1)

                def d_exps(i):
                    n = P * (i + 1)
                    act.wait_ge(dmax_done, h * 4 + (i + 1))
                    if i >= 2:
                        act.wait_ge(dp_turned, h * 4 + (i - 1))
                    for c in range(2):
                        act.activation(prob[:, i % 2, c, 0:n], ps[:, 2 * (i % 2) + c, 0:n], ACT.Exp,
                                       bias=nmax[:, i % 2, c:c + 1],
                                       accum_out=rsum[:, i % 2, c:c + 1]).then_inc(dexp_done, 1)

                def d_turned_hi(i):
                    n = P * (i + 1)
                    act.wait_ge(dp_turned, h * 4 + (i + 1))
                    if i >= 2:
                        act.wait_ge(dpv_done, h * 4 + (i - 1))
                    act.copy(dpt[0][:, i % 2, 0:n], ps[:, 4 + i % 2, 0:n]).then_inc(dpt_hi, 1)

                for i in range(T):
                    d_exps(i)
                    if i >= 1:
                        d_turned_hi(i - 1)
                d_turned_hi(T - 1)
                for i in range(T):
                    act.wait_ge(do_free, h * 4 + (i + 1))
                    act.activation(y_buf[:, P * i:P * (i + 1)], o_buf[:, P * i:P * (i + 1)], ACT.Square,
                                   accum_out=d_ss[:, i:i + 1]).then_inc(d_ss_done, 1)
                act.wait_ge(dz_done, h + 1)
                act.copy(act_hi[:, bass.ds(h, 1), :].rearrange("p o c -> p (o c)"), o_buf[:, :]).then_inc(do_hi, 1)

            act.dma_start(gfin, a["final_g"].partition_broadcast(P).rearrange("p o c -> p (o c)")
                          ).then_inc(gfin_landed, 16)
            for j in range(4):
                split_next(B_OUT1 + 1, j, (do_lo, DH))
            for j in range(4):
                split_next(B_MLP1, j, (tok_done, G_OUT1 + 4))
            norm_tail(12, G_OUT1 + 4)
            mlp_layer(B_MLP1, G_MLP1, 32, "end")
            for t in range(T):
                act.wait_ge(tok_free, G_MLP1 + 28 + t + 1)
                if t:
                    act.wait_ge(ss_done, 16 + t)
                act.activation(y_buf, x_res[:, t, :], ACT.Square, accum_out=ss[:, 16 + t:17 + t]).then_inc(ss_done, 1)

        @block.vector
        def _(dve):
            order = Order(dve, dve_order)

            def sub(out_, in0, hi):
                return dve.tensor_tensor(out_, in0, hi.bitcast(F32), ALU.subtract)

            def split_lo(n, j, slot=None):
                dve.wait_ge(hi_split, n * 4 + (j + 1))
                sl = slot_of(n) if slot is None else slot
                sub(w_lo[:, sl, 1024 * j:1024 * (j + 1)], w_raw[:, j, :],
                    w_hi[:, sl, 1024 * j:1024 * (j + 1)]).then_inc(lo_split, 1)

            def norm_z(q, t):
                r = q // 4
                dve.wait_ge(turned, q + 1)
                if q:
                    dve.wait_ge(act_ready, q)
                b = 4 + 2 * (t % 2)
                g = vec[:, V_G + KT * r:V_G + KT * (r + 1)].unsqueeze(2).broadcast_to([P, KT, P])
                dve.tensor_tensor(z_buf.rearrange("p (k c) -> p k c", k=KT),
                                  ps[:, b:b + 2, :].rearrange("p b (k c) -> p (b k) c", c=P), g,
                                  ALU.mult).then_inc(z_done, 1)
                dve.wait_ge(act_hi_done, q + 1)
                sub(act_lo[:, :, P * t:P * (t + 1)], z_buf.rearrange("p (k c) -> p k c", k=KT),
                    act_hi[:, :, P * t:P * (t + 1)]).then_inc(act_ready, 1)

            dve.wait_ge(cst_landed, 32)
            dve.tensor_copy(ident_b[:, :], ident).then_inc(small_lo, 1)
            dve.tensor_copy(mask_b[:, :], tab(C_MASK, P)).then_inc(small_lo, 1)
            dve.tensor_scalar(subg[:, :], vec[:, V_SUB:V_SUB + 1], 1.0 - LAMBDA_INIT, None, ALU.mult)
            dve.wait_ge(small_hi, 2)
            sub(tail_r[:, 1, :], tail_raw, tail_r[:, 0, :]).then_inc(small_lo, 1)
            sub(w2_r[:, 1, :], w2_raw, w2_r[:, 0, :]).then_inc(small_lo, 1)
            lv = lamv_in[:, :].rearrange("p (v u c) -> p v u c", v=2, u=2)
            order.after(dve.tensor_tensor(rtmp[:, 0:128].rearrange("p (v c) -> p v c", v=2), lv[:, :, 0, :],
                                          lv[:, :, 1, :], ALU.mult))
            dve.tensor_reduce(lam_s[:, 0:2], rtmp[:, 0:128].rearrange("p (v c) -> p v c", v=2), X,
                              ALU.add).then_inc(lam_arg, 1)
            for t in range(T):
                split_lo(0, t)
                norm_z(t, t)

            dve.wait_ge(act_ready, 4)
            order.after(dve.memset(x_cmp.rearrange("p j (g n) -> p j g n", g=GROUPS)[:, :, :, NC - 1:NC], 0.0))
            for m in range(4):
                v, bank = m // 2, (G_CMP + m) % 4
                if m == 2:
                    dve.wait_ge(xc_hi_done, 1)
                    sub(xc_lo[0], x_cmp, xc_hi[0]).then_inc(xc_ready, 1)
                    dve.wait_ge(xc_ready, 1)
                if m < 2:
                    split_lo(1, m)
                dve.wait_ge(tok_done, G_CMP + m + 1)
                for gl in range(2):
                    r, g = HD * gl, 2 * (m % 2) + gl
                    src = ps[r:r + HD, bank, :].rearrange("p (n b) -> p b n", b=16)
                    for par in range(2):
                        for jh in range(2):
                            pos = vec[r:r + HD, V_POS + 32 * v + 16 * par + 8 * jh:V_POS + 32 * v + 16 * par + 8 * jh + 8]
                            ins = dve.tensor_tensor(
                                x_cmp[HD * par:HD * (par + 1), 8 * jh:8 * jh + 8, NC * g:NC * g + NC - 1],
                                src[:, par::2, jh:jh + NC - 1],
                                pos.unsqueeze(2).broadcast_to([HD, 8, NC - 1]), ALU.add)
                ins.then_inc(tok_free, 1)
            split_lo(1, 2)
            split_lo(1, 3)
            dve.wait_ge(xc_hi_done, 2)
            sub(xc_lo[1], x_cmp, xc_hi[1]).then_inc(xc_ready, 1)
            for j in range(4):
                split_lo(2, j)

            def gelu(v):
                gr = G_W1K + v
                dve.wait_ge(tok_done, gr + 1)
                dve.tensor_copy(g_h, ps[:, gr % 4, 0:256]).then_inc(tok_free, 1)
                dve.wait_ge(tok_free, gr + 1)
                order.after(dve.tensor_tensor(g_a, g_h, g_h, ALU.mult))
                order.after(dve.tensor_scalar(g_a, g_a, 0.044715, 1.0, ALU.mult, ALU.add))
                dve.tensor_tensor(g_a, g_a, g_h, ALU.mult).then_inc(gelu_arg, 1)
                dve.wait_ge(gelu_tanh, v + 1)
                order.after(dve.scalar_tensor_tensor(out=g_b, in0=g_a, scalar=1.0, in1=g_h, op0=ALU.add, op1=ALU.mult))
                dve.tensor_scalar(g_a, g_b, 0.5, None, ALU.mult).then_inc(hid_done, 1)
                dve.wait_ge(hid_hi, v + 1)
                sub(hid_t[:, 1, :], ps[:, 4, 0:256], hid_t[:, 0, :]).then_inc(hid_lo, 1)

            def rope_small(dst, src, cos, sin, tmp):
                h = ROT // 2
                dve.tensor_tensor(tmp[..., 0:h], src[..., h:ROT], sin[..., 0:h], ALU.mult)
                dve.tensor_tensor(dst, src[..., 0:ROT], cos, ALU.mult)
                order.after(dve.tensor_tensor(tmp[..., h:ROT], src[..., 0:h], sin[..., h:ROT], ALU.mult))
                return dve.tensor_tensor(dst, dst, tmp, ALU.add)

            def kv_evac(n, gr, br, t):
                bank = gr % 4
                dve.wait_ge(tok_done, gr + 1)
                dve.tensor_copy(k_raw[:, br, t, :], ps[:, bank, 0:256])
                vp = ps[:, bank, 256:512].rearrange("p (g c) -> p g c", g=GROUPS)
                order.after(dve.tensor_copy(v_all[:, t, br, :, 0:HD], vp))
                sub(v_all[:, t, br, :, HD:P], vp, v_all[:, t, br, :, 0:HD]).then_inc(tok_free, 1)

            gelu(0)
            for j in range(4):
                split_lo(B_SLC, j)
            dve.wait_ge(cmp_done, 1)
            order.after(dve.tensor_copy(kc_f, ps[:, 5, 0:HD]))
            order.after(dve.tensor_copy(kc_r[:, ROT:], kc_f[:, ROT:]))
            rope_small(kc_r[:, 0:ROT], kc_f, tab(C_CCOS, ROT), tab(C_CSIN, ROT), rtmp[:, 0:ROT]).then_inc(kc_roped, 1)
            dve.wait_ge(kc_hi, 2)
            sub(kc[0:HD, 1, :], ps[0:HD, 6, 0:P], kc[0:HD, 0, :])
            sub(kc[HD:P, 1, :], ps[0:HD, 6, 0:P], kc[0:HD, 0, :]).then_inc(cmp_ready, 1)
            gelu(1)
            for t in range(T):
                split_lo(B_WIN, t)
                kv_evac(B_SLC, G_SLC + t, 0, t)
            dve.wait_ge(cmp_done, 2)
            order.after(dve.tensor_copy(vc[:, 0:HD], ps[:, 5, 0:HD]))
            order.after(sub(vc[:, HD:P], ps[:, 5, 0:HD], vc[:, 0:HD]))
            for g in range(GROUPS):
                for h in range(HPG):
                    ins = dve.tensor_copy(vc_rep[NC * h:NC * (h + 1), g, :], vc[NC * g:NC * (g + 1), :].bitcast(F32))
            ins.then_inc(cmp_ready, 1)
            for t in range(T):
                split_lo(B_Q0, t)
                kv_evac(B_WIN, G_WIN + t, 1, t)
            for b in range(2):
                for t in range(T):
                    split_lo(B_Q1 + b, t)
                    dve.wait_ge(tok_done, G_Q + 4 * b + t + 1)
                    dve.tensor_copy(q_raw[:, t, NB * b:NB * (b + 1)], ps[:, (G_Q + 4 * b + t) % 4, :]).then_inc(tok_free, 1)
            for t in range(T):
                dve.wait_ge(tok_done, G_GATE + t + 1)
                dve.tensor_copy(gate[:, t, :], ps[:, (G_GATE + t) % 4, 0:48]).then_inc(tok_free, 1)
            dve.wait_ge(gate_tanh, 1)
            order.after(dve.tensor_scalar(gate[:, :, :], gate[:, :, :], 0.5, 0.5, ALU.mult, ALU.add))
            dve.wait_ge(lam_exp, 1)
            order.after(dve.tensor_tensor(lam2[:, 1:2], lam_s[:, 3:4], lam_s[:, 2:3], ALU.subtract))
            order.after(dve.tensor_scalar(lam2[:, 1:2], lam2[:, 1:2], -LAMBDA_INIT, None, ALU.add))
            order.after(dve.memset(lam2[:, 0:1], 1.0))

            cos4 = tab(C_COS, 64, T)
            sin4 = tab(C_SIN, 64, T)
            rq = rtmp[:, 0:256].rearrange("p (t h r) -> p t h r", t=T, h=HPG)
            rk = rtmp[:, 256:384].rearrange("p (b t r) -> p b t r", b=2, t=T)
            with dve.Fori(0, GROUPS) as g:
                order.enter(g, 2 + 4 + 16)
                h8 = ROT // 2
                qg = q_raw[:, :, bass.ds(g * 256, 256)].rearrange("p t (h d) -> p t h d", h=HPG)
                kg = k_raw[:, :, :, bass.ds(g * HD, HD)]
                cq = cos4.unsqueeze(2).broadcast_to([P, T, HPG, ROT])
                sq = sin4.unsqueeze(2).broadcast_to([P, T, HPG, ROT])
                rope_small(q_st[:, :, :, 0:ROT], qg, cq, sq, rq)
                ck = cos4.unsqueeze(1).broadcast_to([P, 2, T, ROT])
                sk = sin4.unsqueeze(1).broadcast_to([P, 2, T, ROT])
                rope_small(k_st.rearrange("p t b d -> p b t d")[:, :, :, 0:ROT], kg, ck, sk, rk).then_inc(roped, 1)
                for e in range(3):
                    dve.wait_ge(stack_hi, g * 3 + (e + 1))
                    for c in range(2):
                        r = HD * c
                        if e == 0:
                            for z in (0, HD):
                                ins = sub(k_stack[z:z + HD, 1, c, :], ps[r:r + HD, 0, :], k_stack[0:HD, 0, c, :])
                        else:
                            h = 2 * (e - 1) + c
                            ins = dve.scalar_tensor_tensor(out=q_stack[HD - r:P - r, h, :], in0=ps[r:r + HD, e, :],
                                                           scalar=SCALE, in1=q_stack[r:r + HD, h, :].bitcast(F32),
                                                           op0=ALU.mult, op1=ALU.subtract)
                    ins.then_inc(stack_lo, 1)

                def maxes(s):
                    n = P * (s % 4 + 1)
                    b = 2 * (s % 2)
                    dve.wait_ge(s_done, g * 16 + (s + 1))
                    dve.tensor_reduce(nmax[:, s % 2, :], ps[:, b:b + 2, 0:n], X, ALU.max, negate=True
                                      ).then_inc(max_done, 1)

                def factors(s):
                    h, i = s // 4, s % 4
                    dve.wait_ge(exp_done, g * 32 + (2 * s + 2))
                    order.after(dve.reciprocal(rinv[:, s % 2, :], rsum[:, s % 2, :]))
                    gg = gate[:, i, :][:, bass.ds(g * 12 + (3 * h + 1), 2)]
                    dve.tensor_tensor(coef[:, s % 2, :], rinv[:, s % 2, :], gg, ALU.mult).then_inc(coef_done, 1)

                def turned_lo(s):
                    i = s % 4
                    dve.wait_ge(pt_hi, g * 16 + (s + 1))
                    dims = [[PT_BR, 2], [PT_ROW, i + 1], [1, P]]
                    dve.tensor_tensor(view(slot0[1], P * i, dims),
                                      view(ps[:, 4, :], 4 * NB, [[NB, 2], [P, i + 1], [1, P]]),
                                      view(slot0[0], P * i, dims).bitcast(F32), ALU.subtract).then_inc(pt_lo, 1)

                def out_sum(h):
                    r = HD * (h % 2)
                    dve.wait_ge(o_half, g * 4 + (h + 1))
                    dve.tensor_tensor(o_buf[r:r + HD, :], ps[0:HD, 6, :], o_buf[r:r + HD, :], ALU.add).then_inc(o_sum, 1)

                def out_lo(h):
                    r = HD * (h % 2)
                    dve.wait_ge(o_hi, g * 4 + (h + 1))
                    pair = bass.ds(g * 2 + h // 2, 1)
                    sub(act_lo[r:r + HD, pair, :].rearrange("p o c -> p (o c)"), o_buf[r:r + HD, :],
                        act_hi[r:r + HD, pair, :].rearrange("p o c -> p (o c)")).then_inc(o_lo, 1)

                dve.wait_ge(cs_done, g + 1)
                e4 = c_sc.rearrange("p (i h n) -> p i h n", i=T, h=HPG)
                er = c_sc.rearrange("p (r n) -> p r n", n=NC)
                order.after(dve.tensor_tensor(e4, ps[:, 7, :].rearrange("p (i h n) -> p i h n", i=T, h=HPG),
                                              tab(C_CADD, 128, T).unsqueeze(2).broadcast_to([P, T, HPG, NC]), ALU.add))
                order.after(dve.tensor_reduce(c_st[:, 0, :], er, X, ALU.max))
                dve.tensor_tensor(er, er, c_st[:, 0, :].unsqueeze(2).broadcast_to([P, 16, NC]),
                                  ALU.subtract).then_inc(cs_sub, 1)
                maxes(0)
                dve.wait_ge(cs_exp, g + 1)
                order.after(dve.tensor_reduce(c_st[:, 1, :], er, X, ALU.add))
                order.after(dve.reciprocal(c_st[:, 2, :], c_st[:, 1, :]))
                gc = gate[:, :, bass.ds(g * 12, 12)].rearrange("p t (h b) -> p t h b", b=3)[:, :, :, 0]
                dve.tensor_tensor(c_st[:, 3, :].rearrange("p (t h) -> p t h", t=T),
                                  c_st[:, 2, :].rearrange("p (t h) -> p t h", t=T), gc, ALU.mult).then_inc(cs_coef, 1)
                for s in range(16):
                    factors(s)
                    if s == 1:
                        dve.wait_ge(pc_hi, g + 1)
                        sub(pct[1], ps[:, 7, :], pct[0]).then_inc(pc_lo, 1)
                    if s >= 1:
                        turned_lo(s - 1)
                    if s < 15:
                        maxes(s + 1)
                    if s >= 6 and s % 4 == 2:
                        out_sum((s - 6) // 4)
                    if s >= 7 and s % 4 == 3:
                        out_lo((s - 7) // 4)
                turned_lo(15)
                out_sum(3)
                out_lo(3)
            order.leave(GROUPS)

            def residual(gr, bank, t, dh):
                dve.wait_ge(tok_done, gr + 1)
                xs = x_res[:, t, NB * dh:NB * (dh + 1)]
                dve.tensor_tensor(xs, ps[:, bank, :], xs, ALU.add).then_inc(tok_free, 1)

            def norm_tail(q0):
                for t in range(T):
                    norm_z(q0 + t, t)

            def out_layer(b0, g0):
                for dh in range(2):
                    for t in range(T):
                        split_lo(b0 + 1 + dh, t)
                        residual(g0 + 4 * dh + t, (g0 + 4 * dh + t) % 4, t, dh)

            out_layer(B_OUT0, G_OUT0)
            norm_tail(4)

            def mlp_step(n, gr, up, last):
                for c in range(4):
                    for j in range(4):
                        if not (c == 3 and last == "end"):
                            split_lo(n + (c + 1), j, (B_MLP0 + c + 1) % 2)
                        if c < 2:
                            u = 4 * c + j
                            dve.wait_ge(up_free, up + (u + 1))
                            if u >= 2:
                                dve.wait_ge(a_ready, up + (u - 1))
                            dve.tensor_tensor(sq_b[:, u % 2, :], relu_b[:, u % 2, :], relu_b[:, u % 2, :],
                                              ALU.mult).then_inc(sq_done, 1)
                            dve.wait_ge(sq_done, up + (u + 1))
                            dve.wait_ge(a_hi_done, up + (u + 1))
                            sub(a_lo[:, u, :], sq_b[:, u % 2, :], a_hi[:, u, :]).then_inc(a_ready, 1)
                        else:
                            d = 4 * (c - 2) + j
                            residual(gr + d, (G_MLP0 + d) % 4, j, c - 2)

            def mlp_layer(n0, g0, u0, end):
                with dve.Fori(0, STEPS - 1) as it:
                    mlp_step(it * 4 + n0, it * 8 + g0, it * 8 + u0, None)
                k = STEPS - 1
                mlp_step(n0 + 4 * k, g0 + 8 * k, u0 + 8 * k, end)

            mlp_layer(B_MLP0, G_MLP0, 0, None)
            norm_tail(8)

            for b in range(6):
                for t in range(T):
                    split_lo(B_DIFF + b + 1, t)
                    gr = G_DIFF + 4 * b + t
                    dve.wait_ge(tok_done, gr + 1)
                    src = ps[:, gr % 4, :]
                    if b < 4:
                        raw = q_raw if b < 2 else dk_raw
                        dve.tensor_copy(raw[:, t, NB * (b % 2):NB * (b % 2 + 1)], src).then_inc(tok_free, 1)
                    else:
                        v = dv_all[:, t, 4 * (b - 4):4 * (b - 3), :]
                        vp = src.rearrange("p (h c) -> p h c", h=4)
                        order.after(dve.tensor_copy(v[:, :, 0:P], vp))
                        sub(v[:, :, P:2 * P], vp, v[:, :, 0:P]).then_inc(tok_free, 1)

            rd = rtmp[:, 0:128].rearrange("p (t c r) -> p t c r", t=T, c=2)
            rd2 = rtmp[:, 128:256].rearrange("p (t c r) -> p t c r", t=T, c=2)
            with dve.Fori(0, DH) as h:
                order.enter(h, 2 + 4 + 0)
                cd = cos4.unsqueeze(2).broadcast_to([P, T, 2, ROT])
                sd = sin4.unsqueeze(2).broadcast_to([P, T, 2, ROT])
                for z, raw, tmp in ((0, q_raw, rd), (1, dk_raw, rd2)):
                    ins = rope_small(d_st[:, :, z, :, 0:ROT],
                                     raw[:, :, bass.ds(h * P, P)].rearrange("p t (c d) -> p t c d", c=2), cd, sd, tmp)
                ins.then_inc(d_roped, 1)
                dve.wait_ge(d_hi, h * 2 + 1)
                for c in range(2):
                    r = HD * c
                    ins = dve.scalar_tensor_tensor(out=dq_stack[HD - r:P - r, c, :], in0=ps[r:r + HD, 0, :], scalar=SCALE,
                                                   in1=dq_stack[r:r + HD, c, :].bitcast(F32), op0=ALU.mult,
                                                   op1=ALU.subtract)
                ins.then_inc(d_lo, 1)
                dve.wait_ge(d_hi, h * 2 + 2)
                for c in range(2):
                    for r in (0, HD):
                        ins = sub(k_stack[r:r + HD, 1, c, :], ps[HD * c:HD * (c + 1), 1, :],
                                  k_stack[0:HD, 0, c, :])
                ins.then_inc(d_lo, 1)

                def d_max(i):
                    b = 2 * (i % 2)
                    dve.wait_ge(ds_done, h * 4 + (i + 1))
                    dve.tensor_reduce(nmax[:, i % 2, :], ps[:, b:b + 2, 0:P * (i + 1)], X, ALU.max, negate=True
                                      ).then_inc(dmax_done, 1)

                def d_turned_lo(i):
                    n = P * (i + 1)
                    dve.wait_ge(dpt_hi, h * 4 + (i + 1))
                    sub(dpt[1][:, i % 2, 0:n], ps[:, 4 + i % 2, 0:n], dpt[0][:, i % 2, 0:n]).then_inc(dpt_lo, 1)

                def d_out(i):
                    dve.wait_ge(dpv_done, h * 4 + (i + 1))
                    dve.tensor_reduce(o_buf[:, P * i:P * (i + 1)],
                                      ps[:, 6 + i % 2, 0:256].rearrange("p (z c) -> p c z", z=2), X, ALU.add
                                      ).then_inc(do_free, 1)

                d_max(0)
                for i in range(T):
                    n = P * (i + 1)
                    dve.wait_ge(dexp_done, h * 8 + (2 * i + 2))
                    order.after(dve.reciprocal(rinv[:, i % 2, :], rsum[:, i % 2, :]))
                    dve.tensor_tensor(coef[:, i % 2, :], rinv[:, i % 2, :], lam2[:, :], ALU.mult).then_inc(dcoef_done, 1)
                    if i >= 1:
                        d_turned_lo(i - 1)
                    if i < T - 1:
                        d_max(i + 1)
                    dve.wait_ge(dp1_done, h * 4 + (i + 1))
                    dve.wait_ge(dcoef_done, h * 4 + (i + 1))
                    dve.scalar_tensor_tensor(out=prob[:, i % 2, 0, 0:n], in0=prob[:, i % 2, 0, 0:n],
                                             scalar=coef[:, i % 2, 0:1], in1=prob[:, i % 2, 1, 0:n],
                                             op0=ALU.mult, op1=ALU.add).then_inc(da_done, 1)
                    if i >= 2:
                        d_out(i - 2)
                d_turned_lo(T - 1)
                d_out(T - 2)
                d_out(T - 1)
                dve.wait_ge(d_ss_done, h * 4 + 4)
                dve.tensor_scalar(d_ms, d_ss, 1.0 / P, EPS, ALU.mult, ALU.add).then_inc(d_ms_done, 1)
                dve.wait_ge(d_rs_done, h + 1)
                o4 = o_buf[:, :].rearrange("p (t c) -> p t c", t=T)
                dve.tensor_tensor(o4, o4, d_rs.unsqueeze(2).broadcast_to([P, T, P]), ALU.mult).then_inc(dy_done, 1)
                dve.wait_ge(do_turned, h + 1)
                dve.tensor_scalar(o_buf[:, :], ps[:, 4, :], subg[:, 0:1], None, ALU.mult).then_inc(dz_done, 1)
                dve.wait_ge(do_hi, h + 1)
                hh = bass.ds(h, 1)
                sub(act_lo[:, hh, :].rearrange("p o c -> p (o c)"), o_buf[:, :],
                    act_hi[:, hh, :].rearrange("p o c -> p (o c)")).then_inc(do_lo, 1)
            order.leave(DH)

            out_layer(B_OUT1, G_OUT1)
            norm_tail(12)
            mlp_layer(B_MLP1, G_MLP1, 32, "end")
            dve.wait_ge(gfin_landed, 16)
            for t in range(T):
                dve.wait_ge(rstd_done, 16 + t + 1)
                if t >= 2:
                    dve.wait_ge(stored[t % 2], 16)
                dve.scalar_tensor_tensor(out=fin[:, t % 2, :], in0=x_res[:, t, :], scalar=rstd[:, 16 + t:17 + t],
                                         in1=gfin, op0=ALU.mult, op1=ALU.mult).then_inc(z_done, 1)

        @block.tensor
        def _(pe):
            def mm(o, l, r, start, stop):
                return pe.matmul(o, l, r, start=start, stop=stop)

            def product(o, pairs, start=True, stop=True):
                for i, (l, r) in enumerate(pairs):
                    ins = mm(o, l, r, start and i == 0, stop and i == len(pairs) - 1)
                return ins

            def whole(n, sl=None):
                pe.wait_ge(lo_split, n * 4 + 4)

            def norm_turn(q, t):
                pe.wait_ge(y_done, q + 1)
                if q % 4 >= 2:
                    pe.wait_ge(z_done, q - 1)
                b = 4 + 2 * (t % 2)
                for k in range(KT):
                    ins = pe.transpose(ps[:, b + k // 4, P * (k % 4):P * (k % 4 + 1)], y_buf[:, P * k:P * (k + 1)], ident)
                ins.then_inc(turned, 1)

            def token_group(gr, bank, sl, t, n=NB, w=None):
                wh = (lambda k: w_hi[:, sl, NB * k:NB * (k + 1)]) if w is None else (lambda k: w[:, 0, n * k:n * (k + 1)])
                wl = (lambda k: w_lo[:, sl, NB * k:NB * (k + 1)]) if w is None else (lambda k: w[:, 1, n * k:n * (k + 1)])
                pairs = []
                for k in range(KT):
                    xh, xl = act_hi[:, k, P * t:P * (t + 1)], act_lo[:, k, P * t:P * (t + 1)]
                    pairs += [(xh, wh(k)), (xh, wl(k)), (xl, wh(k))]
                product(ps[:, bank, 0:n], pairs).then_inc(tok_done, 1)

            def feature_group(bank, sl, m):
                pairs = []
                for k in range(KT):
                    c = NB * k + P * m
                    wh, wl = w_hi[:, sl, c:c + P], w_lo[:, sl, c:c + P]
                    pairs += [(wh, act_hi[:, k, :]), (wh, act_lo[:, k, :]), (wl, act_hi[:, k, :])]
                return product(ps[:, bank, :], pairs)

            pe.wait_ge(cst_landed, 32)
            pe.wait_ge(small_lo, 4)
            for t in range(T):
                norm_turn(t, t)
            pe.wait_ge(act_ready, 4)
            whole(0)
            for m in range(4):
                feature_group(G_CMP + m, 0, m).then_inc(tok_done, 1)

            def hidden(n, v):
                whole(n)
                gr = G_W1K + v
                pe.wait_ge(xc_ready, v + 1)
                pe.wait_ge(tok_free, gr - 3)
                pairs = []
                for j in range(16):
                    wh, wl = (w[:, n % 2, 256 * j:256 * (j + 1)] for w in (w_hi, w_lo))
                    pairs += [(xc_hi[v][:, j, :], wh), (xc_hi[v][:, j, :], wl), (xc_lo[v][:, j, :], wh)]
                product(ps[:, gr % 4, 0:256], pairs).then_inc(tok_done, 1)

            def second(v):
                pe.wait_ge(hid_done, v + 1)
                for c in range(2):
                    ins = pe.transpose(ps[:, 4, P * c:P * (c + 1)], g_a[:, P * c:P * (c + 1)], ident)
                ins.then_inc(hid_turned, 1)
                pe.wait_ge(hid_lo, v + 1)
                pairs = []
                for c in range(2):
                    h, l = hid_t[:, 0, P * c:P * (c + 1)], hid_t[:, 1, P * c:P * (c + 1)]
                    wh, wl = (w2_r[:, z, P * v + HD * c:P * v + HD * (c + 1)] for z in range(2))
                    pairs += [(h, wh), (h, wl), (l, wh)]
                product(ps[:, 5, 0:HD], pairs).then_inc(cmp_done, 1)

            def token_block(n, g0, norm=None):
                whole(n)
                for t in range(T):
                    if norm is not None:
                        pe.wait_ge(act_ready, 4 * norm + t + 1)
                    pe.wait_ge(tok_free, g0 + t - 3)
                    token_group(g0 + t, (g0 + t) % 4, n % 2, t)

            hidden(B_W1K, 0)
            hidden(B_W1V, 1)
            second(0)
            pe.wait_ge(kc_roped, 1)
            pe.transpose(ps[0:HD, 6, 0:P], kc_r, ident).then_inc(kc_turned, 1)
            second(1)
            token_block(B_SLC, G_SLC)
            token_block(B_WIN, G_WIN)
            token_block(B_Q0, G_Q)
            token_block(B_Q1, G_Q + 4)
            for t in range(T):
                pe.wait_ge(tok_free, G_GATE + t - 3)
                token_group(G_GATE + t, (G_GATE + t) % 4, 0, t, 48, tail_r)

            pe.wait_ge(cmp_ready, 2)
            with pe.Fori(0, GROUPS) as g:
                pe.wait_ge(roped, g + 1)
                pe.wait_ge(rest_copied, g * 2 + 2)
                for e in range(3):
                    for t in range(T):
                        src = k_st[:, t, :, :] if e == 0 else q_st[:, t, 2 * (e - 1):2 * e, :]
                        ins = pe.transpose(ps[:, e, P * t:P * (t + 1)], src.rearrange("p h d -> p (h d)"), ident)
                    ins.then_inc(st_turned, 1)
                pe.wait_ge(stack_lo, g * 3 + 3)
                for h in range(HPG):
                    for i in range(T):
                        q = q_stack[:, h, P * i:P * (i + 1)]
                        c0 = P * i + NC * h
                        ins = product(ps[:, 7, c0:c0 + NC],
                                      [(q, kc[:, z, bass.ds(g * NC, NC)]) for z in range(2)])
                ins.then_inc(cs_done, 1)

                def scores(s):
                    h, i = s // 4, s % 4
                    n = P * (i + 1)
                    if s >= 2:
                        pe.wait_ge(exp_done, g * 32 + 2 * (s - 1))
                    q = q_stack[:, h, P * i:P * (i + 1)]
                    for br in range(2):
                        o = ps[:, 2 * (s % 2) + br, 0:n]
                        product(o, [(q, k_stack[:, z, br, 0:n]) for z in range(2)], stop=False)
                        ins = mm(o[:, n - P:n], ident_b[:, :], mask_b[:, :], False, True)
                    ins.then_inc(s_done, 1)

                def turn(s):
                    i = s % 4
                    pe.wait_ge(normed, g * 32 + (2 * s + 2))
                    if s >= 1:
                        pe.wait_ge(pt_lo, g * 16 + s)
                    for br in range(2):
                        for j in range(i + 1):
                            ins = pe.transpose(ps[:, 4 + br, P * j:P * (j + 1)], prob[:, s % 2, br, P * j:P * (j + 1)], ident)
                    ins.then_inc(p_turned, 1)

                def values(h):
                    pe.wait_ge(pt_lo, g * 16 + (4 * h + 4))
                    if h == 0:
                        pe.wait_ge(v_staged, g * 2 + 2)
                        pe.wait_ge(pc_lo, g + 1)
                    else:
                        pe.wait_ge(o_sum, g * 4 + h)
                    r = NC * h
                    for z in range(2):
                        mm(ps[:, 6, :], vc_st[r:r + NC, :], pct[z][r:r + NC, :], z == 0, False)
                    for br in range(2):
                        for j in range(T):
                            for z in range(2):
                                o0 = PT_BR * br + (PT_ROW + P) * j
                                ins = mm(ps[:, 6, P * j:S], v_st[:, j, br, :], slot0[z][:, o0:o0 + S - P * j], False,
                                         br == 1 and j == T - 1 and z == 1)
                    ins.then_inc(pv_done, 1)

                scores(0)
                scores(1)
                pe.wait_ge(pc_ready, g + 1)
                for i in range(T):
                    ins = pe.transpose(ps[:, 7, P * i:P * (i + 1)], c_sc[:, P * i:P * (i + 1)], ident)
                ins.then_inc(pc_turned, 1)
                for s in range(16):
                    turn(s)
                    if s >= 4 and s % 4 == 0:
                        values(s // 4 - 1)
                    if s + 2 < 16:
                        scores(s + 2)
                values(3)

            pe.wait_ge(o_lo, 4 * GROUPS)
            token_block(B_OUT0, G_OUT0)
            token_block(B_OUT0 + 1, G_OUT0 + 4)
            for t in range(T):
                norm_turn(4 + t, t)
            pe.wait_ge(act_ready, 8)

            def mlp_step(n, gr, up):
                for c in range(4):
                    sl = (B_MLP0 + c) % 2
                    whole(n + c)
                    for j in range(4):
                        if c < 2:
                            u = 4 * c + j
                            if u < 4:
                                pe.wait_ge(tok_free, gr + (u - 3))
                            else:
                                pe.wait_ge(up_free, up + (u - 3))
                            feature_group((u + 2) % 4, sl, j).then_inc(up_done, 1)
                            continue
                        d = 4 * (c - 2) + j
                        if d >= 4:
                            pe.wait_ge(tok_free, gr + (d - 3))
                        bank = (G_MLP0 + d) % 4
                        pairs = []
                        if d < 4:
                            pe.wait_ge(up_free, up + (d + 5))
                        for k in range(KT):
                            if d == 0:
                                pe.wait_ge(a_ready, up + (k + 1))
                            ah, al = a_hi[:, k, P * j:P * (j + 1)], a_lo[:, k, P * j:P * (j + 1)]
                            wh, wl = (w[:, sl, NB * k:NB * (k + 1)] for w in (w_hi, w_lo))
                            ins = product(ps[:, bank, :], [(ah, wh), (ah, wl), (al, wh)], k == 0, k == KT - 1)
                        ins.then_inc(tok_done, 1)

            def mlp_layer(n0, g0, u0):
                with pe.Fori(0, STEPS - 1) as it:
                    mlp_step(it * 4 + n0, it * 8 + g0, it * 8 + u0)
                k = STEPS - 1
                mlp_step(n0 + 4 * k, g0 + 8 * k, u0 + 8 * k)

            mlp_layer(B_MLP0, G_MLP0, 0)
            for t in range(T):
                norm_turn(8 + t, t)
            for b in range(6):
                token_block(B_DIFF + b, G_DIFF + 4 * b, 2)

            with pe.Fori(0, DH) as h:
                pe.wait_ge(d_roped, h + 1)
                pe.wait_ge(d_rest, h * 2 + 2)
                for z in range(2):
                    for t in range(T):
                        ins = pe.transpose(ps[:, z, P * t:P * (t + 1)],
                                           d_st[:, t, z, :, :].rearrange("p c d -> p (c d)"), ident)
                    ins.then_inc(d_turned, 1)
                pe.wait_ge(d_lo, h * 2 + 2)

                def d_scores(i):
                    n = P * (i + 1)
                    if i >= 2:
                        pe.wait_ge(dexp_done, h * 8 + 2 * (i - 1))
                    for c in range(2):
                        o = ps[:, 2 * (i % 2) + c, 0:n]
                        product(o, [(dq_stack[:, c, P * i:P * (i + 1)], k_stack[:, z, c, 0:n]) for z in range(2)],
                                stop=False)
                        ins = mm(o[:, n - P:n], ident_b[:, :], mask_b[:, :], False, True)
                    ins.then_inc(ds_done, 1)

                def d_turn(i):
                    pe.wait_ge(da_done, h * 4 + (i + 1))
                    if i >= 2:
                        pe.wait_ge(dpt_lo, h * 4 + (i - 1))
                    for j in range(i + 1):
                        ins = pe.transpose(ps[:, 4 + i % 2, P * j:P * (j + 1)], prob[:, i % 2, 0, P * j:P * (j + 1)], ident)
                    ins.then_inc(dp_turned, 1)

                def d_values(i):
                    pe.wait_ge(dpt_lo, h * 4 + (i + 1))
                    if i == 0:
                        pe.wait_ge(dv_staged, h + 1)
                    if i >= 2:
                        pe.wait_ge(do_free, h * 4 + (i - 1))
                    pairs = [(dpt[z][:, i % 2, P * j:P * (j + 1)], dv_st[:, j, :]) for j in range(i + 1) for z in range(2)]
                    product(ps[:, 6 + i % 2, 0:256], pairs).then_inc(dpv_done, 1)

                d_scores(0)
                d_scores(1)
                for i in range(T):
                    d_turn(i)
                    if i + 2 < T:
                        d_scores(i + 2)
                    if i >= 1:
                        d_values(i - 1)
                d_values(T - 1)
                pe.wait_ge(dy_done, h + 1)
                for t in range(T):
                    ins = pe.transpose(ps[:, 4, P * t:P * (t + 1)], o_buf[:, P * t:P * (t + 1)], ident)
                ins.then_inc(do_turned, 1)

            pe.wait_ge(do_lo, DH)
            token_block(B_OUT1, G_OUT1)
            token_block(B_OUT1 + 1, G_OUT1 + 4)
            for t in range(T):
                norm_turn(12 + t, t)
            pe.wait_ge(act_ready, 16)
            mlp_layer(B_MLP1, G_MLP1, 32)


def _constants():
    c = np.zeros((P, C_END), np.float32)
    c[:, C_ID:C_ID + P] = np.eye(P, dtype=np.float32)
    q = np.arange(P)
    c[:, C_MASK:C_MASK + P] = np.where(q[None, :] > q[:, None], np.float32(NEG), np.float32(0))
    inv = (np.float32(1.0) / (np.float32(500000.0) ** (np.arange(0, ROT, 2, dtype=np.float32) / np.float32(ROT)))
           ).astype(np.float32)

    def rope(pos):
        ang = pos.astype(np.float32)[:, None] * inv[None, :]
        co, si = np.cos(ang), np.sin(ang)
        return np.concatenate([co, co], 1), np.concatenate([-si, si], 1)

    for t in range(T):
        co, si = rope(P * t + q)
        c[:, C_COS + ROT * t:C_COS + ROT * (t + 1)] = co
        c[:, C_SIN + ROT * t:C_SIN + ROT * (t + 1)] = si
        ends = 16 * np.arange(NC) + 31
        seen = (ends[None, :] <= (P * t + q)[:, None]) & (np.arange(NC) < NC - 1)[None, :]
        c[:, C_CADD + NC * t:C_CADD + NC * (t + 1)] = np.where(seen, 0, NEG)
        c[:, C_CMUL + NC * t:C_CMUL + NC * (t + 1)] = seen
    co, si = rope(16 * (q % NC) + 31)
    c[:, C_CCOS:C_CCOS + ROT] = co
    c[:, C_CSIN:C_CSIN + ROT] = si
    return c


def kernel(x, attn_norm_g, mlp_norm_g, nsa_w_in, nsa_ck_pos, nsa_ck_w1, nsa_ck_w2, nsa_cv_pos, nsa_cv_w1, nsa_cv_w2,
           nsa_w_out, diff_w_in, diff_lq1, diff_lk1, diff_lq2, diff_lk2, diff_subln_g, diff_w_out, mlp_w_up,
           mlp_w_down, final_norm_g):
    import concourse.bacc as bacc
    from concourse.bass_utils import run_bass_kernel_spmd

    def by_partition(g):
        return np.ascontiguousarray(np.asarray(g).reshape(KT, P).T)

    def positions(pos):
        one = np.asarray(pos).reshape(16, 2, HD).transpose(2, 1, 0).reshape(HD, 32)
        return np.concatenate([one, one], 0)

    gains = [attn_norm_g[0], mlp_norm_g[0], attn_norm_g[1], mlp_norm_g[1]]
    vectors = np.concatenate([by_partition(g) for g in gains] + [positions(nsa_ck_pos[0]), positions(nsa_cv_pos[0]),
                             np.asarray(diff_subln_g[0]).reshape(P, 1)], 1)
    ins = {
        "x": np.asarray(x)[0], "consts": _constants(), "vectors": vectors,
        "w_in": np.asarray(nsa_w_in)[0], "ck_w1": np.asarray(nsa_ck_w1)[0], "ck_w2": np.asarray(nsa_ck_w2)[0],
        "cv_w1": np.asarray(nsa_cv_w1)[0], "cv_w2": np.asarray(nsa_cv_w2)[0], "w_out": np.asarray(nsa_w_out)[0],
        "diff_in": np.asarray(diff_w_in)[0], "diff_out": np.asarray(diff_w_out)[0],
        "w_up": np.asarray(mlp_w_up), "w_down": np.asarray(mlp_w_down),
        "lam_in": np.concatenate([np.asarray(v) for v in (diff_lq1, diff_lk1, diff_lq2, diff_lk2)], 1),
        "final_g": np.asarray(final_norm_g).reshape(1, D),
    }
    ins = {n: np.ascontiguousarray(v) for n, v in ins.items()}
    nc = bacc.Bacc("TRN2", target_bir_lowering=False, num_devices=1, dynamic_dma_scratch_size=1024)
    aps = {n: nc.dram_tensor(f"in_{n}", v.shape, mybir.dt.from_np(v.dtype), kind="ExternalInput").ap()
           for n, v in ins.items()}
    out = nc.dram_tensor("out", (S, D), F32, kind="ExternalOutput").ap()
    build(nc, aps, out)
    r = run_bass_kernel_spmd(nc, [{f"in_{n}": v for n, v in ins.items()}], core_ids=[0])
    return r.results[0]["out"].reshape(1, S, D)
```

```python
import math
from contextlib import ExitStack

import numpy as np
import concourse.bass as bass
from concourse import mybir

F32 = mybir.dt.float32
F32R = mybir.dt.float32r
BF16 = mybir.dt.bfloat16
ALU = mybir.AluOpType
ACT = mybir.ActivationFunctionType
X = mybir.AxisListType.X

P = 128
S = 512
D = 1024
T = S // P
KT = D // P
NB = 512
HD = 64
GROUPS = 4
HPG = 4
NC = 32
ROT = 16
FF = 4096
CHUNK = 1024
STEPS = FF // CHUNK
DH = 8
EPS = 1e-6
SCALE = HD ** -0.5
LAMBDA_INIT = 0.8 - 0.6 * math.exp(-0.3)
GELU_C = math.sqrt(2.0 / math.pi)
NEG = -1e30
PT_ROW = 384
PT_BR = 1664

C_ID, C_MASK, C_COS, C_SIN, C_CCOS, C_CSIN, C_CADD, C_CMUL, C_END = (
    0, 128, 256, 320, 384, 400, 416, 544, 548)
V_POS, V_SUB, V_END = 0, 64, 65

B_CMP, B_W1K, B_W1V, B_SLC, B_WIN, B_Q0, B_Q1, B_OUT0 = 0, 1, 2, 3, 4, 5, 6, 7
B_MLP0, B_DIFF, B_OUT1, B_MLP1, B_ALL = 9, 25, 31, 33, 49
G_CMP, G_W1K, G_W1V, G_SLC, G_WIN, G_Q, G_GATE, G_OUT0 = 0, 4, 5, 6, 10, 14, 22, 26
G_MLP0, G_DIFF, G_OUT1, G_MLP1 = 34, 66, 90, 98


def build(nc, a, out):
    with ExitStack() as ctx:
        def sb(name, shape, dt=F32):
            return ctx.enter_context(nc.sbuf_tensor(name, shape, dt))

        def sem(name):
            return ctx.enter_context(nc.semaphore(name))

        x_res = sb("x_res", [P, T, D])
        act_hi = sb("act_hi", [P, KT, S], F32R)
        act_lo = sb("act_lo", [P, KT, S], F32R)
        w_raw = sb("w_raw", [P, 4, 1024])
        w_hi = sb("w_hi", [P, 2, 4096], F32R)
        w_lo = sb("w_lo", [P, 2, 4096], F32R)
        kst = sb("kst", [P, 2, 2, 2, S], F32R)
        ar_r = sb("ar_r", [P, 8192], F32R)
        ar_f = sb("ar_f", [P, 10240])
        o_buf = sb("o_buf", [P, S])
        rtmp = sb("rtmp", [P, 256])
        cst = sb("cst", [P, C_END])
        vec = sb("vec", [P, V_END])
        ident_b = sb("ident_b", [P, P], BF16)
        mask_b = sb("mask_b", [P, P], BF16)
        lam2 = sb("lam2", [P, 2])
        st = sb("st", [P, 96])
        ps = ctx.enter_context(nc.psum_tensor("ps", [P, 8, NB], F32))

        ident = cst[:, C_ID:C_ID + P]

        def tab(c0, n, t=None):
            v = cst[:, c0:c0 + n]
            return v if t is None else v.rearrange("p (t r) -> p t r", t=t)

        def view(base, off, dims):
            return bass.AP(base.tensor, off, [list(base.ap[0])] + [list(d) for d in dims])

        HALF = D // 2
        y_bufs = [ar_f[:, 8192:9216], ar_f[:, 5120:6144]]
        gain = ar_f[:, 9216:10240]
        junk = ar_f[:, 7168:8192]
        x_cmp = ar_f[:, 8192:10240].rearrange("p (j c) -> p j c", j=16)
        q_raw = ar_f[:, 0:4096].rearrange("p (t c) -> p t c", t=T)
        k_raw = ar_f[:, 4096:6144].rearrange("p (b t c) -> p b t c", b=2, t=T)
        lamv_in = ar_f[:, 4096:4352]
        gate = ar_f[:, 7424:7616].rearrange("p (t c) -> p t c", t=T)
        gate_st = ar_f[:, 7616:7664].rearrange("p (t c) -> p t c", t=T)
        stage = ar_f[:, 6144:7168].rearrange("p (u t c) -> p u t c", u=2, t=T)
        c_sc = ar_f[:, 7680:8192]
        probs = ar_f[:, 8192:10240].rearrange("p (u k) -> p u k", u=4)
        g_h, g_a, g_b = (ar_f[:, 6144 + 256 * i:6400 + 256 * i] for i in range(3))
        kc_f = ar_f[:, 6912:6976]
        kc_r = ar_f[:, 6976:7040]
        tail_raw = ar_f[:, 0:384]
        w2_raw = ar_f[:, 384:640]
        relu_b = ar_f[:, 0:1024].rearrange("p (u c) -> p u c", u=2)
        sq_b = ar_f[:, 1024:2048].rearrange("p (u c) -> p u c", u=2)
        gfin = ar_f[:, 2048:3072]
        fin = ar_f[:, 3072:5120].rearrange("p (u c) -> p u c", u=2)
        dk_raw = ar_f[:, 4096:8192].rearrange("p (t c) -> p t c", t=T)

        xc_hi = [ar_r[:, 4096 * v:4096 * v + 2048].rearrange("p (j c) -> p j c", j=16) for v in range(2)]
        xc_lo = [ar_r[:, 4096 * v + 2048:4096 * v + 4096].rearrange("p (j c) -> p j c", j=16) for v in range(2)]
        v_all = ar_r[:, 0:4096].rearrange("p (t b g c) -> p t b g c", t=T, b=2, g=GROUPS)
        v_st = ar_r[:, 4096:5120].rearrange("p (t b c) -> p t b c", t=T, b=2)
        kc = ar_r[:, 5120:5376].rearrange("p (z c) -> p z c", z=2)
        vc = ar_r[:, 5376:5504]
        vc_st = ar_r[:, 5504:5632]
        vc_rep = ar_r[:, 5632:6144].rearrange("p (g c) -> p g c", g=GROUPS)
        q_stack = ar_r[:, 6144:8192].rearrange("p (h q) -> p h q", h=HPG)
        k_stack = kst[:, 0]
        early = kst[:, 1].rearrange("p z b q -> p (z b q)")
        tail_r = early[:, 0:768].rearrange("p (z c) -> p z c", z=2)
        hid_t = early[:, 1024:1536].rearrange("p (z c) -> p z c", z=2)
        w2_r = early[:, 1536:2048].rearrange("p (z c) -> p z c", z=2)
        a_hi = ar_r[:, 0:4096].rearrange("p (f c) -> p f c", f=8)
        a_lo = ar_r[:, 4096:8192].rearrange("p (f c) -> p f c", f=8)
        dv_all = ar_r[:, :].rearrange("p (t h c) -> p t h c", t=T, h=DH)
        slot0 = [w_hi[:, 0, :], w_lo[:, 0, :]]
        pct = [s[:, 3328:3840] for s in slot0]
        dq_stack = w_hi[:, 0, 1024:2048].rearrange("p (c q) -> p c q", c=2)
        dk_stage = w_lo[:, 0, 1024:3072].rearrange("p (c z t d) -> p c z t d", c=2, z=2, t=T)
        dq_stage = w_lo[:, 0, 3072:4096].rearrange("p (a t c d) -> p a t c d", a=2, t=2, c=2)
        dpt = [s[:, 0:1024].rearrange("p (u c) -> p u c", u=2) for s in slot0]

        ss1, pre, rstd = st[:, 0:20], st[:, 20:40], st[:, 40:60]
        ss2 = sb("ss2", [P, 20])
        d_ss, d_ms, d_rs = st[:, 76:80], st[:, 80:84], st[:, 84:88]
        half = st[:, 88:92]
        lam_s = st[:, 92:96]
        c_st = sb("c_st", [P, 4, 16])
        one = sb("one", [P, 1])
        nmax4, rsum4, rinv4 = st[:, 60:64], st[:, 64:68], st[:, 68:72]
        subg = sb("subg", [P, 1])

        x_landed = [sem(f"x_landed{t}") for t in range(T)]
        cst_landed, small_landed, gfin_landed = sem("cst_landed"), sem("small_landed"), sem("gfin_landed")
        part_landed = [sem(f"part_landed{j}") for j in range(4)]
        stored = [sem(f"stored{u}") for u in range(2)]
        hi_split, lo_split = sem("hi_split"), sem("lo_split")
        small_hi, small_lo = sem("small_hi"), sem("small_lo")
        tok_done, tok_free = sem("tok_done"), sem("tok_free")
        up_done, up_free, a_hi_done, a_ready = sem("up_done"), sem("up_free"), sem("a_hi_done"), sem("a_ready")
        sq_done = sem("sq_done")
        ss1_done, ss2_done, rstd_done = sem("ss1_done"), sem("ss2_done"), sem("rstd_done")
        y_done, turned, act_hi_done, act_ready, fin_done = (
            sem(n) for n in ("y_done", "turned", "act_hi_done", "act_ready", "fin_done"))
        gain_landed = sem("gain_landed")
        xc_hi_done, xc_ready = sem("xc_hi_done"), sem("xc_ready")
        gelu_arg, gelu_tanh, hid_done, hid_turned = sem("gelu_arg"), sem("gelu_tanh"), sem("hid_done"), sem("hid_turned")
        hid_hi, hid_lo, cmp_done, kc_roped, kc_turned, kc_hi = (
            sem(n) for n in ("hid_hi", "hid_lo", "cmp_done", "kc_roped", "kc_turned", "kc_hi"))
        cmp_ready = sem("cmp_ready")
        gate_tanh = sem("gate_tanh")
        lam_arg, lam_exp = sem("lam_arg"), sem("lam_exp")
        roped, gates_ready, gate_staged, stage_hi, stage_filled, st_turned, stacked_a, stacked_v = (
            sem(n) for n in ("roped", "gates_ready", "gate_staged", "stage_hi", "stage_filled", "st_turned",
                             "stacked_a", "stacked_v"))
        v_staged, cs_done, cs_sub, cs_exp, cs_coef, pc_ready, pc_turned, pc_hi, pc_lo = (
            sem(n) for n in ("v_staged", "cs_done", "cs_sub", "cs_exp", "cs_coef", "pc_ready", "pc_turned",
                             "pc_hi", "pc_lo"))
        cs_masked, cs_max, cs_sum, cs_inv = (sem(n) for n in ("cs_masked", "cs_max", "cs_sum", "cs_inv"))
        s_done, max_done, exp_done, rinv_done, normed, p_turned, pt_hi, pt_lo = (
            sem(n) for n in ("s_done", "max_done", "exp_done", "rinv_done", "normed", "p_turned", "pt_hi", "pt_lo"))
        pv_done, o_half, o_sum, o_hi, o_lo = (sem(n) for n in ("pv_done", "o_half", "o_sum", "o_hi", "o_lo"))
        d_roped, dq_hi, dk_filled, dq_filled, dk_turned, dq_turned, dk_stacked_a, dk_stacked_v, dq_stacked = (
            sem(n) for n in ("d_roped", "dq_hi", "dk_filled", "dq_filled", "dk_turned", "dq_turned", "dk_stacked_a",
                             "dk_stacked_v", "dq_stacked"))
        ds_done, dmax_done, dexp_done, drinv_done, dp1_done, da_done, dp_turned, dpt_hi, dpt_lo = (
            sem(n) for n in ("ds_done", "dmax_done", "dexp_done", "drinv_done", "dp1_done", "da_done", "dp_turned",
                             "dpt_hi", "dpt_lo"))
        dpv_done, do_free, d_ss_done, d_ms_done, d_rs_done, dy_done, do_turned, do_hi, do_lo = (
            sem(n) for n in ("dpv_done", "do_free", "d_ss_done", "d_ms_done", "d_rs_done", "dy_done", "do_turned",
                             "do_hi", "do_lo"))
        dve_order, act_order, pool_order = sem("dve_order"), sem("act_order"), sem("pool_order")
        pool_passed = sem("pool_passed")

        class Order:

            def __init__(self, eng, s):
                self.eng, self.s, self.base, self.loop = eng, s, 0, 0

            def after(self, ins):
                ins.then_inc(self.s, 1)
                self.base += 1
                self.eng.wait_ge(self.s, self.loop + self.base)

            def enter(self, i, per):
                self.loop, self.at, self.per = i * per, self.base, per

            def leave(self, count):
                assert self.base == self.at + self.per, (self.base - self.at, self.per)
                self.base, self.loop = self.at + self.per * count, 0

        SLOT0 = -22
        UNITS = 2 * HPG * T
        L_MAX, L_EXP, L_NORM, L_TURN, L_SPLIT, L_PV = 1, 2, 3, 4, 5, 6
        TURNS = (-19, -17, -15, -13, -11, -9, -7, 0)

        def at(gg, per, n):
            g, off = gg
            assert isinstance(g, int) or off * per + n > 0, (off, per, n)
            return g * per + (off * per + n)

        def place(gg, per, n):
            return gg[0] * per + (gg[1] * per + n)

        def first(gg):
            return isinstance(gg[0], int) and sum(gg) == 0

        def await_(eng, s, value):
            if not isinstance(value, int) or value > 0:
                return eng.wait_ge(s, value)

        def windows(eng, slot, s0, units, spans, count):
            def window(groups):
                for k in range(s0, s0 + units):
                    for span, gg in groups:
                        slot(gg, k + units * span)

            for m in range(spans - 1):
                window([(w, (m - w, 0)) for w in reversed(range(m + 1))])
            with eng.Fori(0, count - spans + 1) as g:
                window([(w, (g, spans - 1 - w)) for w in reversed(range(spans))])
            for m in range(count, count + spans - 1):
                window([(w, (m - w, 0)) for w in reversed(range(m - count + 1, spans))])

        def keys(gg, z, br, n=S):
            g, off = gg
            par = (g + off) % 2
            if isinstance(par, int):
                return kst[:, par, z, br, 0:n]
            return kst[:, bass.ds(par, 1), z, br, 0:n].rearrange("p o c -> p (o c)")

        def unit(v):
            return v // 8, v // 4 % 2, v % 4, P * (v % 4 + 1)

        D_SLOT0, D_UNITS, D_SPANS = -10, 2 * T, 4
        D_TURN_K, D_TURN_Q = (-8, -7, -6, -5), (-4, -1)
        D_P1, D_A, D_TURN, D_SPLIT, D_PV, D_OUT, D_SS = 4, 5, 6, 7, 8, 9, 10
        D_MS, D_Y, D_OUT_TURN, D_OUT_SPLIT = 17, 18, 20, 21

        def tile_at(k, lag):
            return (k - lag) // 2 if 0 <= k - lag < 2 * T and (k - lag) % 2 == 0 else None

        def cols(w, c0, j):
            return w[256 * j:256 * (j + 1), c0:c0 + NB].rearrange("(k p) c -> p k c", p=P)

        CMP0, SLC0, WIN0, TAIL0 = D, D + 512, D + 1024, D + 1536

        def part_source(n, j):
            if n in (B_W1K, B_W1V):
                w = a["ck_w1"] if n == B_W1K else a["cv_w1"]
                return w[512 * j:512 * (j + 1), :].rearrange("(k p) c -> p k c", p=P)
            if n < B_OUT0:
                c0 = {B_CMP: CMP0, B_SLC: SLC0, B_WIN: WIN0, B_Q0: 0, B_Q1: NB}[n]
                return cols(a["w_in"], c0, j)
            if n < B_MLP0:
                return cols(a["w_out"], NB * (n - B_OUT0), j)
            if n < B_OUT1:
                return cols(a["diff_in"], NB * (n - B_DIFF), j)
            return cols(a["diff_out"], NB * (n - B_OUT1), j)

        def mlp_source(layer, it, c, j):
            if c < 2:
                w = a["w_up"][layer, 256 * j:256 * (j + 1), bass.ds(it * CHUNK + NB * c, NB)]
            else:
                w = a["w_down"][layer, bass.ds(it * CHUNK + 256 * j, 256), NB * (c - 2):NB * (c - 1)]
            return w.rearrange("(k p) c -> p k c", p=P)

        def slot_of(n):
            return n % 2

        block = ctx.enter_context(nc.Block())

        @block.sync
        def _(sp):
            for t in range(T):
                sp.dma_start(x_res[:, t, :], a["x"][P * t:P * (t + 1), :]).then_inc(x_landed[t], 16)

            def load(n, j, src):
                if not isinstance(n, int) or n > 0:
                    sp.wait_ge(lo_split, n * 4 + (j - 3))
                if len(src.shape) == 3 and src.shape[1] == 4:
                    dst = w_raw[:, j, :].rearrange("p (k c) -> p k c", k=4)
                else:
                    dst = w_raw[:, j, :].rearrange("p (k c) -> p k c", k=2)
                sp.dma_start(dst, src).then_inc(part_landed[j], 16)

            def straight(n0, n1):
                for n in range(n0, n1):
                    for j in range(4):
                        load(n, j, part_source(n, j))

            straight(0, B_MLP0)
            with sp.Fori(0, STEPS) as it:
                for c in range(4):
                    for j in range(4):
                        load(it * 4 + (B_MLP0 + c), j, mlp_source(0, it, c, j))
            straight(B_DIFF, B_MLP1)
            with sp.Fori(0, STEPS) as it:
                for c in range(4):
                    for j in range(4):
                        load(it * 4 + (B_MLP1 + c), j, mlp_source(1, it, c, j))
            for t in range(T):
                for b in range(2):
                    sp.wait_ge(fin_done, 2 * t + b + 1)
                    sp.dma_start(out[P * t:P * (t + 1), HALF * b:HALF * (b + 1)],
                                 fin[:, t % 2, HALF * b:HALF * (b + 1)]).then_inc(stored[t % 2], 16)
            for u in range(2):
                sp.wait_ge(stored[u], 16 * T)

        @block.gpsimd
        def _(pool):
            order = Order(pool, pool_order)
            order.after(pool.memset(half, -0.5))

            def norm_stat(q):
                pool.wait_ge(ss1_done, q + 1)
                order.after(pool.tensor_scalar(pre[:, q:q + 1], ss1[:, q:q + 1], 1.0, EPS, ALU.mult, ALU.add))
                pool.wait_ge(ss2_done, q + 1)
                order.after(pool.tensor_tensor(pre[:, q:q + 1], ss2[:, q:q + 1], pre[:, q:q + 1], ALU.add))
                pool.tensor_tensor(rstd[:, q:q + 1], pre[:, q:q + 1], half[:, 0:1], ALU.pow).then_inc(rstd_done, 1)

            for q in range(4):
                norm_stat(q)

            order.after(pool.memset(one[:, :], 1.0))

            def hold(s, value):
                if not isinstance(value, int) or value > 0:
                    pool.wait_ge(s, value).then_inc(pool_passed, 1)

            def fill(gg, e):
                if first(gg):
                    pool.wait_ge(roped, 8 if e < 4 else 12)
                hold(st_turned, at(gg, 8, e - 1))
                hold(stage_filled, at(gg, 8, e))
                if e < 4:
                    br, z = e // 2, e % 2
                    src = k_raw[:, br, :, bass.ds(place(gg, HD, 0), HD)].unsqueeze(2).broadcast_to([P, T, 2, HD])
                    dst = stage[:, z].rearrange("p t (u d) -> p t u d", u=2)
                    if z == 0:
                        pool.tensor_tensor(dst.bitcast(F32R), src, one[:, :].unsqueeze(2).unsqueeze(2).broadcast_to([P, T, 2, HD]),
                                           ALU.mult).then_inc(stage_filled, 1)
                    else:
                        hi = stage[:, 0].rearrange("p t (u d) -> p t u d", u=2)
                        pool.tensor_tensor(dst, src, hi, ALU.subtract).then_inc(stage_filled, 1)
                else:
                    h = e - 4
                    src = q_raw[:, :, bass.ds(place(gg, HPG * HD, HD * h), HD)]
                    hi, lo = stage[:, e % 2, :, 0:HD], stage[:, e % 2, :, HD:P]
                    pool.tensor_tensor(hi.bitcast(F32R), src, one[:, :].unsqueeze(2).broadcast_to([P, T, HD]),
                                       ALU.mult).then_inc(stage_hi, 1)
                    hold(stage_hi, at(gg, HPG, h + 1))
                    pool.tensor_tensor(lo, src, hi, ALU.subtract).then_inc(stage_filled, 1)

            def stage_values(gg, br):
                hold(pv_done, at(gg, 8, br - 1))
                pool.tensor_tensor(v_st[:, :, br, :], v_all[:, :, br, bass.ds(place(gg, 1, 0), 1), :].bitcast(F32)
                                   .rearrange("p t o c -> p t (o c)"), one[:, :].unsqueeze(2).broadcast_to([P, T, P]),
                                   ALU.mult).then_inc(v_staged, 1)
                if br == 1:
                    pool.tensor_tensor(vc_st, vc_rep[:, bass.ds(place(gg, 1, 0), 1), :].bitcast(F32)
                                       .rearrange("p o c -> p (o c)"), one[:, :].broadcast_to([P, P]),
                                       ALU.mult).then_inc(v_staged, 1)

            def norm_probs(gg, v):
                h, br, i, n = unit(v)
                if v == 0:
                    if first(gg):
                        pool.wait_ge(gates_ready, 1)
                    hold(normed, at(gg, UNITS, 0))
                    pool.tensor_copy(gate_st[:, :, :], gate[:, :, bass.ds(place(gg, 3 * HPG, 0), 3 * HPG)]
                                     ).then_inc(gate_staged, 1)
                    hold(gate_staged, at(gg, 1, 1))
                hold(rinv_done, at(gg, UNITS, v + 1))
                p = probs[:, v % 4, 0:n]
                pool.tensor_scalar(p, p, rinv4[:, v % 4:v % 4 + 1], gate_st[:, i, 3 * h + 1 + br:3 * h + 2 + br],
                                   ALU.mult, ALU.mult).then_inc(normed, 1)

            def slot(gg, k):
                if 0 <= k - L_NORM < UNITS:
                    norm_probs(gg, k - L_NORM)
                if k + 2 in TURNS:
                    fill(gg, TURNS.index(k + 2))
                if k == 3:
                    stage_values(gg, 0)
                if k == 7:
                    stage_values(gg, 1)
                if k == 10:
                    hold(cs_coef, at(gg, 1, 1))
                    ef = c_sc.rearrange("p (r n) -> p r n", n=NC)
                    pool.tensor_tensor(ef, ef, c_st[:, 3, :].unsqueeze(2).broadcast_to([P, 16, NC]),
                                       ALU.mult).then_inc(pc_ready, 1)
                if first(gg) and k == SLOT0 + UNITS - 1:
                    pool.wait_ge(roped, 16)

            windows(pool, slot, SLOT0, UNITS, 2, GROUPS)

            for q in range(4, 12):
                norm_stat(q)

            pool.wait_ge(d_roped, 16)
            pool.wait_ge(tok_done, G_OUT1)

            def fill_keys(hh, e):
                c, z = e // 2, e % 2
                src = dk_raw[:, :, bass.ds(place(hh, P, HD * c), HD)].unsqueeze(2).broadcast_to([P, T, 2, HD])
                hi, dst = (dk_stage[:, c, zz].rearrange("p t (u d) -> p t u d", u=2) for zz in (0, z))
                hold(dk_turned, at(hh, 4, e + 1 - 4))
                if z == 0:
                    pool.tensor_tensor(dst, src, one[:, :].unsqueeze(2).unsqueeze(2).broadcast_to([P, T, 2, HD]),
                                       ALU.mult).then_inc(dk_filled, 1)
                else:
                    hold(dk_filled, at(hh, 4, e))
                    pool.tensor_tensor(dst, src, hi.bitcast(F32), ALU.subtract).then_inc(dk_filled, 1)

            def fill_queries(hh, a):
                hold(dq_turned, at(hh, 2, a + 1 - 2))
                hi, lo = dq_stage[:, a, :, :, 0:HD], dq_stage[:, a, :, :, HD:P]
                src = q_raw[:, 2 * a:2 * a + 2, bass.ds(place(hh, P, 0), P)].rearrange("p t (c d) -> p t c d", c=2)
                pool.tensor_tensor(hi, src, one[:, :].unsqueeze(2).unsqueeze(2).broadcast_to([P, 2, 2, HD]),
                                   ALU.mult).then_inc(dq_hi, 1)
                hold(dq_hi, at(hh, 2, a + 1))
                pool.tensor_tensor(lo, src, hi.bitcast(F32), ALU.subtract).then_inc(dq_filled, 1)

            def d_slot(hh, k):
                i = tile_at(k, D_P1)
                if i is not None:
                    hold(drinv_done, at(hh, D_UNITS, 2 * i + 2))
                    u = (2 * i + 1) % 4
                    p = probs[:, u, 0:P * (i + 1)]
                    pool.tensor_scalar(p, p, rinv4[:, u:u + 1], lam2[:, 1:2], ALU.mult, ALU.mult).then_inc(dp1_done, 1)
                if k == D_MS:
                    hold(d_ms_done, at(hh, 1, 1))
                    pool.tensor_tensor(d_rs, d_ms, half, ALU.pow).then_inc(d_rs_done, 1)
                if k + 2 in D_TURN_K:
                    fill_keys(hh, D_TURN_K.index(k + 2))
                if k + 2 in D_TURN_Q:
                    fill_queries(hh, D_TURN_Q.index(k + 2))

            windows(pool, d_slot, D_SLOT0, D_UNITS, D_SPANS, DH)
            for q in range(12, 20):
                norm_stat(q)

        @block.scalar
        def _(act):
            order = Order(act, act_order)
            act.dma_start(cst[:, :], a["consts"]).then_inc(cst_landed, 16)
            act.dma_start(vec[:, :], a["vectors"]).then_inc(cst_landed, 16)
            act.dma_start(tail_raw.rearrange("p (k c) -> p k c", k=KT),
                          a["w_in"][:, TAIL0:TAIL0 + 48].rearrange("(k p) c -> p k c", p=P)).then_inc(small_landed, 16)
            for v, w in enumerate((a["ck_w2"], a["cv_w2"])):
                act.dma_start(w2_raw[:, P * v:P * (v + 1)].rearrange("p (k c) -> p k c", k=2),
                              w.rearrange("(k p) c -> p k c", p=P)).then_inc(small_landed, 16)
            act.dma_start(lamv_in[:, :], a["lam_in"].partition_broadcast(P).rearrange("p o c -> p (o c)")
                          ).then_inc(small_landed, 16)

            def split_hi(n, j):
                act.wait_ge(part_landed[j], n * 16 + 16)
                act.copy(w_hi[:, slot_of(n), 1024 * j:1024 * (j + 1)], w_raw[:, j, :]).then_inc(hi_split, 1)

            def load_gain(r):
                act.dma_start(gain, a["norm_g"][r:r + 1, :].partition_broadcast(P).rearrange("p o c -> p (o c)")
                              ).then_inc(gain_landed, 16)

            def norm_sum(q, t, b):
                done = (ss1_done, ss2_done)[b]
                if q:
                    act.wait_ge(done, q)
                act.activation(junk[:, HALF * b:HALF * (b + 1)], x_res[:, t, HALF * b:HALF * (b + 1)], ACT.Square,
                               scale=D ** -0.5, accum_out=(ss1, ss2)[b][:, q:q + 1]).then_inc(done, 1)

            def norm_hi(q, t):
                for b in range(2):
                    act.wait_ge(turned, 2 * q + b + 1)
                    act.copy(act_hi[:, 4 * b:4 * b + 4, P * t:P * (t + 1)],
                             ps[:, 4 + 2 * (q % 2) + b, :].rearrange("p (k c) -> p k c", c=P)).then_inc(act_hi_done, 1)

            def norm_first(q0, g):
                for t in range(T):
                    act.wait_ge(tok_free, g + t + 1)
                    norm_sum(q0 + t, t, 0)

            def norm_tail(q0, g, last=False):
                for t in range(T):
                    act.wait_ge(tok_free, g + t + 1)
                    norm_sum(q0 + t, t, 1)
                    if t and not last:
                        norm_hi(q0 + t - 1, t - 1)
                if not last:
                    norm_hi(q0 + T - 1, T - 1)

            load_gain(0)
            act.wait_ge(small_landed, 64)
            act.copy(tail_r[:, 0, :], tail_raw).then_inc(small_hi, 1)
            act.copy(w2_r[:, 0, :], w2_raw).then_inc(small_hi, 1)
            for t in range(T):
                act.wait_ge(x_landed[t], 16)
                norm_sum(t, t, 0)
                norm_sum(t, t, 1)
                if t:
                    norm_hi(t - 1, t - 1)
                split_hi(0, t)
            norm_hi(T - 1, T - 1)

            def split_next(n, j, wait):
                if j == 0:
                    act.wait_ge(*wait)
                split_hi(n, j)

            for j in range(2):
                split_hi(1, j)
            act.wait_ge(tok_free, G_CMP + 2)
            act.copy(xc_hi[0], x_cmp).then_inc(xc_hi_done, 1)
            for j in range(2, 4):
                split_hi(1, j)
            act.wait_ge(tok_free, G_CMP + 4)
            act.copy(xc_hi[1], x_cmp).then_inc(xc_hi_done, 1)
            for j in range(4):
                split_next(B_W1V, j, (tok_done, G_W1K))

            def gelu(v):
                act.wait_ge(gelu_arg, v + 1)
                act.activation(g_a, g_a, ACT.Tanh, scale=GELU_C).then_inc(gelu_tanh, 1)
                act.wait_ge(hid_turned, v + 1)
                act.copy(hid_t[:, 0, :], ps[:, 4, 0:256]).then_inc(hid_hi, 1)

            for j in range(4):
                split_next(B_SLC, j, (tok_done, G_W1V))
            gelu(0)
            act.wait_ge(kc_turned, 1)
            act.copy(kc[0:HD, 0, :], ps[0:HD, 6, 0:P]).then_inc(kc_hi, 1)
            act.copy(kc[HD:P, 0, :], ps[0:HD, 6, 0:P]).then_inc(kc_hi, 1)
            for j in range(4):
                split_next(B_WIN, j, (tok_done, G_SLC))
            gelu(1)
            for j in range(4):
                split_next(B_Q0, j, (tok_done, G_WIN))
            for j in range(4):
                split_next(B_Q1, j, (tok_done, G_Q))
            for j in range(4):
                split_next(B_OUT0, j, (tok_done, G_Q + 4))
            act.wait_ge(tok_free, G_GATE + T)
            act.activation(gate[:, :, :], gate[:, :, :], ACT.Tanh, scale=0.5).then_inc(gate_tanh, 1)
            act.wait_ge(lam_arg, 1)
            act.activation(lam_s[:, 2:4], lam_s[:, 0:2], ACT.Exp).then_inc(lam_exp, 1)

            def stack(gg, e):
                act.wait_ge(st_turned, at(gg, 8, e + 1))
                if e < 4:
                    act.copy(keys(gg, 0, e // 2), ps[:, 7, :]).then_inc(stacked_a, 1)
                else:
                    h = e - 4
                    await_(act, s_done, at(gg, UNITS, 8 * (h + 1) - UNITS))
                    act.mul(q_stack[:, h, :], ps[:, 7, :], SCALE).then_inc(stacked_a, 1)

            def exps(gg, v):
                n = unit(v)[3]
                act.wait_ge(max_done, at(gg, UNITS, v + 1))
                await_(act, p_turned, at(gg, UNITS, v - 3))
                act.activation(probs[:, v % 4, 0:n], ps[:, v % 4, 0:n], ACT.Exp, bias=nmax4[:, v % 4:v % 4 + 1],
                               accum_out=rsum4[:, v % 4:v % 4 + 1]).then_inc(exp_done, 1)

            def turned_hi(gg, v):
                h, br, i, n = unit(v)
                act.wait_ge(p_turned, at(gg, UNITS, v + 1))
                if i == 0:
                    await_(act, pv_done, at(gg, 8, 2 * (h - 1) + br + 1))
                act.copy(view(slot0[0], PT_BR * br + P * i, [[PT_ROW, i + 1], [1, P]]),
                         ps[:, 4 + v % 2, 0:n].rearrange("p (j c) -> p j c", c=P)).then_inc(pt_hi, 1)

            def out_half(gg, h):
                r = HD * (h % 2)
                act.wait_ge(pv_done, at(gg, 8, 2 * h + 2))
                if h >= 2:
                    act.wait_ge(o_lo, at(gg, 4, h - 1))
                act.copy(o_buf[r:r + HD, :], ps[HD:P, 6, :]).then_inc(o_half, 1)

            def out_hi(gg, h):
                r = HD * (h % 2)
                act.wait_ge(o_sum, at(gg, 4, h + 1))
                act.copy(act_hi[r:r + HD, bass.ds(place(gg, 2, h // 2), 1), :].rearrange("p o c -> p (o c)"),
                         o_buf[r:r + HD, :]).then_inc(o_hi, 1)

            def slot(gg, k):
                if 0 <= k - L_SPLIT < UNITS:
                    turned_hi(gg, k - L_SPLIT)
                if 0 <= k - L_EXP < UNITS:
                    exps(gg, k - L_EXP)
                if k - 1 in TURNS and TURNS.index(k - 1) not in (1, 3):
                    stack(gg, TURNS.index(k - 1))
                if k == 8:
                    act.wait_ge(cs_sub, at(gg, 1, 1))
                    act.activation(c_sc, c_sc, ACT.Exp).then_inc(cs_exp, 1)
                if k == 12:
                    act.wait_ge(pc_turned, at(gg, 1, 1))
                    act.copy(pct[0], ps[:, 7, :]).then_inc(pc_hi, 1)
                if k >= 14 and (k - 14) % 8 == 0:
                    out_half(gg, (k - 14) // 8)
                if k >= 16 and (k - 16) % 8 == 0:
                    out_hi(gg, (k - 16) // 8)

            windows(act, slot, SLOT0, UNITS, 2, GROUPS)

            for j in range(4):
                split_next(B_OUT0 + 1, j, (pv_done, 8 * GROUPS))
            load_gain(1)
            norm_first(4, G_OUT0)
            for j in range(4):
                split_next(B_MLP0, j, (tok_done, G_OUT0 + 4))
            norm_tail(4, G_OUT0 + 4)
            load_gain(2)

            def relu(u, u_abs):
                act.wait_ge(up_done, u_abs + (u + 1))
                if u >= 2:
                    act.wait_ge(a_ready, u_abs + (u - 1))
                act.activation(relu_b[:, u % 2, :], ps[:, (u + 2) % 4, :], ACT.Relu).then_inc(up_free, 1)
                act.wait_ge(up_free, u_abs + (u + 1))
                act.activation(a_hi[:, u, :], relu_b[:, u % 2, :], ACT.Square).then_inc(a_hi_done, 1)

            def mlp_step(n, gr, up, last):
                for c in range(4):
                    for j in range(4):
                        if not (c == 3 and last == 16):
                            w = [(tok_done, gr), (up_done, up + 4), (up_done, up + 8), (tok_done, gr + 4)][c]
                            if j == 0:
                                act.wait_ge(*w)
                            act.wait_ge(part_landed[j], (n + (c + 1)) * 16 + 16)
                            act.copy(w_hi[:, (c + B_MLP0 + 1) % 2, 1024 * j:1024 * (j + 1)],
                                     w_raw[:, j, :]).then_inc(hi_split, 1)
                        if c < 2:
                            relu(4 * c + j, up)
                    if c == 2 and last is not None:
                        norm_first(last, gr)

            def mlp_layer(n0, g0, u0, end):
                with act.Fori(0, STEPS - 1) as it:
                    mlp_step(it * 4 + n0, it * 8 + g0, it * 8 + u0, None)
                k = STEPS - 1
                mlp_step(n0 + 4 * k, g0 + 8 * k, u0 + 8 * k, end)

            mlp_layer(B_MLP0, G_MLP0, 0, 8)
            norm_tail(8, G_DIFF - 4)

            for b in range(6):
                prev = (tok_done, G_DIFF + 4 * b)
                if b < 6:
                    for j in range(4):
                        split_next(B_DIFF + b + 1, j, prev)

            def d_stack_queries(hh, a):
                act.wait_ge(dq_turned, at(hh, 2, a + 1))
                await_(act, ds_done, at(hh, D_UNITS, 4 * (a + 1) - D_UNITS))
                act.mul(dq_stack[:, :, 2 * P * a:2 * P * (a + 1)],
                        ps[:, (7, 5)[a], :].rearrange("p (c q) -> p c q", c=2), SCALE).then_inc(dq_stacked, 1)

            def d_exps(hh, u):
                i, c, n = u // 2, u % 2, P * (u // 2 + 1)
                act.wait_ge(dmax_done, at(hh, D_UNITS, u + 1))
                await_(act, dp_turned if c else da_done, at(hh, T, i - 1))
                act.activation(probs[:, u % 4, 0:n], ps[:, u % 4, 0:n], ACT.Exp, bias=nmax4[:, u % 4:u % 4 + 1],
                               accum_out=rsum4[:, u % 4:u % 4 + 1]).then_inc(dexp_done, 1)

            def d_slot(hh, k):
                i = tile_at(k, D_SPLIT)
                if i is not None:
                    act.wait_ge(dp_turned, at(hh, T, i + 1))
                    await_(act, dpv_done, at(hh, T, i - 1))
                    n = P * (i + 1)
                    act.copy(dpt[0][:, i % 2, 0:n], ps[:, 4, 0:n]).then_inc(dpt_hi, 1)
                if 0 <= k - L_EXP < D_UNITS:
                    d_exps(hh, k - L_EXP)
                i = tile_at(k, D_SS)
                if i is not None:
                    act.wait_ge(do_free, at(hh, T, i + 1))
                    if i == 0:
                        await_(act, d_ms_done, at(hh, 1, 0))
                    cols_ = bass.ds(place(hh, P, 0), P)
                    act.activation(dk_raw[:, i, cols_], q_raw[:, i, cols_], ACT.Square,
                                   accum_out=d_ss[:, i:i + 1]).then_inc(d_ss_done, 1)
                if k - 1 in D_TURN_K[::2]:
                    e = D_TURN_K.index(k - 1)
                    act.wait_ge(dk_turned, at(hh, 4, e + 1))
                    act.copy(keys(hh, 0, e // 2), ps[:, 7, :]).then_inc(dk_stacked_a, 1)
                if k - 1 in D_TURN_Q:
                    d_stack_queries(hh, D_TURN_Q.index(k - 1))
                if k == D_OUT_SPLIT:
                    act.wait_ge(do_turned, at(hh, 1, 1))
                    act.activation(act_hi[:, bass.ds(place(hh, 1, 0), 1), :].rearrange("p o c -> p (o c)"), ps[:, 5, :],
                                   ACT.Copy, scale=subg[:, 0:1]).then_inc(do_hi, 1)

            windows(act, d_slot, D_SLOT0, D_UNITS, D_SPANS, DH)

            act.dma_start(gfin, a["final_g"].partition_broadcast(P).rearrange("p o c -> p (o c)")
                          ).then_inc(gfin_landed, 16)
            for j in range(4):
                split_next(B_OUT1 + 1, j, (dpv_done, T * DH))
            load_gain(3)
            norm_first(12, G_OUT1)
            for j in range(4):
                split_next(B_MLP1, j, (tok_done, G_OUT1 + 4))
            norm_tail(12, G_OUT1 + 4)
            mlp_layer(B_MLP1, G_MLP1, 32, 16)
            norm_tail(16, G_MLP1 + 28, last=True)

        @block.vector
        def _(dve):
            order = Order(dve, dve_order)

            def sub(out_, in0, hi):
                return dve.tensor_tensor(out_, in0, hi.bitcast(F32), ALU.subtract)

            def split_lo(n, j, slot=None):
                dve.wait_ge(hi_split, n * 4 + (j + 1))
                sl = slot_of(n) if slot is None else slot
                sub(w_lo[:, sl, 1024 * j:1024 * (j + 1)], w_raw[:, j, :],
                    w_hi[:, sl, 1024 * j:1024 * (j + 1)]).then_inc(lo_split, 1)

            def norm_y(q, t):
                if t == 0:
                    dve.wait_ge(gain_landed, 16 * (q // 4 + 1))
                dve.wait_ge(rstd_done, q + 1)
                if q >= 2:
                    dve.wait_ge(turned, 2 * (q - 1))
                for b in range(2):
                    c = slice(HALF * b, HALF * (b + 1))
                    dve.scalar_tensor_tensor(out=y_bufs[q % 2][:, c], in0=x_res[:, t, c], scalar=rstd[:, q:q + 1],
                                             in1=gain[:, c], op0=ALU.mult, op1=ALU.mult).then_inc(y_done, 1)

            def norm_lo(q, t):
                for b in range(2):
                    dve.wait_ge(act_hi_done, 2 * q + b + 1)
                    at_ = (slice(None), slice(4 * b, 4 * b + 4), slice(P * t, P * (t + 1)))
                    sub(act_lo[at_], ps[:, 4 + 2 * (q % 2) + b, :].rearrange("p (k c) -> p k c", c=P), act_hi[at_]
                        ).then_inc(act_ready, 1)

            dve.wait_ge(cst_landed, 32)
            dve.tensor_copy(ident_b[:, :], ident).then_inc(small_lo, 1)
            dve.tensor_copy(mask_b[:, :], tab(C_MASK, P)).then_inc(small_lo, 1)
            dve.tensor_scalar(subg[:, :], vec[:, V_SUB:V_SUB + 1], 1.0 - LAMBDA_INIT, None, ALU.mult)
            dve.wait_ge(small_hi, 2)
            sub(tail_r[:, 1, :], tail_raw, tail_r[:, 0, :]).then_inc(small_lo, 1)
            sub(w2_r[:, 1, :], w2_raw, w2_r[:, 0, :]).then_inc(small_lo, 1)
            lv = lamv_in[:, :].rearrange("p (v u c) -> p v u c", v=2, u=2)
            order.after(dve.tensor_tensor(rtmp[:, 0:128].rearrange("p (v c) -> p v c", v=2), lv[:, :, 0, :],
                                          lv[:, :, 1, :], ALU.mult))
            dve.tensor_reduce(lam_s[:, 0:2], rtmp[:, 0:128].rearrange("p (v c) -> p v c", v=2), X,
                              ALU.add).then_inc(lam_arg, 1)
            for t in range(T):
                norm_y(t, t)
                if t:
                    norm_lo(t - 1, t - 1)
                split_lo(0, t)
            norm_lo(T - 1, T - 1)

            dve.wait_ge(act_ready, 8)
            order.after(dve.memset(x_cmp.rearrange("p j (g n) -> p j g n", g=GROUPS)[:, :, :, NC - 1:NC], 0.0))
            for m in range(4):
                v, bank = m // 2, (G_CMP + m) % 4
                if m == 2:
                    dve.wait_ge(xc_hi_done, 1)
                    sub(xc_lo[0], x_cmp, xc_hi[0]).then_inc(xc_ready, 1)
                    dve.wait_ge(xc_ready, 1)
                if m < 2:
                    split_lo(1, m)
                dve.wait_ge(tok_done, G_CMP + m + 1)
                for gl in range(2):
                    r, g = HD * gl, 2 * (m % 2) + gl
                    src = ps[r:r + HD, bank, :].rearrange("p (n b) -> p b n", b=16)
                    for par in range(2):
                        for jh in range(2):
                            pos = vec[r:r + HD, V_POS + 32 * v + 16 * par + 8 * jh:V_POS + 32 * v + 16 * par + 8 * jh + 8]
                            ins = dve.tensor_tensor(
                                x_cmp[HD * par:HD * (par + 1), 8 * jh:8 * jh + 8, NC * g:NC * g + NC - 1],
                                src[:, par::2, jh:jh + NC - 1],
                                pos.unsqueeze(2).broadcast_to([HD, 8, NC - 1]), ALU.add)
                ins.then_inc(tok_free, 1)
            split_lo(1, 2)
            split_lo(1, 3)
            dve.wait_ge(xc_hi_done, 2)
            sub(xc_lo[1], x_cmp, xc_hi[1]).then_inc(xc_ready, 1)
            for j in range(4):
                split_lo(2, j)

            def gelu(v):
                gr = G_W1K + v
                dve.wait_ge(tok_done, gr + 1)
                dve.tensor_copy(g_h, ps[:, gr % 4, 0:256]).then_inc(tok_free, 1)
                dve.wait_ge(tok_free, gr + 1)
                order.after(dve.tensor_tensor(g_a, g_h, g_h, ALU.mult))
                order.after(dve.tensor_scalar(g_a, g_a, 0.044715, 1.0, ALU.mult, ALU.add))
                dve.tensor_tensor(g_a, g_a, g_h, ALU.mult).then_inc(gelu_arg, 1)
                dve.wait_ge(gelu_tanh, v + 1)
                order.after(dve.scalar_tensor_tensor(out=g_b, in0=g_a, scalar=1.0, in1=g_h, op0=ALU.add, op1=ALU.mult))
                dve.tensor_scalar(g_a, g_b, 0.5, None, ALU.mult).then_inc(hid_done, 1)
                dve.wait_ge(hid_hi, v + 1)
                sub(hid_t[:, 1, :], ps[:, 4, 0:256], hid_t[:, 0, :]).then_inc(hid_lo, 1)

            def rope_small(dst, src, cos, sin, tmp):
                h = ROT // 2
                dve.tensor_tensor(tmp[..., 0:h], src[..., h:ROT], sin[..., 0:h], ALU.mult)
                dve.tensor_tensor(dst, src[..., 0:ROT], cos, ALU.mult)
                order.after(dve.tensor_tensor(tmp[..., h:ROT], src[..., 0:h], sin[..., h:ROT], ALU.mult))
                return dve.tensor_tensor(dst, dst, tmp, ALU.add)

            def rope_out(dst, src, t, u):
                n, h = src.shape[1], ROT // 2
                cos = tab(C_COS + ROT * t, ROT).unsqueeze(1).broadcast_to([P, n, ROT])
                sin = tab(C_SIN + ROT * t, ROT).unsqueeze(1).broadcast_to([P, n, ROT])
                tmp = rtmp[:, 128 * u:128 * u + ROT * n].rearrange("p (n r) -> p n r", r=ROT)
                dve.tensor_tensor(tmp[:, :, 0:h], src[:, :, h:ROT], sin[:, :, 0:h], ALU.mult)
                dve.tensor_tensor(tmp[:, :, h:ROT], src[:, :, 0:h], sin[:, :, h:ROT], ALU.mult)
                dve.tensor_tensor(dst[:, :, 0:ROT], src[:, :, 0:ROT], cos, ALU.mult)
                ins = dve.tensor_copy(dst[:, :, ROT:], src[:, :, ROT:])
                return ins, lambda: dve.tensor_tensor(dst[:, :, 0:ROT], dst[:, :, 0:ROT], tmp, ALU.add)

            def kv_evac(n, gr, br, t):
                bank = gr % 4
                dve.wait_ge(tok_done, gr + 1)
                ins, last = rope_out(k_raw[:, br, t, :].rearrange("p (g d) -> p g d", d=HD),
                                     ps[:, bank, 0:256].rearrange("p (g d) -> p g d", d=HD), t, t % 2)
                vp = ps[:, bank, 256:512].rearrange("p (g c) -> p g c", g=GROUPS)
                order.after(dve.tensor_copy(v_all[:, t, br, :, 0:HD], vp))
                last().then_inc(roped, 1)
                sub(v_all[:, t, br, :, HD:P], vp, v_all[:, t, br, :, 0:HD]).then_inc(tok_free, 1)

            gelu(0)
            for j in range(4):
                split_lo(B_SLC, j)
            dve.wait_ge(cmp_done, 1)
            order.after(dve.tensor_copy(kc_f, ps[:, 5, 0:HD]))
            order.after(dve.tensor_copy(kc_r[:, ROT:], kc_f[:, ROT:]))
            rope_small(kc_r[:, 0:ROT], kc_f, tab(C_CCOS, ROT), tab(C_CSIN, ROT), rtmp[:, 0:ROT]).then_inc(kc_roped, 1)
            dve.wait_ge(kc_hi, 2)
            sub(kc[0:HD, 1, :], ps[0:HD, 6, 0:P], kc[0:HD, 0, :])
            sub(kc[HD:P, 1, :], ps[0:HD, 6, 0:P], kc[0:HD, 0, :]).then_inc(cmp_ready, 1)
            gelu(1)
            for t in range(T):
                split_lo(B_WIN, t)
                kv_evac(B_SLC, G_SLC + t, 0, t)
            dve.wait_ge(cmp_done, 2)
            order.after(dve.tensor_copy(vc[:, 0:HD], ps[:, 5, 0:HD]))
            order.after(sub(vc[:, HD:P], ps[:, 5, 0:HD], vc[:, 0:HD]))
            for g in range(GROUPS):
                for h in range(HPG):
                    ins = dve.tensor_copy(vc_rep[NC * h:NC * (h + 1), g, :], vc[NC * g:NC * (g + 1), :].bitcast(F32))
            ins.then_inc(cmp_ready, 1)
            for t in range(T):
                split_lo(B_Q0, t)
                kv_evac(B_WIN, G_WIN + t, 1, t)
            for b in range(2):
                for t in range(T):
                    split_lo(B_Q1 + b, t)
                    dve.wait_ge(tok_done, G_Q + 4 * b + t + 1)
                    ins, last = rope_out(q_raw[:, t, NB * b:NB * (b + 1)].rearrange("p (h d) -> p h d", d=HD),
                                         ps[:, (G_Q + 4 * b + t) % 4, :].rearrange("p (h d) -> p h d", d=HD), t, t % 2)
                    ins.then_inc(tok_free, 1)
                    dve.wait_ge(tok_free, G_Q + 4 * b + t + 1)
                    last().then_inc(roped, 1)
            for t in range(T):
                dve.wait_ge(tok_done, G_GATE + t + 1)
                dve.tensor_copy(gate[:, t, :], ps[:, (G_GATE + t) % 4, 0:48]).then_inc(tok_free, 1)
            dve.wait_ge(gate_tanh, 1)
            order.after(dve.tensor_scalar(gate[:, :, :], gate[:, :, :], 0.5, 0.5, ALU.mult, ALU.add))
            g0 = gate[:, :, :].rearrange("p t (h b) -> p t h b", b=3)[:, :, :, 0]
            dve.tensor_tensor(g0, g0, tab(C_CMUL, T).unsqueeze(2).broadcast_to([P, T, 16]),
                              ALU.mult).then_inc(gates_ready, 1)
            dve.wait_ge(lam_exp, 1)
            order.after(dve.tensor_tensor(lam2[:, 1:2], lam_s[:, 3:4], lam_s[:, 2:3], ALU.subtract))
            order.after(dve.tensor_scalar(lam2[:, 1:2], lam2[:, 1:2], -LAMBDA_INIT, None, ALU.add))
            order.after(dve.memset(lam2[:, 0:1], 1.0))

            cos4 = tab(C_COS, 64, T)
            sin4 = tab(C_SIN, 64, T)

            def stack(gg, e):
                dve.wait_ge(st_turned, at(gg, 8, e + 1))
                dve.tensor_copy(keys(gg, 1, e // 2), ps[:, 7, :]).then_inc(stacked_v, 1)

            def maxes(gg, v):
                dve.wait_ge(s_done, at(gg, UNITS, v + 1))
                dve.tensor_reduce(nmax4[:, v % 4:v % 4 + 1], ps[:, v % 4, 0:unit(v)[3]], X, ALU.max, negate=True
                                  ).then_inc(max_done, 1)

            def inverse(gg, v):
                dve.wait_ge(exp_done, at(gg, UNITS, v + 1))
                dve.reciprocal(rinv4[:, v % 4:v % 4 + 1], rsum4[:, v % 4:v % 4 + 1]).then_inc(rinv_done, 1)

            def turned_lo(gg, v):
                h, br, i, n = unit(v)
                dve.wait_ge(pt_hi, at(gg, UNITS, v + 1))
                o, dims = PT_BR * br + P * i, [[PT_ROW, i + 1], [1, P]]
                sub(view(slot0[1], o, dims), ps[:, 4 + v % 2, 0:n].rearrange("p (j c) -> p j c", c=P),
                    view(slot0[0], o, dims)).then_inc(pt_lo, 1)

            def out_sum(gg, h):
                r = HD * (h % 2)
                dve.wait_ge(o_half, at(gg, 4, h + 1))
                dve.tensor_tensor(o_buf[r:r + HD, :], ps[0:HD, 6, :], o_buf[r:r + HD, :], ALU.add).then_inc(o_sum, 1)

            def out_lo(gg, h):
                r = HD * (h % 2)
                dve.wait_ge(o_hi, at(gg, 4, h + 1))
                pair = bass.ds(place(gg, 2, h // 2), 1)
                sub(act_lo[r:r + HD, pair, :].rearrange("p o c -> p (o c)"), o_buf[r:r + HD, :],
                    act_hi[r:r + HD, pair, :].rearrange("p o c -> p (o c)")).then_inc(o_lo, 1)

            e4 = c_sc.rearrange("p (i h n) -> p i h n", i=T, h=HPG)
            er = c_sc.rearrange("p (r n) -> p r n", n=NC)

            def slot(gg, k):
                if k == 6:
                    dve.wait_ge(cs_done, at(gg, 1, 1))
                    dve.tensor_tensor(e4, ps[:, 7, :].rearrange("p (i h n) -> p i h n", i=T, h=HPG),
                                      tab(C_CADD, 128, T).unsqueeze(2).broadcast_to([P, T, HPG, NC]), ALU.add
                                      ).then_inc(cs_masked, 1)
                if k == 7:
                    dve.wait_ge(cs_masked, at(gg, 1, 1))
                    dve.tensor_reduce(c_st[:, 0, :], er, X, ALU.max).then_inc(cs_max, 1)
                if k == 9:
                    dve.wait_ge(cs_exp, at(gg, 1, 1))
                    dve.tensor_reduce(c_st[:, 1, :], er, X, ALU.add).then_inc(cs_sum, 1)
                if k == 10:
                    dve.wait_ge(cs_inv, at(gg, 1, 1))
                    gc = gate[:, :, bass.ds(place(gg, 12, 0), 12)].rearrange("p t (h b) -> p t h b", b=3)[:, :, :, 0]
                    dve.tensor_tensor(c_st[:, 3, :].rearrange("p (t h) -> p t h", t=T),
                                      c_st[:, 2, :].rearrange("p (t h) -> p t h", t=T), gc, ALU.mult).then_inc(cs_coef, 1)
                if 0 <= k - L_NORM < UNITS:
                    inverse(gg, k - L_NORM)
                if 0 <= k - L_MAX < UNITS:
                    maxes(gg, k - L_MAX)
                if 0 <= k - L_SPLIT < UNITS:
                    turned_lo(gg, k - L_SPLIT)
                if k == 7:
                    dve.wait_ge(cs_max, at(gg, 1, 1))
                    dve.tensor_tensor(er, er, c_st[:, 0, :].unsqueeze(2).broadcast_to([P, 16, NC]),
                                      ALU.subtract).then_inc(cs_sub, 1)
                if k == 9:
                    dve.wait_ge(cs_sum, at(gg, 1, 1))
                    dve.reciprocal(c_st[:, 2, :], c_st[:, 1, :]).then_inc(cs_inv, 1)
                if k - 1 in TURNS and TURNS.index(k - 1) in (1, 3):
                    stack(gg, TURNS.index(k - 1))
                if k == 12:
                    dve.wait_ge(pc_hi, at(gg, 1, 1))
                    sub(pct[1], ps[:, 7, :], pct[0]).then_inc(pc_lo, 1)
                if k >= 15 and (k - 15) % 8 == 0:
                    out_sum(gg, (k - 15) // 8)
                if k >= 17 and (k - 17) % 8 == 0:
                    out_lo(gg, (k - 17) // 8)

            windows(dve, slot, SLOT0, UNITS, 2, GROUPS)

            def residual(gr, bank, t, dh):
                dve.wait_ge(tok_done, gr + 1)
                xs = x_res[:, t, NB * dh:NB * (dh + 1)]
                dve.tensor_tensor(xs, ps[:, bank, :], xs, ALU.add).then_inc(tok_free, 1)

            def norm_tail(q0, step):
                for t in range(T):
                    step(t)
                    if t:
                        norm_lo(q0 + t - 1, t - 1)
                    norm_y(q0 + t, t)
                norm_lo(q0 + T - 1, T - 1)

            def out_layer(b0, g0, q0):
                for t in range(T):
                    split_lo(b0 + 1, t)
                    residual(g0 + t, (g0 + t) % 4, t, 0)
                for t in range(T):
                    split_lo(b0 + 2, t)
                norm_tail(q0, lambda t: residual(g0 + 4 + t, (g0 + 4 + t) % 4, t, 1))

            out_layer(B_OUT0, G_OUT0, 4)

            def final_norm(step):
                dve.wait_ge(gfin_landed, 16)
                for t in range(T):
                    step(t)
                    dve.wait_ge(rstd_done, 16 + t + 1)
                    if t >= 2:
                        dve.wait_ge(stored[t % 2], 32)
                    for b in range(2):
                        c = slice(HALF * b, HALF * (b + 1))
                        dve.scalar_tensor_tensor(out=fin[:, t % 2, c], in0=x_res[:, t, c], scalar=rstd[:, 16 + t:17 + t],
                                                 in1=gfin[:, c], op0=ALU.mult, op1=ALU.mult).then_inc(fin_done, 1)

            def mlp_step(n, gr, up, last):
                for c in range(4):
                    if c == 3 and last is not None:
                        if last < 16:
                            for j in range(4):
                                split_lo(n + 4, j, B_MLP0 % 2)
                            norm_tail(last, lambda t: residual(gr + 4 + t, (G_MLP0 + 4 + t) % 4, t, 1))
                        else:
                            final_norm(lambda t: residual(gr + 4 + t, (G_MLP0 + 4 + t) % 4, t, 1))
                        continue
                    for j in range(4):
                        split_lo(n + (c + 1), j, (B_MLP0 + c + 1) % 2)
                        if c < 2:
                            u = 4 * c + j
                            dve.wait_ge(up_free, up + (u + 1))
                            if u >= 2:
                                dve.wait_ge(a_ready, up + (u - 1))
                            dve.tensor_tensor(sq_b[:, u % 2, :], relu_b[:, u % 2, :], relu_b[:, u % 2, :],
                                              ALU.mult).then_inc(sq_done, 1)
                            dve.wait_ge(sq_done, up + (u + 1))
                            dve.wait_ge(a_hi_done, up + (u + 1))
                            sub(a_lo[:, u, :], sq_b[:, u % 2, :], a_hi[:, u, :]).then_inc(a_ready, 1)
                        else:
                            d = 4 * (c - 2) + j
                            residual(gr + d, (G_MLP0 + d) % 4, j, c - 2)

            def mlp_layer(n0, g0, u0, end):
                with dve.Fori(0, STEPS - 1) as it:
                    mlp_step(it * 4 + n0, it * 8 + g0, it * 8 + u0, None)
                k = STEPS - 1
                mlp_step(n0 + 4 * k, g0 + 8 * k, u0 + 8 * k, end)

            mlp_layer(B_MLP0, G_MLP0, 0, 8)

            for b in range(6):
                for t in range(T):
                    split_lo(B_DIFF + b + 1, t)
                    gr = G_DIFF + 4 * b + t
                    dve.wait_ge(tok_done, gr + 1)
                    src = ps[:, gr % 4, :]
                    if b < 4:
                        raw = q_raw if b < 2 else dk_raw
                        ins, last = rope_out(raw[:, t, NB * (b % 2):NB * (b % 2 + 1)].rearrange("p (h d) -> p h d", d=HD),
                                             src.rearrange("p (h d) -> p h d", d=HD), t, t % 2)
                        ins.then_inc(tok_free, 1)
                        dve.wait_ge(tok_free, gr + 1)
                        last().then_inc(d_roped, 1)
                    else:
                        v = dv_all[:, t, 4 * (b - 4):4 * (b - 3), :]
                        vp = src.rearrange("p (h c) -> p h c", h=4)
                        order.after(dve.tensor_copy(v[:, :, 0:P], vp))
                        sub(v[:, :, P:2 * P], vp, v[:, :, 0:P]).then_inc(tok_free, 1)

            def d_slot(hh, k):
                if 0 <= k - L_NORM < D_UNITS:
                    u = k - L_NORM
                    dve.wait_ge(dexp_done, at(hh, D_UNITS, u + 1))
                    await_(dve, da_done, at(hh, T, u // 2 - 1))
                    dve.reciprocal(rinv4[:, u % 4:u % 4 + 1], rsum4[:, u % 4:u % 4 + 1]).then_inc(drinv_done, 1)
                if 0 <= k - L_MAX < D_UNITS:
                    u = k - L_MAX
                    dve.wait_ge(ds_done, at(hh, D_UNITS, u + 1))
                    dve.tensor_reduce(nmax4[:, u % 4:u % 4 + 1], ps[:, u % 4, 0:P * (u // 2 + 1)], X, ALU.max, negate=True
                                      ).then_inc(dmax_done, 1)
                i = tile_at(k, D_A)
                if i is not None:
                    n, u = P * (i + 1), 2 * i % 4
                    dve.wait_ge(dp1_done, at(hh, T, i + 1))
                    dve.wait_ge(drinv_done, at(hh, D_UNITS, 2 * i + 1))
                    dve.scalar_tensor_tensor(out=probs[:, u + 1, 0:n], in0=probs[:, u, 0:n], scalar=rinv4[:, u:u + 1],
                                             in1=probs[:, u + 1, 0:n], op0=ALU.mult, op1=ALU.add).then_inc(da_done, 1)
                i = tile_at(k, D_SPLIT)
                if i is not None:
                    n = P * (i + 1)
                    dve.wait_ge(dpt_hi, at(hh, T, i + 1))
                    sub(dpt[1][:, i % 2, 0:n], ps[:, 4, 0:n], dpt[0][:, i % 2, 0:n]).then_inc(dpt_lo, 1)
                i = tile_at(k, D_OUT)
                if i is not None:
                    dve.wait_ge(dpv_done, at(hh, T, i + 1))
                    dve.tensor_reduce(q_raw[:, i, bass.ds(place(hh, P, 0), P)],
                                      ps[:, 6, 0:256].rearrange("p (z c) -> p c z", z=2), X,
                                      ALU.add).then_inc(do_free, 1)
                if k - 1 in D_TURN_K[1::2]:
                    e = D_TURN_K.index(k - 1)
                    dve.wait_ge(dk_turned, at(hh, 4, e + 1))
                    dve.tensor_copy(keys(hh, 1, e // 2), ps[:, 5, :]).then_inc(dk_stacked_v, 1)
                if k == D_MS:
                    dve.wait_ge(d_ss_done, at(hh, T, T))
                    dve.tensor_scalar(d_ms, d_ss, 1.0 / P, EPS, ALU.mult, ALU.add).then_inc(d_ms_done, 1)
                if k == D_Y:
                    dve.wait_ge(d_rs_done, at(hh, 1, 1))
                    dve.tensor_tensor(o_buf[:, :].rearrange("p (t c) -> p t c", t=T), q_raw[:, :, bass.ds(place(hh, P, 0), P)],
                                      d_rs.unsqueeze(2).broadcast_to([P, T, P]), ALU.mult).then_inc(dy_done, 1)
                if k == D_OUT_SPLIT:
                    dve.wait_ge(do_hi, at(hh, 1, 1))
                    feat = bass.ds(place(hh, 1, 0), 1)
                    dve.scalar_tensor_tensor(out=act_lo[:, feat, :].rearrange("p o c -> p (o c)"), in0=ps[:, 5, :],
                                             scalar=subg[:, 0:1],
                                             in1=act_hi[:, feat, :].rearrange("p o c -> p (o c)").bitcast(F32),
                                             op0=ALU.mult, op1=ALU.subtract).then_inc(do_lo, 1)

            windows(dve, d_slot, D_SLOT0, D_UNITS, D_SPANS, DH)

            out_layer(B_OUT1, G_OUT1, 12)
            mlp_layer(B_MLP1, G_MLP1, 32, 16)

        @block.tensor
        def _(pe):
            def mm(o, l, r, start, stop):
                return pe.matmul(o, l, r, start=start, stop=stop)

            def product(o, pairs, start=True, stop=True):
                for i, (l, r) in enumerate(pairs):
                    ins = mm(o, l, r, start and i == 0, stop and i == len(pairs) - 1)
                return ins

            def whole(n, sl=None):
                pe.wait_ge(lo_split, n * 4 + 4)

            def norm_turn(q):
                for b in range(2):
                    pe.wait_ge(y_done, 2 * q + b + 1)
                    if q >= 2:
                        pe.wait_ge(act_ready, 2 * (q - 2) + b + 1)
                    for k in range(4):
                        c = HALF * b + P * k
                        ins = pe.transpose(ps[:, 4 + 2 * (q % 2) + b, P * k:P * (k + 1)], y_bufs[q % 2][:, c:c + P], ident)
                    ins.then_inc(turned, 1)

            def token_group(gr, bank, sl, t, n=NB, w=None):
                wh = (lambda k: w_hi[:, sl, NB * k:NB * (k + 1)]) if w is None else (lambda k: w[:, 0, n * k:n * (k + 1)])
                wl = (lambda k: w_lo[:, sl, NB * k:NB * (k + 1)]) if w is None else (lambda k: w[:, 1, n * k:n * (k + 1)])
                pairs = []
                for k in range(KT):
                    xh, xl = act_hi[:, k, P * t:P * (t + 1)], act_lo[:, k, P * t:P * (t + 1)]
                    pairs += [(xh, wh(k)), (xh, wl(k)), (xl, wh(k))]
                product(ps[:, bank, 0:n], pairs).then_inc(tok_done, 1)

            def feature_group(bank, sl, m):
                pairs = []
                for k in range(KT):
                    c = NB * k + P * m
                    wh, wl = w_hi[:, sl, c:c + P], w_lo[:, sl, c:c + P]
                    pairs += [(wh, act_hi[:, k, :]), (wh, act_lo[:, k, :]), (wl, act_hi[:, k, :])]
                return product(ps[:, bank, :], pairs)

            pe.wait_ge(cst_landed, 32)
            pe.wait_ge(small_lo, 4)
            for t in range(T):
                norm_turn(t)
            pe.wait_ge(act_ready, 8)
            whole(0)
            for m in range(4):
                feature_group(G_CMP + m, 0, m).then_inc(tok_done, 1)

            def hidden(n, v):
                whole(n)
                gr = G_W1K + v
                pe.wait_ge(xc_ready, v + 1)
                pe.wait_ge(tok_free, gr - 3)
                pairs = []
                for j in range(16):
                    wh, wl = (w[:, n % 2, 256 * j:256 * (j + 1)] for w in (w_hi, w_lo))
                    pairs += [(xc_hi[v][:, j, :], wh), (xc_hi[v][:, j, :], wl), (xc_lo[v][:, j, :], wh)]
                product(ps[:, gr % 4, 0:256], pairs).then_inc(tok_done, 1)

            def second(v):
                pe.wait_ge(hid_done, v + 1)
                for c in range(2):
                    ins = pe.transpose(ps[:, 4, P * c:P * (c + 1)], g_a[:, P * c:P * (c + 1)], ident)
                ins.then_inc(hid_turned, 1)
                pe.wait_ge(hid_lo, v + 1)
                pairs = []
                for c in range(2):
                    h, l = hid_t[:, 0, P * c:P * (c + 1)], hid_t[:, 1, P * c:P * (c + 1)]
                    wh, wl = (w2_r[:, z, P * v + HD * c:P * v + HD * (c + 1)] for z in range(2))
                    pairs += [(h, wh), (h, wl), (l, wh)]
                product(ps[:, 5, 0:HD], pairs).then_inc(cmp_done, 1)

            def token_block(n, g0, norm=None, q0=None):
                whole(n)
                for t in range(T):
                    if norm is not None:
                        pe.wait_ge(act_ready, 2 * (4 * norm + t + 1))
                    pe.wait_ge(tok_free, g0 + t - 3)
                    token_group(g0 + t, (g0 + t) % 4, n % 2, t)
                    if q0 is not None and t:
                        norm_turn(q0 + t - 1)
                if q0 is not None:
                    norm_turn(q0 + T - 1)

            hidden(B_W1K, 0)
            hidden(B_W1V, 1)
            second(0)
            pe.wait_ge(kc_roped, 1)
            pe.transpose(ps[0:HD, 6, 0:P], kc_r, ident).then_inc(kc_turned, 1)
            second(1)
            token_block(B_SLC, G_SLC)
            token_block(B_WIN, G_WIN)
            token_block(B_Q0, G_Q)
            token_block(B_Q1, G_Q + 4)
            for t in range(T):
                pe.wait_ge(tok_free, G_GATE + t - 3)
                token_group(G_GATE + t, (G_GATE + t) % 4, 0, t, 48, tail_r)

            pe.wait_ge(cmp_ready, 2)
            pe.wait_ge(tok_free, G_GATE + T)

            def turn_stack(gg, e):
                pe.wait_ge(stage_filled, at(gg, 8, e + 1))
                if e == 0:
                    await_(pe, pc_lo, at(gg, 1, 0))
                elif e in (2, 4):
                    pe.wait_ge(stacked_v, at(gg, 2, e // 2))
                else:
                    pe.wait_ge(stacked_a, at(gg, 6, 1 + e // 2 if e < 4 else e - 2))
                for t in range(T):
                    ins = pe.transpose(ps[:, 7, P * t:P * (t + 1)], stage[:, e % 2, t, :], ident)
                ins.then_inc(st_turned, 1)

            def scores(gg, v):
                h, br, i, n = unit(v)
                await_(pe, exp_done, at(gg, UNITS, v - 3))
                if v == 0:
                    pe.wait_ge(stacked_v, at(gg, 2, 2))
                if v % 8 == 0:
                    pe.wait_ge(stacked_a, at(gg, 6, 3 + h))
                q = q_stack[:, h, P * i:P * (i + 1)]
                o = ps[:, v % 4, 0:n]
                product(o, [(q, keys(gg, z, br, n)) for z in range(2)], stop=False)
                mm(o[:, n - P:n], ident_b[:, :], mask_b[:, :], False, True).then_inc(s_done, 1)

            def block_scores(gg, h):
                if h == 0:
                    pe.wait_ge(stacked_a, at(gg, 6, 6))
                for i in range(T):
                    q = q_stack[:, h, P * i:P * (i + 1)]
                    c0 = P * i + NC * h
                    ins = product(ps[:, 7, c0:c0 + NC],
                                  [(q, kc[:, z, bass.ds(place(gg, NC, 0), NC)]) for z in range(2)])
                if h == HPG - 1:
                    ins.then_inc(cs_done, 1)

            def turn(gg, v):
                pe.wait_ge(normed, at(gg, UNITS, v + 1))
                await_(pe, pt_lo, at(gg, UNITS, v - 1))
                for j in range(v % 4 + 1):
                    ins = pe.transpose(ps[:, 4 + v % 2, P * j:P * (j + 1)], probs[:, v % 4, P * j:P * (j + 1)], ident)
                ins.then_inc(p_turned, 1)

            def values(gg, h, br):
                pe.wait_ge(pt_lo, at(gg, UNITS, 8 * h + 4 * br + 4))
                if br == 0:
                    await_(pe, o_sum, at(gg, 4, h))
                if h == 0:
                    pe.wait_ge(v_staged, at(gg, 3, 1 + 2 * br))
                if br == 1:
                    if h == 0:
                        pe.wait_ge(pc_lo, at(gg, 1, 1))
                    r = NC * h
                    for z in range(2):
                        mm(ps[:, 6, :], vc_st[r:r + NC, :], pct[z][r:r + NC, :], False, False)
                for j in range(T):
                    for z in range(2):
                        o0 = PT_BR * br + (PT_ROW + P) * j
                        ins = mm(ps[:, 6, P * j:S], v_st[:, j, br, :], slot0[z][:, o0:o0 + S - P * j],
                                 br == 0 and j == 0 and z == 0, br == 1 and j == T - 1 and z == 1)
                ins.then_inc(pv_done, 1)

            def slot(gg, k):
                if 0 <= k < UNITS:
                    scores(gg, k)
                if 0 <= k - L_TURN < UNITS:
                    turn(gg, k - L_TURN)
                v = k - L_PV
                if 0 <= v < UNITS and v % 4 == 3:
                    values(gg, v // 8, v // 4 % 2)
                if k in TURNS:
                    turn_stack(gg, TURNS.index(k))
                if 2 <= k < 6:
                    block_scores(gg, k - 2)
                if k == 11:
                    pe.wait_ge(pc_ready, at(gg, 1, 1))
                    for i in range(T):
                        ins = pe.transpose(ps[:, 7, P * i:P * (i + 1)], c_sc[:, P * i:P * (i + 1)], ident)
                    ins.then_inc(pc_turned, 1)

            windows(pe, slot, SLOT0, UNITS, 2, GROUPS)

            pe.wait_ge(o_lo, 4 * GROUPS)
            token_block(B_OUT0, G_OUT0)
            token_block(B_OUT0 + 1, G_OUT0 + 4, q0=4)
            pe.wait_ge(act_ready, 16)

            def mlp_step(n, gr, up, q0=None):
                for c in range(4):
                    sl = (B_MLP0 + c) % 2
                    whole(n + c)
                    for j in range(4):
                        if c < 2:
                            u = 4 * c + j
                            if u < 4:
                                pe.wait_ge(tok_free, gr + (u - 3))
                            else:
                                pe.wait_ge(up_free, up + (u - 3))
                            feature_group((u + 2) % 4, sl, j).then_inc(up_done, 1)
                            continue
                        d = 4 * (c - 2) + j
                        if d >= 4:
                            pe.wait_ge(tok_free, gr + (d - 3))
                        bank = (G_MLP0 + d) % 4
                        pairs = []
                        if d < 4:
                            pe.wait_ge(up_free, up + (d + 5))
                        for k in range(KT):
                            if d == 0:
                                pe.wait_ge(a_ready, up + (k + 1))
                            ah, al = a_hi[:, k, P * j:P * (j + 1)], a_lo[:, k, P * j:P * (j + 1)]
                            wh, wl = (w[:, sl, NB * k:NB * (k + 1)] for w in (w_hi, w_lo))
                            ins = product(ps[:, bank, :], [(ah, wh), (ah, wl), (al, wh)], k == 0, k == KT - 1)
                        ins.then_inc(tok_done, 1)
                        if q0 is not None and d >= 5:
                            norm_turn(q0 + d - 5)
                if q0 is not None:
                    norm_turn(q0 + T - 1)

            def mlp_layer(n0, g0, u0, q0):
                with pe.Fori(0, STEPS - 1) as it:
                    mlp_step(it * 4 + n0, it * 8 + g0, it * 8 + u0)
                k = STEPS - 1
                mlp_step(n0 + 4 * k, g0 + 8 * k, u0 + 8 * k, q0)

            mlp_layer(B_MLP0, G_MLP0, 0, 8)
            for b in range(6):
                token_block(B_DIFF + b, G_DIFF + 4 * b, 2)

            pe.wait_ge(tok_free, G_OUT1)

            def d_turn_keys(hh, e):
                pe.wait_ge(dk_filled, at(hh, 4, e + 1))
                if e < 2:
                    await_(pe, dq_stacked, at(hh, 2, e - 1))
                else:
                    pe.wait_ge((dk_stacked_a, dk_stacked_v)[e % 2], at(hh, 2, 1))
                for t in range(T):
                    ins = pe.transpose(ps[:, (7, 5)[e % 2], P * t:P * (t + 1)],
                                       dk_stage[:, e // 2, e % 2, t, :].bitcast(F32), ident)
                ins.then_inc(dk_turned, 1)

            def d_turn_queries(hh, a):
                pe.wait_ge(dq_filled, at(hh, 2, a + 1))
                if a == 0:
                    pe.wait_ge(dk_stacked_a, at(hh, 2, 2))
                else:
                    pe.wait_ge(dk_stacked_v, at(hh, 2, 2))
                    await_(pe, dmax_done, at(hh, D_UNITS, 6 - D_UNITS))
                for c in range(2):
                    for t in range(2):
                        o = P * (2 * c + t)
                        ins = pe.transpose(ps[:, (7, 5)[a], o:o + P], dq_stage[:, a, t, c, :].bitcast(F32), ident)
                ins.then_inc(dq_turned, 1)

            def d_scores(hh, u):
                i, c, n = u // 2, u % 2, P * (u // 2 + 1)
                await_(pe, dexp_done, at(hh, D_UNITS, u - 3))
                if u == 0:
                    pe.wait_ge(dk_stacked_v, at(hh, 2, 2))
                if u % 4 == 0:
                    pe.wait_ge(dq_stacked, at(hh, 2, u // 4 + 1))
                o = ps[:, u % 4, 0:n]
                product(o, [(dq_stack[:, c, P * i:P * (i + 1)], keys(hh, z, c, n)) for z in range(2)], stop=False)
                mm(o[:, n - P:n], ident_b[:, :], mask_b[:, :], False, True).then_inc(ds_done, 1)

            def d_slot(hh, k):
                if 0 <= k < D_UNITS:
                    d_scores(hh, k)
                i = tile_at(k, D_TURN)
                if i is not None:
                    pe.wait_ge(da_done, at(hh, T, i + 1))
                    await_(pe, dpt_lo, at(hh, T, i))
                    for j in range(i + 1):
                        ins = pe.transpose(ps[:, 4, P * j:P * (j + 1)], probs[:, (2 * i + 1) % 4, P * j:P * (j + 1)], ident)
                    ins.then_inc(dp_turned, 1)
                i = tile_at(k, D_PV)
                if i is not None:
                    pe.wait_ge(dpt_lo, at(hh, T, i + 1))
                    await_(pe, do_free, at(hh, T, i))
                    pairs = [(dpt[z][:, i % 2, P * j:P * (j + 1)],
                              dv_all[:, j, bass.ds(place(hh, 1, 0), 1), :].rearrange("p o c -> p (o c)"))
                             for j in range(i + 1) for z in range(2)]
                    product(ps[:, 6, 0:256], pairs).then_inc(dpv_done, 1)
                if k in D_TURN_K:
                    d_turn_keys(hh, D_TURN_K.index(k))
                if k in D_TURN_Q:
                    d_turn_queries(hh, D_TURN_Q.index(k))
                if k == D_OUT_TURN:
                    pe.wait_ge(dy_done, at(hh, 1, 1))
                    if not isinstance(hh[0], int) or sum(hh) + 3 < DH:
                        pe.wait_ge(dk_stacked_v, at(hh, 2, 8))
                    else:
                        pe.wait_ge(dq_stacked, 2 * DH)
                        pe.wait_ge(do_lo, sum(hh))
                    for t in range(T):
                        ins = pe.transpose(ps[:, 5, P * t:P * (t + 1)], o_buf[:, P * t:P * (t + 1)], ident)
                    ins.then_inc(do_turned, 1)

            windows(pe, d_slot, D_SLOT0, D_UNITS, D_SPANS, DH)

            pe.wait_ge(do_lo, DH)
            token_block(B_OUT1, G_OUT1)
            token_block(B_OUT1 + 1, G_OUT1 + 4, q0=12)
            pe.wait_ge(act_ready, 32)
            mlp_layer(B_MLP1, G_MLP1, 32, None)


def _constants():
    c = np.zeros((P, C_END), np.float32)
    c[:, C_ID:C_ID + P] = np.eye(P, dtype=np.float32)
    q = np.arange(P)
    c[:, C_MASK:C_MASK + P] = np.where(q[None, :] > q[:, None], np.float32(NEG), np.float32(0))
    inv = (np.float32(1.0) / (np.float32(500000.0) ** (np.arange(0, ROT, 2, dtype=np.float32) / np.float32(ROT)))
           ).astype(np.float32)

    def rope(pos):
        ang = pos.astype(np.float32)[:, None] * inv[None, :]
        co, si = np.cos(ang), np.sin(ang)
        return np.concatenate([co, co], 1), np.concatenate([-si, si], 1)

    for t in range(T):
        co, si = rope(P * t + q)
        c[:, C_COS + ROT * t:C_COS + ROT * (t + 1)] = co
        c[:, C_SIN + ROT * t:C_SIN + ROT * (t + 1)] = si
        ends = 16 * np.arange(NC) + 31
        seen = (ends[None, :] <= (P * t + q)[:, None]) & (np.arange(NC) < NC - 1)[None, :]
        c[:, C_CADD + NC * t:C_CADD + NC * (t + 1)] = np.where(seen, 0, NEG)
        c[:, C_CMUL + t] = seen[:, 0]
    co, si = rope(16 * (q % NC) + 31)
    c[:, C_CCOS:C_CCOS + ROT] = co
    c[:, C_CSIN:C_CSIN + ROT] = si
    return c


def kernel(x, attn_norm_g, mlp_norm_g, nsa_w_in, nsa_ck_pos, nsa_ck_w1, nsa_ck_w2, nsa_cv_pos, nsa_cv_w1, nsa_cv_w2,
           nsa_w_out, diff_w_in, diff_lq1, diff_lk1, diff_lq2, diff_lk2, diff_subln_g, diff_w_out, mlp_w_up,
           mlp_w_down, final_norm_g):
    import concourse.bacc as bacc
    from concourse.bass_utils import run_bass_kernel_spmd

    def positions(pos):
        one = np.asarray(pos).reshape(16, 2, HD).transpose(2, 1, 0).reshape(HD, 32)
        return np.concatenate([one, one], 0)

    gains = [attn_norm_g[0], mlp_norm_g[0], attn_norm_g[1], mlp_norm_g[1]]
    vectors = np.concatenate([positions(nsa_ck_pos[0]), positions(nsa_cv_pos[0]),
                              np.asarray(diff_subln_g[0]).reshape(P, 1)], 1)
    ins = {
        "x": np.asarray(x)[0], "consts": _constants(), "vectors": vectors,
        "w_in": np.asarray(nsa_w_in)[0], "ck_w1": np.asarray(nsa_ck_w1)[0], "ck_w2": np.asarray(nsa_ck_w2)[0],
        "cv_w1": np.asarray(nsa_cv_w1)[0], "cv_w2": np.asarray(nsa_cv_w2)[0], "w_out": np.asarray(nsa_w_out)[0],
        "diff_in": np.asarray(diff_w_in)[0], "diff_out": np.asarray(diff_w_out)[0],
        "w_up": np.asarray(mlp_w_up), "w_down": np.asarray(mlp_w_down),
        "lam_in": np.concatenate([np.asarray(v) for v in (diff_lq1, diff_lk1, diff_lq2, diff_lk2)], 1),
        "norm_g": np.stack([np.asarray(g) for g in gains]),
        "final_g": np.asarray(final_norm_g).reshape(1, D),
    }
    ins = {n: np.ascontiguousarray(v) for n, v in ins.items()}
    nc = bacc.Bacc("TRN2", target_bir_lowering=False, num_devices=1, dynamic_dma_scratch_size=1024)
    aps = {n: nc.dram_tensor(f"in_{n}", v.shape, mybir.dt.from_np(v.dtype), kind="ExternalInput").ap()
           for n, v in ins.items()}
    out = nc.dram_tensor("out", (S, D), F32, kind="ExternalOutput").ap()
    build(nc, aps, out)
    r = run_bass_kernel_spmd(nc, [{f"in_{n}": v for n, v in ins.items()}], core_ids=[0])
    return r.results[0]["out"].reshape(1, S, D)
```

```python
import math
from contextlib import ExitStack

import numpy as np
import concourse.bass as bass
from concourse import mybir

F32 = mybir.dt.float32
F32R = mybir.dt.float32r
BF16 = mybir.dt.bfloat16
ALU = mybir.AluOpType
ACT = mybir.ActivationFunctionType
X = mybir.AxisListType.X

P = 128
S = 512
D = 1024
T = S // P
KT = D // P
NB = 512
HD = 64
GROUPS = 4
HPG = 4
NC = 32
ROT = 16
FF = 4096
CHUNK = 1024
STEPS = FF // CHUNK
DH = 8
EPS = 1e-6
SCALE = HD ** -0.5
LAMBDA_INIT = 0.8 - 0.6 * math.exp(-0.3)
GELU_C = math.sqrt(2.0 / math.pi)
NEG = -1e30
PT_ROW = 384
PT_BR = 1664

C_ID, C_MASK, C_COS, C_SIN, C_CCOS, C_CSIN, C_CADD, C_CMUL, C_END = (
    0, 128, 256, 320, 384, 400, 416, 544, 548)
V_POS, V_SUB, V_END = 0, 64, 65

B_CMP, B_W1K, B_SLC, B_W1V, B_WIN, B_Q0, B_Q1, B_OUT0 = 0, 1, 2, 3, 4, 5, 6, 7
B_MLP0, B_DIFF, B_OUT1, B_MLP1, B_ALL = 9, 25, 31, 33, 49
G_CMP, G_W1K, G_SLC, G_W1V, G_WIN, G_Q0, G_Q1, G_OUT0 = 0, 4, 5, 9, 10, 14, 18, 22
G_MLP0, G_DIFF, G_OUT1, G_MLP1 = 30, 62, 86, 94


def build(nc, a, out):
    with ExitStack() as ctx:
        def sb(name, shape, dt=F32):
            return ctx.enter_context(nc.sbuf_tensor(name, shape, dt))

        def sem(name):
            return ctx.enter_context(nc.semaphore(name))

        x_res = sb("x_res", [P, T, D])
        act_hi = sb("act_hi", [P, KT, S], F32R)
        act_lo = sb("act_lo", [P, KT, S], F32R)
        w_raw = sb("w_raw", [P, 4, 1024])
        w_hi = sb("w_hi", [P, 2, 4096], F32R)
        w_lo = sb("w_lo", [P, 2, 4096], F32R)
        kst = sb("kst", [P, 2, 2, 2, S], F32R)
        ar_r = sb("ar_r", [P, 8192], F32R)
        ar_f = sb("ar_f", [P, 10240])
        o_buf = sb("o_buf", [P, S])
        rtmp = sb("rtmp", [P, 256])
        cst = sb("cst", [P, C_END])
        vec = sb("vec", [P, V_END])
        ident_b = sb("ident_b", [P, P], BF16)
        mask_b = sb("mask_b", [P, P], BF16)
        lam2 = sb("lam2", [P, 2])
        st = sb("st", [P, 96])
        ps = ctx.enter_context(nc.psum_tensor("ps", [P, 8, NB], F32))

        ident = cst[:, C_ID:C_ID + P]

        def tab(c0, n, t=None):
            v = cst[:, c0:c0 + n]
            return v if t is None else v.rearrange("p (t r) -> p t r", t=t)

        def view(base, off, dims):
            return bass.AP(base.tensor, off, [list(base.ap[0])] + [list(d) for d in dims])

        HALF = D // 2
        y_bufs = [ar_f[:, 8192:9216], ar_f[:, 5120:6144]]
        gain = ar_f[:, 9216:10240]
        junk = ar_f[:, 7168:8192]
        x_cmp = ar_f[:, 8192:10240].rearrange("p (j c) -> p j c", j=16)
        q_raw = ar_f[:, 0:4096].rearrange("p (t c) -> p t c", t=T)
        k_raw = ar_f[:, 4096:6144].rearrange("p (b t c) -> p b t c", b=2, t=T)
        lamv_in = ar_f[:, 4096:4352]
        gate = ar_f[:, 7424:7616].rearrange("p (t c) -> p t c", t=T)
        gate_st = ar_f[:, 7616:7664].rearrange("p (t c) -> p t c", t=T)
        stage = ar_f[:, 6144:7168].rearrange("p (u t c) -> p u t c", u=2, t=T)
        c_sc = ar_f[:, 7680:8192]
        probs = ar_f[:, 8192:10240].rearrange("p (u k) -> p u k", u=4)
        g_h = [ar_f[:, 6144:6400], ar_f[:, 7168:7424]]
        g_a = [ar_f[:, 6400:6656], ar_f[:, 7680:7936]]
        g_b = ar_f[:, 6656:6912]
        kc_f = ar_f[:, 6912:6976]
        kc_r = ar_f[:, 6976:7040]
        tail_raw = ar_f[:, 0:384]
        w2_raw = ar_f[:, 384:640]
        relu_b = ar_f[:, 0:1024].rearrange("p (u c) -> p u c", u=2)
        sq_b = ar_f[:, 1024:2048].rearrange("p (u c) -> p u c", u=2)
        gfin = ar_f[:, 2048:3072]
        fin = ar_f[:, 3072:5120].rearrange("p (u c) -> p u c", u=2)
        dk_raw = ar_f[:, 4096:8192].rearrange("p (t c) -> p t c", t=T)

        xc_hi = [ar_r[:, 4096 * v:4096 * v + 2048].rearrange("p (j c) -> p j c", j=16) for v in range(2)]
        xc_lo = [ar_r[:, 4096 * v + 2048:4096 * v + 4096].rearrange("p (j c) -> p j c", j=16) for v in range(2)]
        v_all = ar_r[:, 0:4096].rearrange("p (t b g c) -> p t b g c", t=T, b=2, g=GROUPS)
        v_st = ar_r[:, 4096:5120].rearrange("p (t b c) -> p t b c", t=T, b=2)
        kc = ar_r[:, 5120:5376].rearrange("p (z c) -> p z c", z=2)
        vc = ar_r[:, 5376:5504]
        vc_st = ar_r[:, 5504:5632]
        vc_rep = ar_r[:, 5632:6144].rearrange("p (g c) -> p g c", g=GROUPS)
        q_stack = ar_r[:, 6144:8192].rearrange("p (h q) -> p h q", h=HPG)
        k_stack = kst[:, 0]
        early = kst[:, 1].rearrange("p z b q -> p (z b q)")
        tail_r = early[:, 0:768].rearrange("p (z c) -> p z c", z=2)
        hid_t = early[:, 1024:1536].rearrange("p (z c) -> p z c", z=2)
        w2_r = early[:, 1536:2048].rearrange("p (z c) -> p z c", z=2)
        a_hi = ar_r[:, 0:4096].rearrange("p (f c) -> p f c", f=8)
        a_lo = ar_r[:, 4096:8192].rearrange("p (f c) -> p f c", f=8)
        dv_all = ar_r[:, :].rearrange("p (t h c) -> p t h c", t=T, h=DH)
        slot0 = [w_hi[:, 0, :], w_lo[:, 0, :]]
        pct = [s[:, 3328:3840] for s in slot0]
        dq_stack = w_hi[:, 0, 1024:2048].rearrange("p (c q) -> p c q", c=2)
        dk_stage = w_lo[:, 0, 1024:3072].rearrange("p (c z t d) -> p c z t d", c=2, z=2, t=T)
        dq_stage = w_lo[:, 0, 3072:4096].rearrange("p (a t c d) -> p a t c d", a=2, t=2, c=2)
        dpt = [s[:, 0:1024].rearrange("p (u c) -> p u c", u=2) for s in slot0]

        ss1, pre, rstd = st[:, 0:20], st[:, 20:40], st[:, 40:60]
        ss2 = sb("ss2", [P, 20])
        d_ss, d_ms, d_rs = st[:, 76:80], st[:, 80:84], st[:, 84:88]
        half = st[:, 88:92]
        lam_s = st[:, 92:96]
        c_st = sb("c_st", [P, 4, 16])
        one = sb("one", [P, 1])
        nmax4, rsum4, rinv4 = st[:, 60:64], st[:, 64:68], st[:, 68:72]
        subg = sb("subg", [P, 1])

        x_landed = [sem(f"x_landed{t}") for t in range(T)]
        cst_landed, small_landed, gfin_landed = sem("cst_landed"), sem("small_landed"), sem("gfin_landed")
        part_landed = [sem(f"part_landed{j}") for j in range(4)]
        stored = [sem(f"stored{u}") for u in range(2)]
        hi_split, lo_split = sem("hi_split"), sem("lo_split")
        small_hi, small_lo = sem("small_hi"), sem("small_lo")
        tok_done, tok_free = sem("tok_done"), sem("tok_free")
        up_done, up_free, a_hi_done, a_ready = sem("up_done"), sem("up_free"), sem("a_hi_done"), sem("a_ready")
        sq_done = sem("sq_done")
        ss1_done, ss2_done, rstd_done = sem("ss1_done"), sem("ss2_done"), sem("rstd_done")
        y_done, turned, act_hi_done, act_ready, fin_done = (
            sem(n) for n in ("y_done", "turned", "act_hi_done", "act_ready", "fin_done"))
        gain_landed = sem("gain_landed")
        xc_hi_done, xc_ready = sem("xc_hi_done"), sem("xc_ready")
        gelu_arg, gelu_tanh, hid_done, hid_turned = sem("gelu_arg"), sem("gelu_tanh"), sem("hid_done"), sem("hid_turned")
        hid_hi, hid_lo, cmp_done, kc_roped, kc_turned, kc_hi = (
            sem(n) for n in ("hid_hi", "hid_lo", "cmp_done", "kc_roped", "kc_turned", "kc_hi"))
        cmp_ready = sem("cmp_ready")
        gate_done, gate_tanh, gate_turned = sem("gate_done"), sem("gate_tanh"), sem("gate_turned")
        lam_arg, lam_exp = sem("lam_arg"), sem("lam_exp")
        roped, gates_ready, gate_staged, stage_hi, stage_filled, st_turned, stacked_a, stacked_v = (
            sem(n) for n in ("roped", "gates_ready", "gate_staged", "stage_hi", "stage_filled", "st_turned",
                             "stacked_a", "stacked_v"))
        v_staged, cs_done, cs_sub, cs_exp, cs_coef, pc_ready, pc_turned, pc_hi, pc_lo = (
            sem(n) for n in ("v_staged", "cs_done", "cs_sub", "cs_exp", "cs_coef", "pc_ready", "pc_turned",
                             "pc_hi", "pc_lo"))
        cs_masked, cs_max, cs_sum, cs_inv = (sem(n) for n in ("cs_masked", "cs_max", "cs_sum", "cs_inv"))
        s_done, max_done, exp_done, rinv_done, normed, p_turned, pt_hi, pt_lo = (
            sem(n) for n in ("s_done", "max_done", "exp_done", "rinv_done", "normed", "p_turned", "pt_hi", "pt_lo"))
        pv_done, o_half, o_sum, o_hi, o_lo = (sem(n) for n in ("pv_done", "o_half", "o_sum", "o_hi", "o_lo"))
        d_roped, dq_hi, dk_filled, dq_filled, dk_turned, dq_turned, dk_stacked, dq_stacked = (
            sem(n) for n in ("d_roped", "dq_hi", "dk_filled", "dq_filled", "dk_turned", "dq_turned", "dk_stacked",
                             "dq_stacked"))
        ds_done, dmax_done, dexp_done, drinv_done, dp1_done, da_done, dp_turned, dpt_hi, dpt_lo = (
            sem(n) for n in ("ds_done", "dmax_done", "dexp_done", "drinv_done", "dp1_done", "da_done", "dp_turned",
                             "dpt_hi", "dpt_lo"))
        dpv_done, do_free, d_ss_done, d_ms_done, d_rs_done, dy_done, do_turned, do_hi, do_lo = (
            sem(n) for n in ("dpv_done", "do_free", "d_ss_done", "d_ms_done", "d_rs_done", "dy_done", "do_turned",
                             "do_hi", "do_lo"))
        dve_order, act_order, pool_order = sem("dve_order"), sem("act_order"), sem("pool_order")
        pool_passed = sem("pool_passed")

        class Order:

            def __init__(self, eng, s):
                self.eng, self.s, self.base, self.loop = eng, s, 0, 0

            def after(self, ins):
                ins.then_inc(self.s, 1)
                self.base += 1
                self.eng.wait_ge(self.s, self.loop + self.base)

            def enter(self, i, per):
                self.loop, self.at, self.per = i * per, self.base, per

            def leave(self, count):
                assert self.base == self.at + self.per, (self.base - self.at, self.per)
                self.base, self.loop = self.at + self.per * count, 0

        SLOT0 = -22
        UNITS = 2 * HPG * T
        TILE_ORDER = (3, 0, 2, 1)
        L_MAX, L_EXP, L_NORM, L_TURN, L_SPLIT, L_PV = 1, 2, 3, 4, 5, 6
        TURNS = (-19, -18, -16, -14, -12, -10, -7, 0)

        def at(gg, per, n):
            g, off = gg
            assert isinstance(g, int) or off * per + n > 0, (off, per, n)
            return g * per + (off * per + n)

        def place(gg, per, n):
            return gg[0] * per + (gg[1] * per + n)

        def first(gg):
            return isinstance(gg[0], int) and sum(gg) == 0

        def await_(eng, s, value):
            if not isinstance(value, int) or value > 0:
                return eng.wait_ge(s, value)

        def windows(eng, slot, s0, units, spans, count, begun=None):
            def window(groups):
                for k in range(s0, s0 + units):
                    for span, gg in groups:
                        if begun is None or not first(gg) or k + units * span >= begun:
                            slot(gg, k + units * span)

            for m in range(spans - 1):
                window([(w, (m - w, 0)) for w in reversed(range(m + 1))])
            with eng.Fori(0, count - spans + 1) as g:
                window([(w, (g, spans - 1 - w)) for w in reversed(range(spans))])
            for m in range(count, count + spans - 1):
                window([(w, (m - w, 0)) for w in reversed(range(m - count + 1, spans))])

        def keys(gg, z, br, n=S):
            g, off = gg
            par = (g + off) % 2
            if isinstance(par, int):
                return kst[:, par, z, br, 0:n]
            return kst[:, bass.ds(par, 1), z, br, 0:n].rearrange("p o c -> p (o c)")

        def unit(v):
            i = TILE_ORDER[v % 4]
            return v // 8, v // 4 % 2, i, P * (i + 1)

        D_SLOT0, D_UNITS, D_SPANS = -10, 2 * T, 4
        D_TURN_K, D_TURN_Q = (-8, -7, -6, -3), (-4, -1)
        D_P1, D_A, D_TURN, D_SPLIT, D_PV, D_OUT, D_SS = 4, 5, 6, 7, 8, 9, 10
        D_MS, D_Y, D_OUT_TURN, D_OUT_SPLIT = 17, 18, 19, 20

        def key_stage(hh):
            if first(hh):
                return early.rearrange("p (c z t d) -> p c z t d", c=2, z=2, t=T)
            return dk_stage

        def query_stage(hh):
            if first(hh):
                return ar_f[:, 8192:9216].rearrange("p (a t c d) -> p a t c d", a=2, t=2, c=2).bitcast(F32R)
            return dq_stage

        def tile_at(k, lag):
            return (k - lag) // 2 if 0 <= k - lag < 2 * T and (k - lag) % 2 == 0 else None

        def cols(w, c0, j):
            return w[256 * j:256 * (j + 1), c0:c0 + NB].rearrange("(k p) c -> p k c", p=P)

        CMP0, SLC0, WIN0, TAIL0 = D, D + 512, D + 1024, D + 1536

        def part_source(n, j):
            if n in (B_W1K, B_W1V):
                w = a["ck_w1"] if n == B_W1K else a["cv_w1"]
                return w[512 * j:512 * (j + 1), :].rearrange("(k p) c -> p k c", p=P)
            if n < B_OUT0:
                c0 = {B_CMP: CMP0, B_SLC: SLC0, B_WIN: WIN0, B_Q0: 0, B_Q1: NB}[n]
                return cols(a["w_in"], c0, j)
            if n < B_MLP0:
                return cols(a["w_out"], NB * (n - B_OUT0), j)
            if n < B_OUT1:
                return cols(a["diff_in"], NB * (n - B_DIFF), j)
            return cols(a["diff_out"], NB * (n - B_OUT1), j)

        def mlp_source(layer, it, c, j):
            if c < 2:
                w = a["w_up"][layer, 256 * j:256 * (j + 1), bass.ds(it * CHUNK + NB * c, NB)]
            else:
                w = a["w_down"][layer, bass.ds(it * CHUNK + 256 * j, 256), NB * (c - 2):NB * (c - 1)]
            return w.rearrange("(k p) c -> p k c", p=P)

        def slot_of(n):
            return n % 2

        block = ctx.enter_context(nc.Block())

        @block.sync
        def _(sp):
            for t in range(T):
                sp.dma_start(x_res[:, t, :], a["x"][P * t:P * (t + 1), :]).then_inc(x_landed[t], 16)

            def load(n, j, src):
                if not isinstance(n, int) or n > 0:
                    sp.wait_ge(lo_split, n * 4 + (j - 3))
                if len(src.shape) == 3 and src.shape[1] == 4:
                    dst = w_raw[:, j, :].rearrange("p (k c) -> p k c", k=4)
                else:
                    dst = w_raw[:, j, :].rearrange("p (k c) -> p k c", k=2)
                sp.dma_start(dst, src).then_inc(part_landed[j], 16)

            def straight(n0, n1):
                for n in range(n0, n1):
                    for j in range(4):
                        load(n, j, part_source(n, j))

            straight(0, B_MLP0)
            with sp.Fori(0, STEPS) as it:
                for c in range(4):
                    for j in range(4):
                        load(it * 4 + (B_MLP0 + c), j, mlp_source(0, it, c, j))
            straight(B_DIFF, B_MLP1)
            with sp.Fori(0, STEPS) as it:
                for c in range(4):
                    for j in range(4):
                        load(it * 4 + (B_MLP1 + c), j, mlp_source(1, it, c, j))
            for t in range(T):
                for b in range(2):
                    sp.wait_ge(fin_done, 2 * t + b + 1)
                    sp.dma_start(out[P * t:P * (t + 1), HALF * b:HALF * (b + 1)],
                                 fin[:, t % 2, HALF * b:HALF * (b + 1)]).then_inc(stored[t % 2], 16)
            for u in range(2):
                sp.wait_ge(stored[u], 16 * T)

        @block.gpsimd
        def _(pool):
            order = Order(pool, pool_order)
            order.after(pool.memset(half, -0.5))

            def norm_stat(q):
                pool.wait_ge(ss1_done, q + 1)
                order.after(pool.tensor_scalar(pre[:, q:q + 1], ss1[:, q:q + 1], 1.0, EPS, ALU.mult, ALU.add))
                pool.wait_ge(ss2_done, q + 1)
                order.after(pool.tensor_tensor(pre[:, q:q + 1], ss2[:, q:q + 1], pre[:, q:q + 1], ALU.add))
                pool.tensor_tensor(rstd[:, q:q + 1], pre[:, q:q + 1], half[:, 0:1], ALU.pow).then_inc(rstd_done, 1)

            for q in range(4):
                norm_stat(q)
            for j in range(2):
                pool.wait_ge(hi_split, j + 1)
                pool.tensor_tensor(w_lo[:, 0, 1024 * j:1024 * (j + 1)], w_raw[:, j, :],
                                   w_hi[:, 0, 1024 * j:1024 * (j + 1)].bitcast(F32), ALU.subtract).then_inc(lo_split, 1)
            order.after(pool.memset(one[:, :], 1.0))

            def hold(s, value):
                if not isinstance(value, int) or value > 0:
                    pool.wait_ge(s, value).then_inc(pool_passed, 1)

            def fill(gg, e):
                if first(gg):
                    pool.wait_ge(roped, 8 if e < 4 else 12)
                hold(st_turned, at(gg, 8, e - 1))
                hold(stage_filled, at(gg, 8, e))
                if e < 4:
                    br, z = e // 2, e % 2
                    src = k_raw[:, br, :, bass.ds(place(gg, HD, 0), HD)].unsqueeze(2).broadcast_to([P, T, 2, HD])
                    dst = stage[:, z].rearrange("p t (u d) -> p t u d", u=2)
                    if z == 0:
                        pool.tensor_tensor(dst.bitcast(F32R), src, one[:, :].unsqueeze(2).unsqueeze(2).broadcast_to([P, T, 2, HD]),
                                           ALU.mult).then_inc(stage_filled, 1)
                    else:
                        hi = stage[:, 0].rearrange("p t (u d) -> p t u d", u=2)
                        pool.tensor_tensor(dst, src, hi, ALU.subtract).then_inc(stage_filled, 1)
                else:
                    h = e - 4
                    src = q_raw[:, :, bass.ds(place(gg, HPG * HD, HD * h), HD)]
                    hi, lo = stage[:, e % 2, :, 0:HD], stage[:, e % 2, :, HD:P]
                    pool.tensor_tensor(hi.bitcast(F32R), src, one[:, :].unsqueeze(2).broadcast_to([P, T, HD]),
                                       ALU.mult).then_inc(stage_hi, 1)
                    hold(stage_hi, at(gg, HPG, h + 1))
                    pool.tensor_tensor(lo, src, hi, ALU.subtract).then_inc(stage_filled, 1)

            def stage_values(gg, br):
                hold(pv_done, at(gg, 8, br - 1))
                pool.tensor_tensor(v_st[:, :, br, :], v_all[:, :, br, bass.ds(place(gg, 1, 0), 1), :].bitcast(F32)
                                   .rearrange("p t o c -> p t (o c)"), one[:, :].unsqueeze(2).broadcast_to([P, T, P]),
                                   ALU.mult).then_inc(v_staged, 1)
                if br == 1:
                    pool.tensor_tensor(vc_st, vc_rep[:, bass.ds(place(gg, 1, 0), 1), :].bitcast(F32)
                                       .rearrange("p o c -> p (o c)"), one[:, :].broadcast_to([P, P]),
                                       ALU.mult).then_inc(v_staged, 1)

            def norm_probs(gg, v):
                h, br, i, n = unit(v)
                if v == 0:
                    hold(gate_staged, at(gg, 1, 1))
                hold(rinv_done, at(gg, UNITS, v + 1))
                p = probs[:, v % 4, 0:n]
                pool.tensor_scalar(p, p, rinv4[:, v % 4:v % 4 + 1], gate_st[:, i, 3 * h + 1 + br:3 * h + 2 + br],
                                   ALU.mult, ALU.mult).then_inc(normed, 1)

            def slot(gg, k):
                if 0 <= k - L_NORM < UNITS:
                    norm_probs(gg, k - L_NORM)
                if k == L_NORM - 1:
                    if first(gg):
                        pool.wait_ge(gates_ready, 1)
                    hold(normed, at(gg, UNITS, 0))
                    pool.tensor_copy(gate_st[:, :, :], gate[:, :, bass.ds(place(gg, 3 * HPG, 0), 3 * HPG)]
                                     ).then_inc(gate_staged, 1)
                if k + 2 in TURNS:
                    fill(gg, TURNS.index(k + 2))
                if k == 3:
                    stage_values(gg, 0)
                if k == 7:
                    stage_values(gg, 1)
                if k == 10:
                    hold(cs_coef, at(gg, 1, 1))
                    ef = c_sc.rearrange("p (r n) -> p r n", n=NC)
                    pool.tensor_tensor(ef, ef, c_st[:, 3, :].unsqueeze(2).broadcast_to([P, 16, NC]),
                                       ALU.mult).then_inc(pc_ready, 1)
                if first(gg) and k == SLOT0 + UNITS - 1:
                    pool.wait_ge(roped, 16)

            windows(pool, slot, SLOT0, UNITS, 2, GROUPS)

            for q in range(4, 12):
                norm_stat(q)

            pool.wait_ge(d_roped, 16)

            def fill_keys(hh, e):
                c, z = e // 2, e % 2
                src = dk_raw[:, :, bass.ds(place(hh, P, HD * c), HD)].unsqueeze(2).broadcast_to([P, T, 2, HD])
                if e == 0 and isinstance(hh[0], int) and sum(hh) == 1:
                    pool.wait_ge(tok_done, G_OUT1)
                hi, dst = (key_stage(hh)[:, c, zz].rearrange("p t (u d) -> p t u d", u=2) for zz in (0, z))
                hold(dk_turned, at(hh, 4, e + 1 - 4))
                if z == 0:
                    pool.tensor_tensor(dst, src, one[:, :].unsqueeze(2).unsqueeze(2).broadcast_to([P, T, 2, HD]),
                                       ALU.mult).then_inc(dk_filled, 1)
                else:
                    hold(dk_filled, at(hh, 4, e))
                    pool.tensor_tensor(dst, src, hi.bitcast(F32), ALU.subtract).then_inc(dk_filled, 1)

            def fill_queries(hh, a):
                hold(dq_turned, at(hh, 2, a + 1 - 2))
                hi, lo = query_stage(hh)[:, a, :, :, 0:HD], query_stage(hh)[:, a, :, :, HD:P]
                src = q_raw[:, 2 * a:2 * a + 2, bass.ds(place(hh, P, 0), P)].rearrange("p t (c d) -> p t c d", c=2)
                pool.tensor_tensor(hi, src, one[:, :].unsqueeze(2).unsqueeze(2).broadcast_to([P, 2, 2, HD]),
                                   ALU.mult).then_inc(dq_hi, 1)
                hold(dq_hi, at(hh, 2, a + 1))
                pool.tensor_tensor(lo, src, hi.bitcast(F32), ALU.subtract).then_inc(dq_filled, 1)

            def d_slot(hh, k):
                i = tile_at(k, D_P1)
                if i is not None:
                    hold(drinv_done, at(hh, D_UNITS, 2 * i + 2))
                    u = (2 * i + 1) % 4
                    p = probs[:, u, 0:P * (i + 1)]
                    pool.tensor_scalar(p, p, rinv4[:, u:u + 1], lam2[:, 1:2], ALU.mult, ALU.mult).then_inc(dp1_done, 1)
                if k == D_MS:
                    hold(d_ms_done, at(hh, 1, 1))
                    pool.tensor_tensor(d_rs, d_ms, half, ALU.pow).then_inc(d_rs_done, 1)
                if k + 2 in D_TURN_K:
                    fill_keys(hh, D_TURN_K.index(k + 2))
                if k + 2 in D_TURN_Q:
                    fill_queries(hh, D_TURN_Q.index(k + 2))

            windows(pool, d_slot, D_SLOT0, D_UNITS, D_SPANS, DH)
            for q in range(12, 20):
                norm_stat(q)

        @block.scalar
        def _(act):
            order = Order(act, act_order)
            def load_gain(r):
                act.dma_start(gain, a["norm_g"][r:r + 1, :].partition_broadcast(P).rearrange("p o c -> p (o c)")
                              ).then_inc(gain_landed, 16)

            load_gain(0)
            act.dma_start(cst[:, :], a["consts"]).then_inc(cst_landed, 16)
            act.dma_start(vec[:, :], a["vectors"]).then_inc(cst_landed, 16)
            act.dma_start(tail_raw.rearrange("p (k c) -> p k c", k=KT),
                          a["w_in"][:, TAIL0:TAIL0 + 48].rearrange("(k p) c -> p k c", p=P)).then_inc(small_landed, 16)
            for v, w in enumerate((a["ck_w2"], a["cv_w2"])):
                act.dma_start(w2_raw[:, P * v:P * (v + 1)].rearrange("p (k c) -> p k c", k=2),
                              w.rearrange("(k p) c -> p k c", p=P)).then_inc(small_landed, 16)
            act.dma_start(lamv_in[:, :], a["lam_in"].partition_broadcast(P).rearrange("p o c -> p (o c)")
                          ).then_inc(small_landed, 16)

            def split_hi(n, j):
                act.wait_ge(part_landed[j], n * 16 + 16)
                act.copy(w_hi[:, slot_of(n), 1024 * j:1024 * (j + 1)], w_raw[:, j, :]).then_inc(hi_split, 1)

            def norm_sum(q, t, b):
                done = (ss1_done, ss2_done)[b]
                if q:
                    act.wait_ge(done, q)
                act.activation(junk[:, HALF * b:HALF * (b + 1)], x_res[:, t, HALF * b:HALF * (b + 1)], ACT.Square,
                               scale=D ** -0.5, accum_out=(ss1, ss2)[b][:, q:q + 1]).then_inc(done, 1)

            def norm_hi(q, t):
                for b in range(2):
                    act.wait_ge(turned, 2 * q + b + 1)
                    act.copy(act_hi[:, 4 * b:4 * b + 4, P * t:P * (t + 1)],
                             ps[:, 4 + 2 * (q % 2) + b, :].rearrange("p (k c) -> p k c", c=P)).then_inc(act_hi_done, 1)

            def norm_first(q0, g):
                for t in range(T):
                    act.wait_ge(tok_free, g + t + 1)
                    norm_sum(q0 + t, t, 0)

            def norm_tail(q0, g, last=False):
                for t in range(T):
                    act.wait_ge(tok_free, g + t + 1)
                    norm_sum(q0 + t, t, 1)
                    if t and not last:
                        norm_hi(q0 + t - 1, t - 1)
                if not last:
                    norm_hi(q0 + T - 1, T - 1)

            act.wait_ge(pool_order, 1)
            act.activation(c_st[:, 0, 0:4], half, ACT.Exp)
            for t in range(T):
                act.wait_ge(x_landed[t], 16)
                norm_sum(t, t, 0)
                norm_sum(t, t, 1)
            norm_hi(0, 0)
            for t in range(1, T):
                norm_hi(t, t)
                split_hi(0, t - 1)
            split_hi(0, T - 1)

            def split_next(n, j, wait):
                if j == 0:
                    act.wait_ge(*wait)
                split_hi(n, j)

            for j in range(4):
                split_hi(B_W1K, j)
            act.wait_ge(tok_free, G_CMP + 2)
            act.copy(xc_hi[0], x_cmp).then_inc(xc_hi_done, 1)
            for j in range(4):
                split_next(B_SLC, j, (tok_done, G_CMP + 4))
            act.wait_ge(tok_free, G_CMP + 4)
            act.copy(xc_hi[1], x_cmp).then_inc(xc_hi_done, 1)
            act.wait_ge(small_landed, 64)
            act.copy(tail_r[:, 0, :], tail_raw).then_inc(small_hi, 1)
            act.copy(w2_r[:, 0, :], w2_raw).then_inc(small_hi, 1)
            for j in range(4):
                split_next(B_W1V, j, (tok_done, G_W1K + 1))

            def gelu(v):
                act.wait_ge(gelu_arg, v + 1)
                act.activation(g_a[v], g_a[v], ACT.Tanh, scale=GELU_C).then_inc(gelu_tanh, 1)

            def hidden_hi(v):
                act.wait_ge(hid_turned, v + 1)
                act.copy(hid_t[:, 0, :], ps[:, 4, 0:256]).then_inc(hid_hi, 1)

            gelu(0)
            for j in range(4):
                split_next(B_WIN, j, (tok_done, G_SLC + 4))
            for j in range(4):
                split_next(B_Q0, j, (tok_done, G_W1V + 1))
            gelu(1)
            hidden_hi(0)
            act.wait_ge(kc_turned, 1)
            act.copy(kc[0:HD, 0, :], ps[0:HD, 6, 0:P]).then_inc(kc_hi, 1)
            act.copy(kc[HD:P, 0, :], ps[0:HD, 6, 0:P]).then_inc(kc_hi, 1)
            hidden_hi(1)
            for j in range(4):
                split_next(B_Q1, j, (tok_done, G_WIN + 4))
            for j in range(4):
                split_next(B_OUT0, j, (tok_done, G_Q0 + 4))
            act.wait_ge(gate_done, 1)
            act.activation(o_buf[0:48, :], ps[0:48, 6, :], ACT.Tanh, scale=0.5).then_inc(gate_tanh, 1)
            act.wait_ge(lam_arg, 1)
            act.activation(lam_s[:, 2:4], lam_s[:, 0:2], ACT.Exp).then_inc(lam_exp, 1)

            def stack(gg, e):
                act.wait_ge(st_turned, at(gg, 8, e + 1))
                if e < 4:
                    act.copy(keys(gg, 0, e // 2), ps[:, 7, :]).then_inc(stacked_a, 1)
                else:
                    h = e - 4
                    await_(act, s_done, at(gg, UNITS, 8 * (h + 1) - UNITS))
                    act.mul(q_stack[:, h, :], ps[:, 7, :], SCALE).then_inc(stacked_a, 1)

            for e in (0, 2, 4, 5, 6):
                stack((0, 0), e)

            def exps(gg, v):
                n = unit(v)[3]
                act.wait_ge(max_done, at(gg, UNITS, v + 1))
                await_(act, p_turned, at(gg, UNITS, v - 3))
                act.activation(probs[:, v % 4, 0:n], ps[:, v % 4, 0:n], ACT.Exp, bias=nmax4[:, v % 4:v % 4 + 1],
                               accum_out=rsum4[:, v % 4:v % 4 + 1]).then_inc(exp_done, 1)

            def turned_hi(gg, v):
                h, br, i, n = unit(v)
                act.wait_ge(p_turned, at(gg, UNITS, v + 1))
                if v % 4 == 0:
                    await_(act, pv_done, at(gg, 8, 2 * (h - 1) + br + 1))
                act.copy(view(slot0[0], PT_BR * br + P * i, [[PT_ROW, i + 1], [1, P]]),
                         ps[:, 4 + v % 2, 0:n].rearrange("p (j c) -> p j c", c=P)).then_inc(pt_hi, 1)

            def out_half(gg, h):
                r = HD * (h % 2)
                act.wait_ge(pv_done, at(gg, 8, 2 * h + 2))
                if h >= 2:
                    act.wait_ge(o_lo, at(gg, 4, h - 1))
                act.copy(o_buf[r:r + HD, :], ps[HD:P, 6, :]).then_inc(o_half, 1)

            def out_hi(gg, h):
                r = HD * (h % 2)
                act.wait_ge(o_sum, at(gg, 4, h + 1))
                act.copy(act_hi[r:r + HD, bass.ds(place(gg, 2, h // 2), 1), :].rearrange("p o c -> p (o c)"),
                         o_buf[r:r + HD, :]).then_inc(o_hi, 1)

            def slot(gg, k):
                if 0 <= k - L_SPLIT < UNITS:
                    turned_hi(gg, k - L_SPLIT)
                if 0 <= k - L_EXP < UNITS:
                    exps(gg, k - L_EXP)
                if k - 1 in TURNS and TURNS.index(k - 1) not in (1, 3):
                    stack(gg, TURNS.index(k - 1))
                if k == 8:
                    act.wait_ge(cs_sub, at(gg, 1, 1))
                    act.activation(c_sc, c_sc, ACT.Exp).then_inc(cs_exp, 1)
                if k == 12:
                    act.wait_ge(pc_turned, at(gg, 1, 1))
                    act.copy(pct[0], ps[:, 7, :]).then_inc(pc_hi, 1)
                if k >= 14 and (k - 14) % 8 == 0:
                    out_half(gg, (k - 14) // 8)
                if k >= 16 and (k - 16) % 8 == 0:
                    out_hi(gg, (k - 16) // 8)

            windows(act, slot, SLOT0, UNITS, 2, GROUPS, begun=0)

            for j in range(4):
                split_next(B_OUT0 + 1, j, (pv_done, 8 * GROUPS))
            load_gain(1)
            norm_first(4, G_OUT0)
            for j in range(4):
                split_next(B_MLP0, j, (tok_done, G_OUT0 + 4))
            norm_tail(4, G_OUT0 + 4)
            load_gain(2)

            def relu(u, u_abs):
                act.wait_ge(up_done, u_abs + (u + 1))
                if u >= 2:
                    act.wait_ge(a_ready, u_abs + (u - 1))
                act.activation(relu_b[:, u % 2, :], ps[:, (u + 2) % 4, :], ACT.Relu).then_inc(up_free, 1)
                act.wait_ge(up_free, u_abs + (u + 1))
                act.activation(a_hi[:, u, :], relu_b[:, u % 2, :], ACT.Square).then_inc(a_hi_done, 1)

            def mlp_step(n, gr, up, last):
                for c in range(4):
                    for j in range(4):
                        if not (c == 3 and last == 16):
                            w = [(tok_done, gr), (up_done, up + 4), (up_done, up + 8), (tok_done, gr + 4)][c]
                            if j == 0:
                                act.wait_ge(*w)
                            act.wait_ge(part_landed[j], (n + (c + 1)) * 16 + 16)
                            act.copy(w_hi[:, (c + B_MLP0 + 1) % 2, 1024 * j:1024 * (j + 1)],
                                     w_raw[:, j, :]).then_inc(hi_split, 1)
                        if c < 2:
                            relu(4 * c + j, up)
                    if c == 2 and last is not None:
                        norm_first(last, gr)

            def mlp_layer(n0, g0, u0, end):
                with act.Fori(0, STEPS - 1) as it:
                    mlp_step(it * 4 + n0, it * 8 + g0, it * 8 + u0, None)
                k = STEPS - 1
                mlp_step(n0 + 4 * k, g0 + 8 * k, u0 + 8 * k, end)

            mlp_layer(B_MLP0, G_MLP0, 0, 8)
            norm_tail(8, G_DIFF - 4)

            for b in range(6):
                prev = (tok_done, G_DIFF + 4 * b)
                if b < 6:
                    for j in range(4):
                        split_next(B_DIFF + b + 1, j, prev)

            def d_stack_keys(hh, e):
                act.wait_ge(dk_turned, at(hh, 4, e + 1))
                act.copy(keys(hh, e % 2, e // 2), ps[:, (7, 5)[e % 2], :]).then_inc(dk_stacked, 1)

            for e in range(4):
                d_stack_keys((0, 0), e)

            def d_stack_queries(hh, a):
                act.wait_ge(dq_turned, at(hh, 2, a + 1))
                await_(act, ds_done, at(hh, D_UNITS, 4 * (a + 1) - D_UNITS))
                act.mul(dq_stack[:, :, 2 * P * a:2 * P * (a + 1)],
                        ps[:, (7, 5)[a], :].rearrange("p (c q) -> p c q", c=2), SCALE).then_inc(dq_stacked, 1)

            def d_exps(hh, u):
                i, c, n = u // 2, u % 2, P * (u // 2 + 1)
                act.wait_ge(dmax_done, at(hh, D_UNITS, u + 1))
                await_(act, dp_turned if c else da_done, at(hh, T, i - 1))
                act.activation(probs[:, u % 4, 0:n], ps[:, u % 4, 0:n], ACT.Exp, bias=nmax4[:, u % 4:u % 4 + 1],
                               accum_out=rsum4[:, u % 4:u % 4 + 1]).then_inc(dexp_done, 1)

            def d_slot(hh, k):
                i = tile_at(k, D_SPLIT)
                if i is not None:
                    act.wait_ge(dp_turned, at(hh, T, i + 1))
                    await_(act, dpv_done, at(hh, T, i - 1))
                    n = P * (i + 1)
                    act.copy(dpt[0][:, i % 2, 0:n], ps[:, 4, 0:n]).then_inc(dpt_hi, 1)
                if 0 <= k - L_EXP < D_UNITS:
                    d_exps(hh, k - L_EXP)
                i = tile_at(k, D_SS)
                if i is not None:
                    act.wait_ge(do_free, at(hh, T, i + 1))
                    if i == 0:
                        await_(act, d_ms_done, at(hh, 1, 0))
                    head = bass.ds(place(hh, P, 0), P)
                    act.activation(dk_raw[:, i, head], q_raw[:, i, head], ACT.Square,
                                   accum_out=d_ss[:, i:i + 1]).then_inc(d_ss_done, 1)
                if k - 1 in D_TURN_K and not first(hh):
                    d_stack_keys(hh, D_TURN_K.index(k - 1))
                if k - 1 in D_TURN_Q:
                    d_stack_queries(hh, D_TURN_Q.index(k - 1))
                if k == D_OUT_SPLIT and isinstance(hh[0], int) and sum(hh) == DH - 1:
                    for j in range(4):
                        split_next(B_OUT1 + 1, j, (dpv_done, T * DH))
                if k == D_OUT_SPLIT:
                    act.wait_ge(do_turned, at(hh, 1, 1))
                    act.activation(act_hi[:, bass.ds(place(hh, 1, 0), 1), :].rearrange("p o c -> p (o c)"), ps[:, 5, :],
                                   ACT.Copy, scale=subg[:, 0:1]).then_inc(do_hi, 1)

            windows(act, d_slot, D_SLOT0, D_UNITS, D_SPANS, DH)

            act.dma_start(gfin, a["final_g"].partition_broadcast(P).rearrange("p o c -> p (o c)")
                          ).then_inc(gfin_landed, 16)
            load_gain(3)
            norm_first(12, G_OUT1)
            for j in range(4):
                split_next(B_MLP1, j, (tok_done, G_OUT1 + 4))
            norm_tail(12, G_OUT1 + 4)
            mlp_layer(B_MLP1, G_MLP1, 32, 16)
            norm_tail(16, G_MLP1 + 28, last=True)

        @block.vector
        def _(dve):
            order = Order(dve, dve_order)

            def sub(out_, in0, hi):
                return dve.tensor_tensor(out_, in0, hi.bitcast(F32), ALU.subtract)

            def split_lo(n, j, slot=None):
                dve.wait_ge(hi_split, n * 4 + (j + 1))
                sl = slot_of(n) if slot is None else slot
                sub(w_lo[:, sl, 1024 * j:1024 * (j + 1)], w_raw[:, j, :],
                    w_hi[:, sl, 1024 * j:1024 * (j + 1)]).then_inc(lo_split, 1)

            def norm_y(q, t):
                if t == 0:
                    dve.wait_ge(gain_landed, 16 * (q // 4 + 1))
                dve.wait_ge(rstd_done, q + 1)
                if q >= 2:
                    dve.wait_ge(turned, 2 * (q - 1))
                for b in range(2):
                    c = slice(HALF * b, HALF * (b + 1))
                    dve.scalar_tensor_tensor(out=y_bufs[q % 2][:, c], in0=x_res[:, t, c], scalar=rstd[:, q:q + 1],
                                             in1=gain[:, c], op0=ALU.mult, op1=ALU.mult).then_inc(y_done, 1)

            def norm_lo(q, t):
                for b in range(2):
                    dve.wait_ge(act_hi_done, 2 * q + b + 1)
                    at_ = (slice(None), slice(4 * b, 4 * b + 4), slice(P * t, P * (t + 1)))
                    sub(act_lo[at_], ps[:, 4 + 2 * (q % 2) + b, :].rearrange("p (k c) -> p k c", c=P), act_hi[at_]
                        ).then_inc(act_ready, 1)

            dve.wait_ge(cst_landed, 32)
            dve.tensor_copy(ident_b[:, :], ident).then_inc(small_lo, 1)
            dve.tensor_copy(mask_b[:, :], tab(C_MASK, P)).then_inc(small_lo, 1)
            dve.tensor_scalar(subg[:, :], vec[:, V_SUB:V_SUB + 1], 1.0 - LAMBDA_INIT, None, ALU.mult)
            for t in range(T):
                norm_y(t, t)
                if t:
                    norm_lo(t - 1, t - 1)
            norm_lo(T - 1, T - 1)
            dve.wait_ge(lo_split, 2)
            split_lo(0, 2)
            split_lo(0, 3)

            dve.wait_ge(act_ready, 8)
            order.after(dve.memset(x_cmp.rearrange("p j (g n) -> p j g n", g=GROUPS)[:, :, :, NC - 1:NC], 0.0))
            for m in range(4):
                v, bank = m // 2, (G_CMP + m) % 4
                if m == 2:
                    split_lo(B_W1K, 2)
                    dve.wait_ge(xc_hi_done, 1)
                    sub(xc_lo[0], x_cmp, xc_hi[0]).then_inc(xc_ready, 1)
                    dve.wait_ge(xc_ready, 1)
                if m == 2:
                    split_lo(B_W1K, 3)
                if m < 2:
                    split_lo(B_W1K, m)
                if m == 3:
                    for j in range(4):
                        split_lo(B_SLC, j)
                dve.wait_ge(tok_done, G_CMP + m + 1)
                for gl in range(2):
                    r, g = HD * gl, 2 * (m % 2) + gl
                    src = ps[r:r + HD, bank, :].rearrange("p (n b) -> p b n", b=16)
                    for par in range(2):
                        for jh in range(2):
                            pos = vec[r:r + HD, V_POS + 32 * v + 16 * par + 8 * jh:V_POS + 32 * v + 16 * par + 8 * jh + 8]
                            ins = dve.tensor_tensor(
                                x_cmp[HD * par:HD * (par + 1), 8 * jh:8 * jh + 8, NC * g:NC * g + NC - 1],
                                src[:, par::2, jh:jh + NC - 1],
                                pos.unsqueeze(2).broadcast_to([HD, 8, NC - 1]), ALU.add)
                ins.then_inc(tok_free, 1)
            dve.wait_ge(xc_hi_done, 2)
            sub(xc_lo[1], x_cmp, xc_hi[1]).then_inc(xc_ready, 1)
            dve.wait_ge(small_hi, 2)
            sub(tail_r[:, 1, :], tail_raw, tail_r[:, 0, :]).then_inc(small_lo, 1)
            sub(w2_r[:, 1, :], w2_raw, w2_r[:, 0, :]).then_inc(small_lo, 1)
            lv = lamv_in[:, :].rearrange("p (v u c) -> p v u c", v=2, u=2)
            order.after(dve.tensor_tensor(rtmp[:, 0:128].rearrange("p (v c) -> p v c", v=2), lv[:, :, 0, :],
                                          lv[:, :, 1, :], ALU.mult))
            dve.tensor_reduce(lam_s[:, 0:2], rtmp[:, 0:128].rearrange("p (v c) -> p v c", v=2), X,
                              ALU.add).then_inc(lam_arg, 1)
            dve.wait_ge(lam_arg, 1)

            def gelu_begin(v, gr):
                dve.wait_ge(tok_done, gr + 1)
                dve.tensor_copy(g_h[v], ps[:, gr % 4, 0:256]).then_inc(tok_free, 1)
                dve.wait_ge(tok_free, gr + 1)
                order.after(dve.tensor_tensor(g_a[v], g_h[v], g_h[v], ALU.mult))
                order.after(dve.tensor_scalar(g_a[v], g_a[v], 0.044715, 1.0, ALU.mult, ALU.add))
                dve.tensor_tensor(g_a[v], g_a[v], g_h[v], ALU.mult).then_inc(gelu_arg, 1)

            def gelu_end(v):
                dve.wait_ge(gelu_tanh, v + 1)
                order.after(dve.scalar_tensor_tensor(out=g_b, in0=g_a[v], scalar=1.0, in1=g_h[v], op0=ALU.add,
                                                     op1=ALU.mult))
                dve.tensor_scalar(g_a[v], g_b, 0.5, None, ALU.mult).then_inc(hid_done, 1)
                dve.wait_ge(hid_done, v + 1)

            def hidden_lo(v):
                dve.wait_ge(hid_hi, v + 1)
                sub(hid_t[:, 1, :], ps[:, 4, 0:256], hid_t[:, 0, :]).then_inc(hid_lo, 1)

            def rope_small(dst, src, cos, sin, tmp):
                h = ROT // 2
                dve.tensor_tensor(tmp[..., 0:h], src[..., h:ROT], sin[..., 0:h], ALU.mult)
                dve.tensor_tensor(dst, src[..., 0:ROT], cos, ALU.mult)
                order.after(dve.tensor_tensor(tmp[..., h:ROT], src[..., 0:h], sin[..., h:ROT], ALU.mult))
                return dve.tensor_tensor(dst, dst, tmp, ALU.add)

            def rope_out(dst, src, t, u):
                n, h = src.shape[1], ROT // 2
                cos = tab(C_COS + ROT * t, ROT).unsqueeze(1).broadcast_to([P, n, ROT])
                sin = tab(C_SIN + ROT * t, ROT).unsqueeze(1).broadcast_to([P, n, ROT])
                tmp = rtmp[:, 128 * u:128 * u + ROT * n].rearrange("p (n r) -> p n r", r=ROT)
                dve.tensor_tensor(tmp[:, :, 0:h], src[:, :, h:ROT], sin[:, :, 0:h], ALU.mult)
                dve.tensor_tensor(tmp[:, :, h:ROT], src[:, :, 0:h], sin[:, :, h:ROT], ALU.mult)
                dve.tensor_tensor(dst[:, :, 0:ROT], src[:, :, 0:ROT], cos, ALU.mult)
                ins = dve.tensor_copy(dst[:, :, ROT:], src[:, :, ROT:])
                return ins, lambda: dve.tensor_tensor(dst[:, :, 0:ROT], dst[:, :, 0:ROT], tmp, ALU.add)

            def kv_evac(n, gr, br, t):
                bank = gr % 4
                dve.wait_ge(tok_done, gr + 1)
                ins, last = rope_out(k_raw[:, br, t, :].rearrange("p (g d) -> p g d", d=HD),
                                     ps[:, bank, 0:256].rearrange("p (g d) -> p g d", d=HD), t, t % 2)
                vp = ps[:, bank, 256:512].rearrange("p (g c) -> p g c", g=GROUPS)
                order.after(dve.tensor_copy(v_all[:, t, br, :, 0:HD], vp))
                last().then_inc(roped, 1)
                sub(v_all[:, t, br, :, HD:P], vp, v_all[:, t, br, :, 0:HD]).then_inc(tok_free, 1)

            def q_evac(b, gr, t):
                dve.wait_ge(tok_done, gr + 1)
                ins, last = rope_out(q_raw[:, t, NB * b:NB * (b + 1)].rearrange("p (h d) -> p h d", d=HD),
                                     ps[:, gr % 4, :].rearrange("p (h d) -> p h d", d=HD), t, t % 2)
                ins.then_inc(tok_free, 1)
                dve.wait_ge(tok_free, gr + 1)
                last().then_inc(roped, 1)

            def compressed_keys():
                dve.wait_ge(cmp_done, 1)
                order.after(dve.tensor_copy(kc_f, ps[:, 5, 0:HD]))
                order.after(dve.tensor_copy(kc_r[:, ROT:], kc_f[:, ROT:]))
                rope_small(kc_r[:, 0:ROT], kc_f, tab(C_CCOS, ROT), tab(C_CSIN, ROT), rtmp[:, 0:ROT]).then_inc(kc_roped, 1)
                dve.wait_ge(kc_roped, 1)

            def compressed_keys_lo():
                dve.wait_ge(kc_hi, 2)
                sub(kc[0:HD, 1, :], ps[0:HD, 6, 0:P], kc[0:HD, 0, :])
                sub(kc[HD:P, 1, :], ps[0:HD, 6, 0:P], kc[0:HD, 0, :]).then_inc(cmp_ready, 1)

            def compressed_values():
                dve.wait_ge(cmp_done, 2)
                order.after(dve.tensor_copy(vc[:, 0:HD], ps[:, 5, 0:HD]))
                order.after(sub(vc[:, HD:P], ps[:, 5, 0:HD], vc[:, 0:HD]))
                for g in range(GROUPS):
                    for h in range(HPG):
                        ins = dve.tensor_copy(vc_rep[NC * h:NC * (h + 1), g, :], vc[NC * g:NC * (g + 1), :].bitcast(F32))
                ins.then_inc(cmp_ready, 1)

            gelu_begin(0, G_W1K)
            for t in range(T):
                split_lo(B_W1V, t)
                kv_evac(B_SLC, G_SLC + t, 0, t)
                if t == 0:
                    gelu_end(0)
            for j in range(4):
                split_lo(B_WIN, j)
            gelu_begin(1, G_W1V)
            for t, then in enumerate((lambda: (gelu_end(1), hidden_lo(0)), compressed_keys, compressed_keys_lo,
                                      lambda: hidden_lo(1))):
                split_lo(B_Q0, t)
                kv_evac(B_WIN, G_WIN + t, 1, t)
                then()
            for t in range(T):
                split_lo(B_Q1, t)
                q_evac(0, G_Q0 + t, t)
                if t == 0:
                    compressed_values()
            def key_stack_lo(gg, e):
                dve.wait_ge(st_turned, at(gg, 8, e + 1))
                dve.tensor_copy(keys(gg, 1, e // 2), ps[:, 7, :]).then_inc(stacked_v, 1)

            for t in range(T):
                split_lo(B_OUT0, t)
                q_evac(1, G_Q1 + t, t)
                if t in (1, 3):
                    key_stack_lo((0, 0), t)
            dve.wait_ge(gate_turned, 1)
            order.after(dve.tensor_scalar(gate[:, :, :], ps[:, 6, 0:T * 48].rearrange("p (t c) -> p t c", t=T), 0.5, 0.5,
                                          ALU.mult, ALU.add))
            g0 = gate[:, :, :].rearrange("p t (h b) -> p t h b", b=3)[:, :, :, 0]
            dve.tensor_tensor(g0, g0, tab(C_CMUL, T).unsqueeze(2).broadcast_to([P, T, 16]),
                              ALU.mult).then_inc(gates_ready, 1)
            dve.wait_ge(lam_exp, 1)
            order.after(dve.tensor_tensor(lam2[:, 1:2], lam_s[:, 3:4], lam_s[:, 2:3], ALU.subtract))
            order.after(dve.tensor_scalar(lam2[:, 1:2], lam2[:, 1:2], -LAMBDA_INIT, None, ALU.add))
            order.after(dve.memset(lam2[:, 0:1], 1.0))

            cos4 = tab(C_COS, 64, T)
            sin4 = tab(C_SIN, 64, T)

            def maxes(gg, v):
                dve.wait_ge(s_done, at(gg, UNITS, v + 1))
                dve.tensor_reduce(nmax4[:, v % 4:v % 4 + 1], ps[:, v % 4, 0:unit(v)[3]], X, ALU.max, negate=True
                                  ).then_inc(max_done, 1)

            def inverse(gg, v):
                dve.wait_ge(exp_done, at(gg, UNITS, v + 1))
                dve.reciprocal(rinv4[:, v % 4:v % 4 + 1], rsum4[:, v % 4:v % 4 + 1]).then_inc(rinv_done, 1)

            def turned_lo(gg, v):
                h, br, i, n = unit(v)
                dve.wait_ge(pt_hi, at(gg, UNITS, v + 1))
                o, dims = PT_BR * br + P * i, [[PT_ROW, i + 1], [1, P]]
                sub(view(slot0[1], o, dims), ps[:, 4 + v % 2, 0:n].rearrange("p (j c) -> p j c", c=P),
                    view(slot0[0], o, dims)).then_inc(pt_lo, 1)

            def out_sum(gg, h):
                r = HD * (h % 2)
                dve.wait_ge(o_half, at(gg, 4, h + 1))
                dve.tensor_tensor(o_buf[r:r + HD, :], ps[0:HD, 6, :], o_buf[r:r + HD, :], ALU.add).then_inc(o_sum, 1)

            def out_lo(gg, h):
                r = HD * (h % 2)
                dve.wait_ge(o_hi, at(gg, 4, h + 1))
                pair = bass.ds(place(gg, 2, h // 2), 1)
                sub(act_lo[r:r + HD, pair, :].rearrange("p o c -> p (o c)"), o_buf[r:r + HD, :],
                    act_hi[r:r + HD, pair, :].rearrange("p o c -> p (o c)")).then_inc(o_lo, 1)

            e4 = c_sc.rearrange("p (i h n) -> p i h n", i=T, h=HPG)
            er = c_sc.rearrange("p (r n) -> p r n", n=NC)

            def slot(gg, k):
                if k == 6:
                    dve.wait_ge(cs_done, at(gg, 1, 1))
                    dve.tensor_tensor(e4, ps[:, 7, :].rearrange("p (i h n) -> p i h n", i=T, h=HPG),
                                      tab(C_CADD, 128, T).unsqueeze(2).broadcast_to([P, T, HPG, NC]), ALU.add
                                      ).then_inc(cs_masked, 1)
                if k == 7:
                    dve.wait_ge(cs_masked, at(gg, 1, 1))
                    dve.tensor_reduce(c_st[:, 0, :], er, X, ALU.max).then_inc(cs_max, 1)
                if k == 9:
                    dve.wait_ge(cs_exp, at(gg, 1, 1))
                    dve.tensor_reduce(c_st[:, 1, :], er, X, ALU.add).then_inc(cs_sum, 1)
                if k == 10:
                    dve.wait_ge(cs_inv, at(gg, 1, 1))
                    gc = gate[:, :, bass.ds(place(gg, 12, 0), 12)].rearrange("p t (h b) -> p t h b", b=3)[:, :, :, 0]
                    dve.tensor_tensor(c_st[:, 3, :].rearrange("p (t h) -> p t h", t=T),
                                      c_st[:, 2, :].rearrange("p (t h) -> p t h", t=T), gc, ALU.mult).then_inc(cs_coef, 1)
                if 0 <= k - L_NORM < UNITS:
                    inverse(gg, k - L_NORM)
                if 0 <= k - L_MAX < UNITS:
                    maxes(gg, k - L_MAX)
                if 0 <= k - L_SPLIT < UNITS:
                    turned_lo(gg, k - L_SPLIT)
                if k == 7:
                    dve.wait_ge(cs_max, at(gg, 1, 1))
                    dve.tensor_tensor(er, er, c_st[:, 0, :].unsqueeze(2).broadcast_to([P, 16, NC]),
                                      ALU.subtract).then_inc(cs_sub, 1)
                if k == 9:
                    dve.wait_ge(cs_sum, at(gg, 1, 1))
                    dve.reciprocal(c_st[:, 2, :], c_st[:, 1, :]).then_inc(cs_inv, 1)
                if k - 1 in TURNS and TURNS.index(k - 1) in (1, 3):
                    key_stack_lo(gg, TURNS.index(k - 1))
                if k == 12:
                    dve.wait_ge(pc_hi, at(gg, 1, 1))
                    sub(pct[1], ps[:, 7, :], pct[0]).then_inc(pc_lo, 1)
                if k >= 15 and (k - 15) % 8 == 0:
                    out_sum(gg, (k - 15) // 8)
                if k >= 17 and (k - 17) % 8 == 0:
                    out_lo(gg, (k - 17) // 8)

            windows(dve, slot, SLOT0, UNITS, 2, GROUPS, begun=0)

            def residual(gr, bank, t, dh):
                dve.wait_ge(tok_done, gr + 1)
                xs = x_res[:, t, NB * dh:NB * (dh + 1)]
                dve.tensor_tensor(xs, ps[:, bank, :], xs, ALU.add).then_inc(tok_free, 1)

            def norm_tail(q0, step):
                for t in range(T):
                    step(t)
                    if t:
                        norm_lo(q0 + t - 1, t - 1)
                    norm_y(q0 + t, t)
                norm_lo(q0 + T - 1, T - 1)

            def out_layer(b0, g0, q0):
                for t in range(T):
                    residual(g0 + t, (g0 + t) % 4, t, 0)
                for t in range(T):
                    split_lo(b0 + 2, t)
                norm_tail(q0, lambda t: residual(g0 + 4 + t, (g0 + 4 + t) % 4, t, 1))

            for j in range(4):
                split_lo(B_OUT0 + 1, j)
            out_layer(B_OUT0, G_OUT0, 4)

            def final_norm(step):
                dve.wait_ge(gfin_landed, 16)
                for t in range(T):
                    step(t)
                    dve.wait_ge(rstd_done, 16 + t + 1)
                    if t >= 2:
                        dve.wait_ge(stored[t % 2], 32)
                    for b in range(2):
                        c = slice(HALF * b, HALF * (b + 1))
                        dve.scalar_tensor_tensor(out=fin[:, t % 2, c], in0=x_res[:, t, c], scalar=rstd[:, 16 + t:17 + t],
                                                 in1=gfin[:, c], op0=ALU.mult, op1=ALU.mult).then_inc(fin_done, 1)

            def mlp_step(n, gr, up, last):
                for c in range(4):
                    if c == 3 and last is not None:
                        if last < 16:
                            for j in range(4):
                                split_lo(n + 4, j, B_MLP0 % 2)
                            norm_tail(last, lambda t: residual(gr + 4 + t, (G_MLP0 + 4 + t) % 4, t, 1))
                        else:
                            final_norm(lambda t: residual(gr + 4 + t, (G_MLP0 + 4 + t) % 4, t, 1))
                        continue
                    for j in range(4):
                        split_lo(n + (c + 1), j, (B_MLP0 + c + 1) % 2)
                        if c < 2:
                            u = 4 * c + j
                            dve.wait_ge(up_free, up + (u + 1))
                            if u >= 2:
                                dve.wait_ge(a_ready, up + (u - 1))
                            dve.tensor_tensor(sq_b[:, u % 2, :], relu_b[:, u % 2, :], relu_b[:, u % 2, :],
                                              ALU.mult).then_inc(sq_done, 1)
                            dve.wait_ge(sq_done, up + (u + 1))
                            dve.wait_ge(a_hi_done, up + (u + 1))
                            sub(a_lo[:, u, :], sq_b[:, u % 2, :], a_hi[:, u, :]).then_inc(a_ready, 1)
                        else:
                            d = 4 * (c - 2) + j
                            residual(gr + d, (G_MLP0 + d) % 4, j, c - 2)

            def mlp_layer(n0, g0, u0, end):
                with dve.Fori(0, STEPS - 1) as it:
                    mlp_step(it * 4 + n0, it * 8 + g0, it * 8 + u0, None)
                k = STEPS - 1
                mlp_step(n0 + 4 * k, g0 + 8 * k, u0 + 8 * k, end)

            mlp_layer(B_MLP0, G_MLP0, 0, 8)

            for b in range(6):
                for t in range(T):
                    split_lo(B_DIFF + b + 1, t)
                    gr = G_DIFF + 4 * b + t
                    dve.wait_ge(tok_done, gr + 1)
                    src = ps[:, gr % 4, :]
                    if b < 4:
                        raw = q_raw if b < 2 else dk_raw
                        ins, last = rope_out(raw[:, t, NB * (b % 2):NB * (b % 2 + 1)].rearrange("p (h d) -> p h d", d=HD),
                                             src.rearrange("p (h d) -> p h d", d=HD), t, t % 2)
                        ins.then_inc(tok_free, 1)
                        dve.wait_ge(tok_free, gr + 1)
                        last().then_inc(d_roped, 1)
                    else:
                        v = dv_all[:, t, 4 * (b - 4):4 * (b - 3), :]
                        vp = src.rearrange("p (h c) -> p h c", h=4)
                        order.after(dve.tensor_copy(v[:, :, 0:P], vp))
                        sub(v[:, :, P:2 * P], vp, v[:, :, 0:P]).then_inc(tok_free, 1)

            def d_slot(hh, k):
                if 0 <= k - L_NORM < D_UNITS:
                    u = k - L_NORM
                    dve.wait_ge(dexp_done, at(hh, D_UNITS, u + 1))
                    await_(dve, da_done, at(hh, T, u // 2 - 1))
                    dve.reciprocal(rinv4[:, u % 4:u % 4 + 1], rsum4[:, u % 4:u % 4 + 1]).then_inc(drinv_done, 1)
                if 0 <= k - L_MAX < D_UNITS:
                    u = k - L_MAX
                    dve.wait_ge(ds_done, at(hh, D_UNITS, u + 1))
                    dve.tensor_reduce(nmax4[:, u % 4:u % 4 + 1], ps[:, u % 4, 0:P * (u // 2 + 1)], X, ALU.max, negate=True
                                      ).then_inc(dmax_done, 1)
                i = tile_at(k, D_SPLIT)
                if i is not None:
                    n = P * (i + 1)
                    dve.wait_ge(dpt_hi, at(hh, T, i + 1))
                    sub(dpt[1][:, i % 2, 0:n], ps[:, 4, 0:n], dpt[0][:, i % 2, 0:n]).then_inc(dpt_lo, 1)
                i = tile_at(k, D_OUT)
                if i is not None:
                    dve.wait_ge(dpv_done, at(hh, T, i + 1))
                    dve.tensor_reduce(q_raw[:, i, bass.ds(place(hh, P, 0), P)],
                                      ps[:, 6, 0:256].rearrange("p (z c) -> p c z", z=2), X,
                                      ALU.add).then_inc(do_free, 1)
                if k == D_MS:
                    dve.wait_ge(d_ss_done, at(hh, T, T))
                    dve.tensor_scalar(d_ms, d_ss, 1.0 / P, EPS, ALU.mult, ALU.add).then_inc(d_ms_done, 1)
                if k == D_Y:
                    dve.wait_ge(d_rs_done, at(hh, 1, 1))
                    dve.tensor_tensor(o_buf[:, :].rearrange("p (t c) -> p t c", t=T), q_raw[:, :, bass.ds(place(hh, P, 0), P)],
                                      d_rs.unsqueeze(2).broadcast_to([P, T, P]), ALU.mult).then_inc(dy_done, 1)
                if k == D_OUT_SPLIT and isinstance(hh[0], int) and sum(hh) == DH - 1:
                    for j in range(4):
                        split_lo(B_OUT1 + 1, j)
                if k == D_OUT_SPLIT:
                    dve.wait_ge(do_hi, at(hh, 1, 1))
                    feat = bass.ds(place(hh, 1, 0), 1)
                    dve.scalar_tensor_tensor(out=act_lo[:, feat, :].rearrange("p o c -> p (o c)"), in0=ps[:, 5, :],
                                             scalar=subg[:, 0:1],
                                             in1=act_hi[:, feat, :].rearrange("p o c -> p (o c)").bitcast(F32),
                                             op0=ALU.mult, op1=ALU.subtract).then_inc(do_lo, 1)
                i = tile_at(k, D_A)
                if i is not None:
                    n, u = P * (i + 1), 2 * i % 4
                    dve.wait_ge(dp1_done, at(hh, T, i + 1))
                    dve.wait_ge(drinv_done, at(hh, D_UNITS, 2 * i + 1))
                    dve.scalar_tensor_tensor(out=probs[:, u + 1, 0:n], in0=probs[:, u, 0:n], scalar=rinv4[:, u:u + 1],
                                             in1=probs[:, u + 1, 0:n], op0=ALU.mult, op1=ALU.add).then_inc(da_done, 1)

            windows(dve, d_slot, D_SLOT0, D_UNITS, D_SPANS, DH)

            out_layer(B_OUT1, G_OUT1, 12)
            mlp_layer(B_MLP1, G_MLP1, 32, 16)

        @block.tensor
        def _(pe):
            def mm(o, l, r, start, stop):
                return pe.matmul(o, l, r, start=start, stop=stop)

            def product(o, pairs, start=True, stop=True):
                for i, (l, r) in enumerate(pairs):
                    ins = mm(o, l, r, start and i == 0, stop and i == len(pairs) - 1)
                return ins

            def whole(n, sl=None):
                pe.wait_ge(lo_split, n * 4 + 4)

            def norm_turn(q):
                for b in range(2):
                    pe.wait_ge(y_done, 2 * q + b + 1)
                    if q >= 2:
                        pe.wait_ge(act_ready, 2 * (q - 2) + b + 1)
                    for k in range(4):
                        c = HALF * b + P * k
                        ins = pe.transpose(ps[:, 4 + 2 * (q % 2) + b, P * k:P * (k + 1)], y_bufs[q % 2][:, c:c + P], ident)
                    ins.then_inc(turned, 1)

            def token_group(gr, bank, sl, t, ks=range(KT), n=None):
                for k in ks:
                    if n is not None and k % 2 == 0:
                        pe.wait_ge(lo_split, n * 4 + (k // 2 + 1))
                    xh, xl = act_hi[:, k, P * t:P * (t + 1)], act_lo[:, k, P * t:P * (t + 1)]
                    wh, wl = (w[:, sl, NB * k:NB * (k + 1)] for w in (w_hi, w_lo))
                    ins = product(ps[:, bank, :], [(xh, wh), (xh, wl), (xl, wh)], k == 0, k == KT - 1)
                if ks[-1] == KT - 1:
                    ins.then_inc(tok_done, 1)

            def feature_group(bank, sl, m, q=slice(0, S), n=None):
                for k in range(KT):
                    if n is not None and k % 2 == 0:
                        pe.wait_ge(lo_split, n * 4 + (k // 2 + 1))
                    c = NB * k + P * m
                    wh, wl = w_hi[:, sl, c:c + P], w_lo[:, sl, c:c + P]
                    ins = product(ps[:, bank, q], [(wh, act_hi[:, k, q]), (wh, act_lo[:, k, q]), (wl, act_hi[:, k, q])],
                                  k == 0, k == KT - 1)
                return ins

            pe.wait_ge(cst_landed, 32)
            pe.wait_ge(small_lo, 2)
            for t in range(T):
                norm_turn(t)
            pe.wait_ge(act_ready, 8)
            for m in range(4):
                feature_group(G_CMP + m, 0, m, n=B_CMP if m == 0 else None).then_inc(tok_done, 1)

            def hidden(n, v):
                whole(n)
                gr = (G_W1K, G_W1V)[v]
                pe.wait_ge(xc_ready, v + 1)
                pe.wait_ge(tok_free, gr - 3)
                pairs = []
                for j in range(16):
                    wh, wl = (w[:, n % 2, 256 * j:256 * (j + 1)] for w in (w_hi, w_lo))
                    pairs += [(xc_hi[v][:, j, :], wh), (xc_hi[v][:, j, :], wl), (xc_lo[v][:, j, :], wh)]
                product(ps[:, gr % 4, 0:256], pairs).then_inc(tok_done, 1)

            def turn_hidden(v):
                pe.wait_ge(hid_done, v + 1)
                for c in range(2):
                    ins = pe.transpose(ps[:, 4, P * c:P * (c + 1)], g_a[v][:, P * c:P * (c + 1)], ident)
                ins.then_inc(hid_turned, 1)

            def second(v):
                pe.wait_ge(small_lo, 4)
                pe.wait_ge(hid_lo, v + 1)
                pairs = []
                for c in range(2):
                    h, l = hid_t[:, 0, P * c:P * (c + 1)], hid_t[:, 1, P * c:P * (c + 1)]
                    wh, wl = (w2_r[:, z, P * v + HD * c:P * v + HD * (c + 1)] for z in range(2))
                    pairs += [(h, wh), (h, wl), (l, wh)]
                product(ps[:, 5, 0:HD], pairs).then_inc(cmp_done, 1)

            def token_block(n, g0, norm=None, q0=None, then=None):
                for t in range(T):
                    if norm is not None:
                        pe.wait_ge(act_ready, 2 * (4 * norm + t + 1))
                    pe.wait_ge(tok_free, g0 + t - 3)
                    token_group(g0 + t, (g0 + t) % 4, n % 2, t, n=n if t == 0 else None)
                    if q0 is not None and t:
                        norm_turn(q0 + t - 1)
                    if then is not None:
                        then(t)

            def turn_keys():
                pe.wait_ge(kc_roped, 1)
                pe.transpose(ps[0:HD, 6, 0:P], kc_r, ident).then_inc(kc_turned, 1)

            def out_begin(n, g0):
                whole(n)
                for t in range(T):
                    token_group(g0 + t, (g0 + t) % 4, n % 2, t, ks=range(KT - 1))

            def out_end(n, g0):
                for t in range(T):
                    token_group(g0 + t, (g0 + t) % 4, n % 2, t, ks=range(KT - 1, KT))

            hidden(B_W1K, 0)
            token_block(B_SLC, G_SLC)
            hidden(B_W1V, 1)
            token_block(B_WIN, G_WIN, then=lambda t: (lambda: turn_hidden(0), lambda: second(0), turn_keys,
                                                      lambda: turn_hidden(1))[t]())
            token_block(B_Q0, G_Q0, then=lambda t: second(1) if t == 0 else None)
            pairs = []
            for k in range(KT):
                wh, wl = (tail_r[:, z, 48 * k:48 * (k + 1)] for z in range(2))
                pairs += [(wh, act_hi[:, k, :]), (wh, act_lo[:, k, :]), (wl, act_hi[:, k, :])]
            product(ps[0:48, 6, :], pairs).then_inc(gate_done, 1)

            def turn_gates():
                pe.wait_ge(gate_tanh, 1)
                for t in range(T):
                    ins = pe.transpose(ps[:, 6, 48 * t:48 * (t + 1)], o_buf[0:48, P * t:P * (t + 1)], ident[0:48, 0:48])
                ins.then_inc(gate_turned, 1)

            def turn_stack(gg, e):
                pe.wait_ge(stage_filled, at(gg, 8, e + 1))
                if e == 0:
                    await_(pe, pc_lo, at(gg, 1, 0))
                elif e in (2, 4):
                    pe.wait_ge(stacked_v, at(gg, 2, e // 2))
                else:
                    pe.wait_ge(stacked_a, at(gg, 6, 1 + e // 2 if e < 4 else e - 2))
                for t in range(T):
                    ins = pe.transpose(ps[:, 7, P * t:P * (t + 1)], stage[:, e % 2, t, :], ident)
                ins.then_inc(st_turned, 1)

            token_block(B_Q1, G_Q1, then=lambda t: turn_stack((0, 0), t))
            turn_gates()
            for e in range(4, 7):
                turn_stack((0, 0), e)

            pe.wait_ge(cmp_ready, 2)
            pe.wait_ge(tok_free, G_Q1 + T)

            def scores(gg, v):
                h, br, i, n = unit(v)
                await_(pe, exp_done, at(gg, UNITS, v - 3))
                if v == 0:
                    pe.wait_ge(stacked_v, at(gg, 2, 2))
                if v % 8 == 0:
                    pe.wait_ge(stacked_a, at(gg, 6, 3 + h))
                q = q_stack[:, h, P * i:P * (i + 1)]
                o = ps[:, v % 4, 0:n]
                product(o, [(q, keys(gg, z, br, n)) for z in range(2)], stop=False)
                mm(o[:, n - P:n], ident_b[:, :], mask_b[:, :], False, True).then_inc(s_done, 1)

            def block_scores(gg, h):
                if h == 0:
                    pe.wait_ge(stacked_a, at(gg, 6, 6))
                for i in range(T):
                    q = q_stack[:, h, P * i:P * (i + 1)]
                    c0 = P * i + NC * h
                    ins = product(ps[:, 7, c0:c0 + NC],
                                  [(q, kc[:, z, bass.ds(place(gg, NC, 0), NC)]) for z in range(2)])
                if h == HPG - 1:
                    ins.then_inc(cs_done, 1)

            def turn(gg, v):
                pe.wait_ge(normed, at(gg, UNITS, v + 1))
                await_(pe, pt_lo, at(gg, UNITS, v - 1))
                for j in range(unit(v)[2] + 1):
                    ins = pe.transpose(ps[:, 4 + v % 2, P * j:P * (j + 1)], probs[:, v % 4, P * j:P * (j + 1)], ident)
                ins.then_inc(p_turned, 1)

            def values(gg, h, br):
                pe.wait_ge(pt_lo, at(gg, UNITS, 8 * h + 4 * br + 4))
                if br == 0:
                    await_(pe, o_sum, at(gg, 4, h))
                if h == 0:
                    pe.wait_ge(v_staged, at(gg, 3, 1 + 2 * br))
                if br == 1:
                    if h == 0:
                        pe.wait_ge(pc_lo, at(gg, 1, 1))
                    r = NC * h
                    for z in range(2):
                        mm(ps[:, 6, :], vc_st[r:r + NC, :], pct[z][r:r + NC, :], False, False)
                for j in range(T):
                    for z in range(2):
                        o0 = PT_BR * br + (PT_ROW + P) * j
                        ins = mm(ps[:, 6, P * j:S], v_st[:, j, br, :], slot0[z][:, o0:o0 + S - P * j],
                                 br == 0 and j == 0 and z == 0, br == 1 and j == T - 1 and z == 1)
                ins.then_inc(pv_done, 1)

            def slot(gg, k):
                if 0 <= k < UNITS:
                    scores(gg, k)
                if k in TURNS:
                    turn_stack(gg, TURNS.index(k))
                if 0 <= k - L_TURN < UNITS:
                    turn(gg, k - L_TURN)
                v = k - L_PV
                if 0 <= v < UNITS and v % 4 == 3:
                    values(gg, v // 8, v // 4 % 2)
                if 2 <= k < 6:
                    block_scores(gg, k - 2)
                if k == 11:
                    pe.wait_ge(pc_ready, at(gg, 1, 1))
                    for i in range(T):
                        ins = pe.transpose(ps[:, 7, P * i:P * (i + 1)], c_sc[:, P * i:P * (i + 1)], ident)
                    ins.then_inc(pc_turned, 1)

            windows(pe, slot, SLOT0, UNITS, 2, GROUPS, begun=0)

            pe.wait_ge(o_lo, 4 * GROUPS - 2)
            pe.wait_ge(exp_done, UNITS * GROUPS)
            out_begin(B_OUT0, G_OUT0)
            pe.wait_ge(o_lo, 4 * GROUPS)
            out_end(B_OUT0, G_OUT0)
            token_block(B_OUT0 + 1, G_OUT0 + 4, q0=4)

            def mlp_begin(n, gr, q0):
                whole(n)
                sl = B_MLP0 % 2
                for u in range(2):
                    pe.wait_ge(act_ready, 2 * (q0 + 2))
                    pe.wait_ge(tok_free, gr + (u - 3))
                    feature_group(u + 2, sl, u, slice(0, S // 2))
                    if u == 0:
                        norm_turn(q0 + T - 1)
                pe.wait_ge(act_ready, 2 * (q0 + T))
                for u in range(2):
                    feature_group(u + 2, sl, u, slice(S // 2, S)).then_inc(up_done, 1)

            def mlp_step(n, gr, up, q0=None, begun=False):
                for c in range(4):
                    sl = (B_MLP0 + c) % 2
                    whole(n + c)
                    for j in range(4):
                        if c < 2:
                            u = 4 * c + j
                            if begun and u < 2:
                                continue
                            if u < 4:
                                pe.wait_ge(tok_free, gr + (u - 3))
                            else:
                                pe.wait_ge(up_free, up + (u - 3))
                            feature_group((u + 2) % 4, sl, j).then_inc(up_done, 1)
                            continue
                        d = 4 * (c - 2) + j
                        if d >= 4:
                            pe.wait_ge(tok_free, gr + (d - 3))
                        bank = (G_MLP0 + d) % 4
                        pairs = []
                        if d < 4:
                            pe.wait_ge(up_free, up + (d + 5))
                        for k in range(KT):
                            if d == 0:
                                pe.wait_ge(a_ready, up + (k + 1))
                            ah, al = a_hi[:, k, P * j:P * (j + 1)], a_lo[:, k, P * j:P * (j + 1)]
                            wh, wl = (w[:, sl, NB * k:NB * (k + 1)] for w in (w_hi, w_lo))
                            ins = product(ps[:, bank, :], [(ah, wh), (ah, wl), (al, wh)], k == 0, k == KT - 1)
                        ins.then_inc(tok_done, 1)
                        if q0 is not None and d >= 5:
                            norm_turn(q0 + d - 5)

            def mlp_layer(n0, g0, u0, q_in, q0):
                mlp_begin(n0, g0, q_in)
                mlp_step(n0, g0, u0, begun=True)
                with pe.Fori(0, STEPS - 2) as it:
                    mlp_step(it * 4 + (n0 + 4), it * 8 + (g0 + 8), it * 8 + (u0 + 8))
                k = STEPS - 1
                mlp_step(n0 + 4 * k, g0 + 8 * k, u0 + 8 * k, q0)

            mlp_layer(B_MLP0, G_MLP0, 0, 4, 8)
            for b in range(5):
                token_block(B_DIFF + b, G_DIFF + 4 * b, 2, then=lambda t: norm_turn(11) if b == 0 and t == 0 else None)

            def d_turn_keys(hh, e):
                pe.wait_ge(dk_filled, at(hh, 4, e + 1))
                if e < 2:
                    await_(pe, dq_stacked, at(hh, 2, e - 1))
                else:
                    pe.wait_ge(dk_stacked, at(hh, 4, e - 1))
                if e == 3:
                    await_(pe, do_lo, at(hh, 1, -2))
                for t in range(T):
                    ins = pe.transpose(ps[:, (7, 5)[e % 2], P * t:P * (t + 1)],
                                       key_stage(hh)[:, e // 2, e % 2, t, :].bitcast(F32), ident)
                ins.then_inc(dk_turned, 1)

            def d_turn_queries(hh, a):
                pe.wait_ge(dq_filled, at(hh, 2, a + 1))
                pe.wait_ge(dk_stacked, at(hh, 4, 3 + a))
                for c in range(2):
                    for t in range(2):
                        o = P * (2 * c + t)
                        ins = pe.transpose(ps[:, (7, 5)[a], o:o + P], query_stage(hh)[:, a, t, c, :].bitcast(F32), ident)
                ins.then_inc(dq_turned, 1)

            token_block(B_DIFF + 5, G_DIFF + 20, 2, then=lambda t: d_turn_keys((0, 0), t))
            pe.wait_ge(tok_free, G_OUT1)

            def d_scores(hh, u):
                i, c, n = u // 2, u % 2, P * (u // 2 + 1)
                await_(pe, dexp_done, at(hh, D_UNITS, u - 3))
                if u == 0:
                    pe.wait_ge(dk_stacked, at(hh, 4, 4))
                if u % 4 == 0:
                    pe.wait_ge(dq_stacked, at(hh, 2, u // 4 + 1))
                o = ps[:, u % 4, 0:n]
                product(o, [(dq_stack[:, c, P * i:P * (i + 1)], keys(hh, z, c, n)) for z in range(2)], stop=False)
                mm(o[:, n - P:n], ident_b[:, :], mask_b[:, :], False, True).then_inc(ds_done, 1)

            def d_slot(hh, k):
                if 0 <= k < D_UNITS:
                    d_scores(hh, k)
                i = tile_at(k, D_TURN)
                if i is not None:
                    pe.wait_ge(da_done, at(hh, T, i + 1))
                    await_(pe, dpt_lo, at(hh, T, i))
                    for j in range(i + 1):
                        ins = pe.transpose(ps[:, 4, P * j:P * (j + 1)], probs[:, (2 * i + 1) % 4, P * j:P * (j + 1)], ident)
                    ins.then_inc(dp_turned, 1)
                i = tile_at(k, D_PV)
                if i is not None:
                    pe.wait_ge(dpt_lo, at(hh, T, i + 1))
                    await_(pe, do_free, at(hh, T, i))
                    pairs = [(dpt[z][:, i % 2, P * j:P * (j + 1)],
                              dv_all[:, j, bass.ds(place(hh, 1, 0), 1), :].rearrange("p o c -> p (o c)"))
                             for j in range(i + 1) for z in range(2)]
                    product(ps[:, 6, 0:256], pairs).then_inc(dpv_done, 1)
                if k in D_TURN_K and not first(hh):
                    d_turn_keys(hh, D_TURN_K.index(k))
                if k in D_TURN_Q:
                    d_turn_queries(hh, D_TURN_Q.index(k))
                if k == D_PV + 2 * T - 1 and isinstance(hh[0], int) and sum(hh) == DH - 1:
                    pe.wait_ge(do_lo, DH - 1)
                    pe.wait_ge(dexp_done, D_UNITS * DH)
                    out_begin(B_OUT1, G_OUT1)
                if k == D_OUT_TURN:
                    pe.wait_ge(dy_done, at(hh, 1, 1))
                    if not isinstance(hh[0], int) or sum(hh) + 3 < DH:
                        pe.wait_ge(dk_stacked, at(hh, 4, 14))
                    else:
                        pe.wait_ge(dq_stacked, 2 * DH)
                        pe.wait_ge(do_lo, sum(hh))
                    for t in range(T):
                        ins = pe.transpose(ps[:, 5, P * t:P * (t + 1)], o_buf[:, P * t:P * (t + 1)], ident)
                    ins.then_inc(do_turned, 1)

            windows(pe, d_slot, D_SLOT0, D_UNITS, D_SPANS, DH)

            pe.wait_ge(do_lo, DH)
            out_end(B_OUT1, G_OUT1)
            token_block(B_OUT1 + 1, G_OUT1 + 4, q0=12)
            mlp_layer(B_MLP1, G_MLP1, 32, 12, None)


def _constants():
    c = np.zeros((P, C_END), np.float32)
    c[:, C_ID:C_ID + P] = np.eye(P, dtype=np.float32)
    q = np.arange(P)
    c[:, C_MASK:C_MASK + P] = np.where(q[None, :] > q[:, None], np.float32(NEG), np.float32(0))
    inv = (np.float32(1.0) / (np.float32(500000.0) ** (np.arange(0, ROT, 2, dtype=np.float32) / np.float32(ROT)))
           ).astype(np.float32)

    def rope(pos):
        ang = pos.astype(np.float32)[:, None] * inv[None, :]
        co, si = np.cos(ang), np.sin(ang)
        return np.concatenate([co, co], 1), np.concatenate([-si, si], 1)

    for t in range(T):
        co, si = rope(P * t + q)
        c[:, C_COS + ROT * t:C_COS + ROT * (t + 1)] = co
        c[:, C_SIN + ROT * t:C_SIN + ROT * (t + 1)] = si
        ends = 16 * np.arange(NC) + 31
        seen = (ends[None, :] <= (P * t + q)[:, None]) & (np.arange(NC) < NC - 1)[None, :]
        c[:, C_CADD + NC * t:C_CADD + NC * (t + 1)] = np.where(seen, 0, NEG)
        c[:, C_CMUL + t] = seen[:, 0]
    co, si = rope(16 * (q % NC) + 31)
    c[:, C_CCOS:C_CCOS + ROT] = co
    c[:, C_CSIN:C_CSIN + ROT] = si
    return c


def kernel(x, attn_norm_g, mlp_norm_g, nsa_w_in, nsa_ck_pos, nsa_ck_w1, nsa_ck_w2, nsa_cv_pos, nsa_cv_w1, nsa_cv_w2,
           nsa_w_out, diff_w_in, diff_lq1, diff_lk1, diff_lq2, diff_lk2, diff_subln_g, diff_w_out, mlp_w_up,
           mlp_w_down, final_norm_g):
    import concourse.bacc as bacc
    from concourse.bass_utils import run_bass_kernel_spmd

    def positions(pos):
        one = np.asarray(pos).reshape(16, 2, HD).transpose(2, 1, 0).reshape(HD, 32)
        return np.concatenate([one, one], 0)

    gains = [attn_norm_g[0], mlp_norm_g[0], attn_norm_g[1], mlp_norm_g[1]]
    vectors = np.concatenate([positions(nsa_ck_pos[0]), positions(nsa_cv_pos[0]),
                              np.asarray(diff_subln_g[0]).reshape(P, 1)], 1)
    ins = {
        "x": np.asarray(x)[0], "consts": _constants(), "vectors": vectors,
        "w_in": np.asarray(nsa_w_in)[0], "ck_w1": np.asarray(nsa_ck_w1)[0], "ck_w2": np.asarray(nsa_ck_w2)[0],
        "cv_w1": np.asarray(nsa_cv_w1)[0], "cv_w2": np.asarray(nsa_cv_w2)[0], "w_out": np.asarray(nsa_w_out)[0],
        "diff_in": np.asarray(diff_w_in)[0], "diff_out": np.asarray(diff_w_out)[0],
        "w_up": np.asarray(mlp_w_up), "w_down": np.asarray(mlp_w_down),
        "lam_in": np.concatenate([np.asarray(v) for v in (diff_lq1, diff_lk1, diff_lq2, diff_lk2)], 1),
        "norm_g": np.stack([np.asarray(g) for g in gains]),
        "final_g": np.asarray(final_norm_g).reshape(1, D),
    }
    ins = {n: np.ascontiguousarray(v) for n, v in ins.items()}
    nc = bacc.Bacc("TRN2", target_bir_lowering=False, num_devices=1, dynamic_dma_scratch_size=1024)
    aps = {n: nc.dram_tensor(f"in_{n}", v.shape, mybir.dt.from_np(v.dtype), kind="ExternalInput").ap()
           for n, v in ins.items()}
    out = nc.dram_tensor("out", (S, D), F32, kind="ExternalOutput").ap()
    build(nc, aps, out)
    r = run_bass_kernel_spmd(nc, [{f"in_{n}": v for n, v in ins.items()}], core_ids=[0])
    return r.results[0]["out"].reshape(1, S, D)
```
